# Optimizing a Trainium2 kernel written in Bass

```python
import math
import jax, jax.numpy as jnp
from jax import lax
import numpy as np

D_MODEL = 1024
BATCH = 1
SEQ = 512
DEPTH = 1

HEAD_DIM = 64
A_HEADS = 6
A_BRANCHES = ((128, 1), (512, 4), (2048, 16))
B_HEADS = 4
B_KEY_DIM = 32
B_VAL_DIM = 64
B_GATE_RANK = 16
B_GATE_TAU = 16.0
B_CHUNK = 16
C_HEADS = 6
C_BLOCK = 256
C_TOPK = 3
C_QCHUNK = 16
REL_BUCKETS = 32
REL_MAX_DIST = 2048
D_FF = 4 * D_MODEL
EPS = 1e-6
NEG_INF = -1e30

A_WIDTH = A_HEADS * HEAD_DIM
B_QK = B_HEADS * B_KEY_DIM
B_WIDTH = B_HEADS * B_VAL_DIM
C_WIDTH = C_HEADS * HEAD_DIM
MIX_WIDTH = A_WIDTH + B_WIDTH + C_WIDTH
IN_SIZES = (A_WIDTH, A_WIDTH, A_WIDTH, B_QK, B_QK, B_WIDTH, B_WIDTH, B_GATE_RANK, C_WIDTH, C_WIDTH, C_WIDTH)
IN_WIDTH = sum(IN_SIZES)


def rmsnorm(x, w):
    xf = x.astype(jnp.float32)
    y = xf * lax.rsqrt(jnp.mean(xf * xf, axis=-1, keepdims=True) + EPS)
    return (y * w.astype(jnp.float32)).astype(x.dtype)

def rel_bucket(dist):
    n = jnp.maximum(dist, 0)
    exact = REL_BUCKETS // 2
    logv = jnp.log(jnp.maximum(n, 1).astype(jnp.float32) / exact) / math.log(REL_MAX_DIST / exact)
    large = jnp.minimum(exact + (logv * (REL_BUCKETS - exact)).astype(jnp.int32), REL_BUCKETS - 1)
    return jnp.where(n < exact, n, large)

def dilated_branch(q, k, v, bias_a, window, dilation):
    Bsz, S, H, Dh = q.shape
    L = S // dilation
    span = window // dilation
    blk = min(span, L)
    nb = -(-L // blk)
    Lp = nb * blk

    def sub(t):
        t = t.reshape(Bsz, L, dilation, H, Dh).transpose(0, 2, 1, 3, 4)
        t = jnp.pad(t, ((0, 0), (0, 0), (0, Lp - L), (0, 0), (0, 0)))
        return t.reshape(Bsz, dilation, nb, blk, H, Dh)

    def with_prev(t):
        prev = jnp.pad(t, ((0, 0), (0, 0), (1, 0), (0, 0), (0, 0), (0, 0)))[:, :, :-1]
        return jnp.concatenate([prev, t], axis=3)

    qb = sub(q)
    kc = with_prev(sub(k))
    vc = with_prev(sub(v))
    logits = jnp.einsum('brnqhe,brnkhe->brnhqk', qb, kc, preferred_element_type=jnp.float32) * (Dh ** -0.5)

    steps = jnp.arange(blk)[:, None] + blk - jnp.arange(2 * blk)[None, :]
    band = (steps >= 0) & (steps <= span)
    key_ok = (jnp.arange(nb)[:, None] * blk + jnp.arange(2 * blk)[None, :] - blk) >= 0
    mask = band[None] & key_ok[:, None, :]
    bias = bias_a[:, rel_bucket(steps * dilation)].astype(jnp.float32)
    logits = jnp.where(mask[None, None, :, None], logits + bias[None, None, None], NEG_INF)

    lse = jax.nn.logsumexp(logits, axis=-1)
    p = jnp.exp(logits - lse[..., None])
    out = jnp.einsum('brnhqk,brnkhe->brnqhe', p.astype(v.dtype), vc)
    out = out.reshape(Bsz, dilation, Lp, H, Dh)[:, :, :L].transpose(0, 2, 1, 3, 4).reshape(Bsz, S, H, Dh)
    lse = lse.transpose(0, 1, 2, 4, 3).reshape(Bsz, dilation, Lp, H)[:, :, :L].transpose(0, 2, 1, 3).reshape(Bsz, S, H)
    return out.astype(jnp.float32), lse

def dilated_attention(q, k, v, bias_a):
    outs, lses = [], []
    for window, dilation in A_BRANCHES:
        o, l = dilated_branch(q, k, v, bias_a, window, dilation)
        outs.append(o)
        lses.append(l)
    wts = jax.nn.softmax(jnp.stack(lses), axis=0)
    out = jnp.einsum('gbsh,gbshe->bshe', wts, jnp.stack(outs))
    return out.astype(q.dtype)

def gla(q, k, v, r, a_lr, w_a2, b_a, norm_w):
    f32 = jnp.float32
    Bsz, S, H, dk = q.shape
    dv = v.shape[-1]
    C = B_CHUNK
    N = S // C
    log_a = jax.nn.log_sigmoid((a_lr @ w_a2 + b_a).astype(f32)) / B_GATE_TAU

    def chunks(t):
        return t.astype(f32).reshape(Bsz, N, C, H, -1).transpose(0, 3, 1, 2, 4)

    qc = chunks(q) * (dk ** -0.5)
    kc = chunks(k)
    vc = chunks(v)
    b = jnp.cumsum(chunks(log_a.reshape(Bsz, S, H, dk)), axis=3)

    causal = jnp.tril(jnp.ones((C, C), dtype=bool))
    diff = b[..., :, None, :] - b[..., None, :, :]
    decay = jnp.exp(jnp.where(causal[:, :, None], diff, NEG_INF))
    attn = jnp.einsum('bhnic,bhnjc,bhnijc->bhnij', qc, kc, decay)
    o_intra = jnp.einsum('bhnij,bhnjv->bhniv', attn, vc)

    b_last = b[..., -1, :]
    u = jnp.einsum('bhnjc,bhnjv->bhncv', kc * jnp.exp(b_last[..., None, :] - b), vc)

    def step(state, inp):
        dec, uu = inp
        return dec[..., None] * state + uu, state

    _, s_prev = lax.scan(step, jnp.zeros((Bsz, H, dk, dv), f32),
                         (jnp.moveaxis(jnp.exp(b_last), 2, 0), jnp.moveaxis(u, 2, 0)))
    s_prev = jnp.moveaxis(s_prev, 0, 2)
    o_inter = jnp.einsum('bhnic,bhncv->bhniv', qc * jnp.exp(b), s_prev)

    o = (o_intra + o_inter).transpose(0, 2, 3, 1, 4).reshape(Bsz, S, H, dv)
    o = o * lax.rsqrt(jnp.mean(o * o, axis=-1, keepdims=True) + EPS)
    o = o.reshape(Bsz, S, H * dv) * norm_w.astype(f32) * jax.nn.silu(r.astype(f32))
    return o.astype(q.dtype)

def moba_attention(q, k, v, bias_c):
    f32 = jnp.float32
    Bsz, S, H, Dh = q.shape
    nblk = -(-S // C_BLOCK)
    Sp = nblk * C_BLOCK

    def pad(t):
        return jnp.pad(t, ((0, 0), (0, Sp - S), (0, 0), (0, 0))).transpose(0, 2, 1, 3)

    qp, kp, vp = pad(q), pad(k), pad(v)
    kb = kp.reshape(Bsz, H, nblk, C_BLOCK, Dh)
    vb = vp.reshape(Bsz, H, nblk, C_BLOCK, Dh)
    k_mean = jnp.mean(kb.astype(f32), axis=3)

    qblk = jnp.arange(Sp) // C_BLOCK
    past = jnp.arange(nblk)[None, :] < qblk[:, None]
    gate = jnp.where(past, jnp.einsum('bhsd,bhnd->bhsn', qp.astype(f32), k_mean), NEG_INF)
    topk = min(C_TOPK, nblk)
    _, idx = lax.top_k(gate, topk)
    valid = idx < qblk[None, None, :, None]

    n_q = Sp // C_QCHUNK
    qch = qp.reshape(Bsz, H, n_q, C_QCHUNK, Dh).transpose(2, 0, 1, 3, 4)
    idxch = idx.reshape(Bsz, H, n_q, C_QCHUNK, topk).transpose(2, 0, 1, 3, 4)
    valch = valid.reshape(Bsz, H, n_q, C_QCHUNK, topk).transpose(2, 0, 1, 3, 4)
    b_ix = jnp.arange(Bsz)[:, None, None, None]
    h_ix = jnp.arange(H)[None, :, None, None]
    scale = Dh ** -0.5
    nsel = topk * C_BLOCK

    def one_chunk(args):
        ci, qc_, idx_, val_ = args
        qpos = ci * C_QCHUNK + jnp.arange(C_QCHUNK)
        ksel = kb[b_ix, h_ix, idx_].reshape(Bsz, H, C_QCHUNK, nsel, Dh)
        vsel = vb[b_ix, h_ix, idx_].reshape(Bsz, H, C_QCHUNK, nsel, Dh)
        kpos = (idx_[..., None] * C_BLOCK + jnp.arange(C_BLOCK)).reshape(Bsz, H, C_QCHUNK, nsel)
        l_sel = jnp.einsum('bhqd,bhqkd->bhqk', qc_, ksel, preferred_element_type=f32) * scale
        l_sel = l_sel + bias_c[h_ix, rel_bucket(qpos[None, None, :, None] - kpos)].astype(f32)
        l_sel = jnp.where(jnp.repeat(val_, C_BLOCK, axis=-1), l_sel, NEG_INF)
        own = (ci * C_QCHUNK) // C_BLOCK
        kown = lax.dynamic_slice_in_dim(kp, own * C_BLOCK, C_BLOCK, axis=2)
        vown = lax.dynamic_slice_in_dim(vp, own * C_BLOCK, C_BLOCK, axis=2)
        d_own = qpos[:, None] - (own * C_BLOCK + jnp.arange(C_BLOCK))[None, :]
        l_own = jnp.einsum('bhqd,bhkd->bhqk', qc_, kown, preferred_element_type=f32) * scale
        l_own = jnp.where(d_own[None, None] >= 0, l_own + bias_c[:, rel_bucket(d_own)].astype(f32)[None], NEG_INF)
        p = jax.nn.softmax(jnp.concatenate([l_sel, l_own], axis=-1), axis=-1)
        out = (jnp.einsum('bhqk,bhqkd->bhqd', p[..., :nsel].astype(vsel.dtype), vsel)
               + jnp.einsum('bhqk,bhkd->bhqd', p[..., nsel:].astype(vown.dtype), vown))
        return out

    outs = lax.map(one_chunk, (jnp.arange(n_q), qch, idxch, valch))
    return outs.transpose(1, 0, 3, 2, 4).reshape(Bsz, Sp, H, Dh)[:, :S]

def hybrid_layer(x, norm1_w, w_in, w_a2, b_a, gla_norm_w, w_out, norm2_w, w_ff1, w_ff2, rel_bias):
    Bsz, S, _ = x.shape
    h = rmsnorm(x, norm1_w)
    proj = h @ w_in
    aq, ak, av, bq, bk, bv, br, ba, cq, ck, cv = jnp.split(proj, list(np.cumsum(IN_SIZES)[:-1]), axis=-1)

    def heads(t, n):
        return t.reshape(Bsz, S, n, -1)

    bias_a = rel_bias[:, :A_HEADS].T
    bias_c = rel_bias[:, A_HEADS:].T
    y_a = dilated_attention(heads(aq, A_HEADS), heads(ak, A_HEADS), heads(av, A_HEADS), bias_a)
    y_b = gla(heads(bq, B_HEADS), heads(bk, B_HEADS), heads(bv, B_HEADS), br, ba, w_a2, b_a, gla_norm_w)
    y_c = moba_attention(heads(cq, C_HEADS), heads(ck, C_HEADS), heads(cv, C_HEADS), bias_c)
    mix = jnp.concatenate([y_a.reshape(Bsz, S, A_WIDTH), y_b, y_c.reshape(Bsz, S, C_WIDTH)], axis=-1)
    x = x + mix @ w_out

    h2 = rmsnorm(x, norm2_w)
    x = x + jnp.square(jax.nn.relu(h2 @ w_ff1)) @ w_ff2
    return x

def first_inputs(seed: int = 0) -> dict:
    key = jax.random.key(seed)
    ks = jax.random.split(key, 14)
    f32 = jnp.float32
    nrm = lambda k, shape, s: (jax.random.normal(k, shape, f32) * s)
    return {
        "x": nrm(ks[0], (BATCH, SEQ, D_MODEL), 1.0),
        "norm1_w": 1.0 + nrm(ks[1], (DEPTH, D_MODEL), 0.02),
        "w_in": nrm(ks[2], (DEPTH, D_MODEL, IN_WIDTH), D_MODEL ** -0.5),
        "gla_w_a2": nrm(ks[3], (DEPTH, B_GATE_RANK, B_QK), B_GATE_RANK ** -0.5),
        "gla_b_a": nrm(ks[4], (DEPTH, B_QK), 0.1),
        "gla_norm_w": 1.0 + nrm(ks[5], (DEPTH, B_WIDTH), 0.02),
        "w_out": nrm(ks[6], (DEPTH, MIX_WIDTH, D_MODEL), MIX_WIDTH ** -0.5),
        "norm2_w": 1.0 + nrm(ks[7], (DEPTH, D_MODEL), 0.02),
        "w_ff1": nrm(ks[8], (DEPTH, D_MODEL, D_FF), D_MODEL ** -0.5),
        "w_ff2": nrm(ks[9], (DEPTH, D_FF, D_MODEL), D_FF ** -0.5),
        "rel_bias": nrm(ks[10], (REL_BUCKETS, A_HEADS + C_HEADS), 0.2),
        "final_norm_w": 1.0 + nrm(ks[11], (D_MODEL,), 0.02),
    }

def first_block(x, norm1_w, w_in, gla_w_a2, gla_b_a, gla_norm_w, w_out, norm2_w, w_ff1, w_ff2, rel_bias, final_norm_w):
    for i in range(DEPTH):
        x = hybrid_layer(x, norm1_w[i], w_in[i], gla_w_a2[i], gla_b_a[i], gla_norm_w[i], w_out[i],
                         norm2_w[i], w_ff1[i], w_ff2[i], rel_bias)
    return rmsnorm(x, final_norm_w)


DEPTH_2 = 2

GRID_W = 64
CTX_LEN = 256

MLA_HEADS = 8
QK_NOPE = 64
QK_ROPE = 32
V_HEAD = 64
Q_LORA = 384
KV_LORA = 256
AXIS_ROPE = QK_ROPE // 2
ROPE_BASE = 10000.0
Q_BLOCK = 128

FNET_GROUPS = 4
FNET_GROUP_W = 64
FNET_W = FNET_GROUPS * FNET_GROUP_W

HYENA_W = 256
HYENA_CONV = 3
FILTER_EMB = 33
FILTER_ORDER = 64
DECAY_TARGET = 1e-2
FAST_DECAY_PCT = 0.3
SLOW_DECAY_PCT = 1.5

MLA_W = MLA_HEADS * V_HEAD
MIX_W = MLA_W + FNET_W + HYENA_W
OFF_Q = 0
OFF_KV = OFF_Q + Q_LORA
OFF_KR = OFF_KV + KV_LORA
OFF_F = OFF_KR + QK_ROPE
OFF_H = OFF_F + FNET_W
IN_W = OFF_H + 3 * HYENA_W
D_FF_2 = 4 * D_MODEL
N_MOD = 6


def rms_norm(x, g):
    xf = x.astype(jnp.float32)
    y = xf * lax.rsqrt(jnp.mean(xf * xf, axis=-1, keepdims=True) + EPS)
    return (y * g.astype(jnp.float32)).astype(x.dtype)

def modulation(cvec, w_mod, b_mod):
    m = (jax.nn.silu(cvec) @ w_mod + b_mod).reshape(-1, 1, N_MOD * D_MODEL)
    return jnp.split(m, N_MOD, axis=-1)

def modulate(h, shift, scale):
    return h * (1.0 + scale) + shift

def grid_rope_tables(n_tokens, dtype):
    rows = n_tokens // GRID_W
    row = jnp.repeat(jnp.arange(rows, dtype=jnp.float32), GRID_W)
    col = jnp.tile(jnp.arange(GRID_W, dtype=jnp.float32), rows)
    inv = ROPE_BASE ** (-jnp.arange(0, AXIS_ROPE, 2, dtype=jnp.float32) / AXIS_ROPE)
    ang = jnp.concatenate([row[:, None] * inv, col[:, None] * inv], axis=-1)
    return jnp.cos(ang).astype(dtype), jnp.sin(ang).astype(dtype)

def _rotate_half(v, cos, sin):
    half = v.shape[-1] // 2
    v1, v2 = v[..., :half], v[..., half:]
    return jnp.concatenate([v1 * cos - v2 * sin, v1 * sin + v2 * cos], axis=-1)

def apply_axial_rope(x, cos, sin):
    n = AXIS_ROPE // 2
    return jnp.concatenate([
        _rotate_half(x[..., :AXIS_ROPE], cos[..., :n], sin[..., :n]),
        _rotate_half(x[..., AXIS_ROPE:], cos[..., n:], sin[..., n:])], axis=-1)

def mla_queries(p, q_norm_g, w_uq, rope):
    B, L, _ = p.shape
    cq = rms_norm(p[..., OFF_Q:OFF_KV], q_norm_g)
    q = (cq @ w_uq).reshape(B, L, MLA_HEADS, QK_NOPE + QK_ROPE)
    q_nope, q_rope = q[..., :QK_NOPE], q[..., QK_NOPE:]
    if rope is not None:
        cos, sin = rope
        q_rope = apply_axial_rope(q_rope, cos[:, None, :], sin[:, None, :])
    return q_nope, q_rope

def mla_keys_values(p_kv, kv_norm_g, w_ukv, rope):
    B, L, _ = p_kv.shape
    ckv = rms_norm(p_kv[..., :KV_LORA], kv_norm_g)
    kv = (ckv @ w_ukv).reshape(B, L, MLA_HEADS, QK_NOPE + V_HEAD)
    k_rope = p_kv[..., KV_LORA:]
    if rope is not None:
        k_rope = apply_axial_rope(k_rope, *rope)
    return kv[..., :QK_NOPE], k_rope, kv[..., QK_NOPE:]

def mla_attention(q_nope, q_rope, k_nope, k_rope, v):
    B, L, H, _ = q_nope.shape
    nb = L // Q_BLOCK
    scale = 1.0 / math.sqrt(QK_NOPE + QK_ROPE)

    def to_blocks(t):
        return jnp.moveaxis(t.reshape(B, nb, Q_BLOCK, *t.shape[2:]), 1, 0)

    def block(qs):
        qn, qr = qs
        s = (jnp.einsum('bqhd,bkhd->bhqk', qn, k_nope)
             + jnp.einsum('bqhr,bkr->bhqk', qr, k_rope))
        prob = jax.nn.softmax(s.astype(jnp.float32) * scale, axis=-1).astype(v.dtype)
        return jnp.einsum('bhqk,bkhd->bqhd', prob, v)

    o = lax.map(block, (to_blocks(q_nope), to_blocks(q_rope)))
    return jnp.moveaxis(o, 0, 1).reshape(B, L, H * V_HEAD)

def fourier_mix(u):
    B, L, _ = u.shape
    g = u.reshape(B, L, FNET_GROUPS, FNET_GROUP_W).astype(jnp.float32)
    f = jnp.fft.fftn(g, axes=(1, 3), norm="ortho").real
    return f.reshape(B, L, FNET_W).astype(u.dtype)

def short_conv(u, w, b):
    L = u.shape[1]
    pad = (HYENA_CONV - 1) // 2
    up = jnp.pad(u, ((0, 0), (pad, HYENA_CONV - 1 - pad), (0, 0)))
    out = b
    for k in range(HYENA_CONV):
        out = out + up[:, k:k + L] * w[k]
    return out

def hyena_filters(L, w1, b1, freq, w2, b2, w3):
    f32 = jnp.float32
    t = jnp.linspace(0.0, 1.0, L, dtype=f32)[:, None]
    bands = (FILTER_EMB - 1) // 2
    fr = jnp.linspace(1e-4, bands - 1, bands, dtype=f32)
    ang = 2.0 * math.pi * jnp.arange(L, dtype=f32)[:, None] / L * fr
    z = jnp.concatenate([t, jnp.cos(ang), -jnp.sin(ang)], axis=-1)
    h = jnp.sin(freq * (z.astype(w1.dtype) @ w1 + b1))
    h = jnp.sin(freq * (h @ w2 + b2))
    h = (h @ w3).astype(f32)
    min_decay = math.log(DECAY_TARGET) / SLOW_DECAY_PCT
    max_decay = math.log(DECAY_TARGET) / FAST_DECAY_PCT
    deltas = jnp.abs(jnp.linspace(min_decay, max_decay, HYENA_W, dtype=f32))
    decay = jnp.exp(-t * deltas)
    h = h * jnp.tile(decay, (1, 2))
    h_fwd, h_bwd = h[:, :HYENA_W], h[:, HYENA_W:]
    k = jnp.concatenate([h_fwd, jnp.zeros((1, HYENA_W), f32), h_bwd[:0:-1]], axis=0)
    return k / jnp.sum(jnp.abs(k), axis=0, keepdims=True)

def hyena_mix(u, conv_w, conv_b, w1, b1, freq, w2, b2, w3, d_bias):
    B, L, _ = u.shape
    u = short_conv(u, conv_w, conv_b)
    x0, x1, v = jnp.split(u, 3, axis=-1)
    z = (x1 * v).astype(jnp.float32)
    k = hyena_filters(L, w1, b1, freq, w2, b2, w3)
    zf = jnp.fft.rfft(z, n=2 * L, axis=1)
    kf = jnp.fft.rfft(k, n=2 * L, axis=0)
    y = jnp.fft.irfft(zf * kf[None], n=2 * L, axis=1)[:, :L] + d_bias.astype(jnp.float32) * z
    return (x0.astype(jnp.float32) * y).astype(u.dtype)

def heads_out(att, p, hy, w_out):
    f = fourier_mix(p[..., OFF_F:OFF_H])
    hz = hyena_mix(p[..., OFF_H:], *hy)
    return jnp.concatenate([att, f, hz], axis=-1) @ w_out

def sq_relu_mlp(h, w1, w2):
    return jnp.square(jax.nn.relu(h @ w1)) @ w2

def second_inputs(seed: int = 0) -> dict:
    key = jax.random.key(seed)
    ks = jax.random.split(key, 26)

    def nrm(k, shape, scale):
        return jax.random.normal(k, shape, jnp.float32) * scale

    D = D_MODEL
    return {
        "x": nrm(ks[0], (BATCH, SEQ, D), 1.0),
        "c": nrm(ks[1], (BATCH, D), 1.0),
        "ctx": nrm(ks[2], (BATCH, CTX_LEN, D), 1.0),
        "c_ctx": nrm(ks[3], (D,), 1.0),
        "norm1_g": 1.0 + nrm(ks[4], (DEPTH_2, D), 0.05),
        "norm2_g": 1.0 + nrm(ks[5], (DEPTH_2, D), 0.05),
        "w_mod": nrm(ks[6], (DEPTH_2, D, N_MOD * D), 0.5 * D ** -0.5),
        "b_mod": nrm(ks[7], (DEPTH_2, N_MOD * D), 0.01),
        "w_in": nrm(ks[8], (DEPTH_2, D, IN_W), D ** -0.5),
        "q_norm_g": 1.0 + nrm(ks[9], (DEPTH_2, Q_LORA), 0.05),
        "kv_norm_g": 1.0 + nrm(ks[10], (DEPTH_2, KV_LORA), 0.05),
        "w_uq": nrm(ks[11], (DEPTH_2, Q_LORA, MLA_HEADS * (QK_NOPE + QK_ROPE)), Q_LORA ** -0.5),
        "w_ukv": nrm(ks[12], (DEPTH_2, KV_LORA, MLA_HEADS * (QK_NOPE + V_HEAD)), KV_LORA ** -0.5),
        "hy_conv_w": nrm(ks[13], (DEPTH_2, HYENA_CONV, 3 * HYENA_W), HYENA_CONV ** -0.5),
        "hy_conv_b": nrm(ks[14], (DEPTH_2, 3 * HYENA_W), 0.01),
        "hy_w1": nrm(ks[15], (DEPTH_2, FILTER_EMB, FILTER_ORDER), FILTER_EMB ** -0.5),
        "hy_b1": nrm(ks[16], (DEPTH_2, FILTER_ORDER), 0.1),
        "hy_freq": 1.0 + nrm(ks[17], (DEPTH_2, FILTER_ORDER), 0.05),
        "hy_w2": nrm(ks[18], (DEPTH_2, FILTER_ORDER, FILTER_ORDER), FILTER_ORDER ** -0.5),
        "hy_b2": nrm(ks[19], (DEPTH_2, FILTER_ORDER), 0.1),
        "hy_w3": nrm(ks[20], (DEPTH_2, FILTER_ORDER, 2 * HYENA_W), FILTER_ORDER ** -0.5),
        "hy_d": nrm(ks[21], (DEPTH_2, HYENA_W), 0.5),
        "w_out": nrm(ks[22], (DEPTH_2, MIX_W, D), MIX_W ** -0.5),
        "w_mlp1": nrm(ks[23], (DEPTH_2, D, D_FF_2), D ** -0.5),
        "w_mlp2": nrm(ks[24], (DEPTH_2, D_FF_2, D), D_FF_2 ** -0.5),
        "final_norm_g": 1.0 + nrm(ks[25], (D,), 0.05),
    }

def second_block(x, c, ctx, c_ctx, norm1_g, norm2_g, w_mod, b_mod, w_in, q_norm_g, kv_norm_g,
              w_uq, w_ukv, hy_conv_w, hy_conv_b, hy_w1, hy_b1, hy_freq, hy_w2, hy_b2, hy_w3,
              hy_d, w_out, w_mlp1, w_mlp2, final_norm_g):
    L = x.shape[1]
    rope = grid_rope_tables(L, x.dtype)
    xc = ctx
    for l in range(DEPTH_2):
        last = l == DEPTH_2 - 1
        hy = (hy_conv_w[l], hy_conv_b[l], hy_w1[l], hy_b1[l], hy_freq[l],
              hy_w2[l], hy_b2[l], hy_w3[l], hy_d[l])
        sh1, sc1, g1, sh2, sc2, g2 = modulation(c, w_mod[l], b_mod[l])
        csh1, csc1, cg1, csh2, csc2, cg2 = modulation(c_ctx, w_mod[l], b_mod[l])

        hx = modulate(rms_norm(x, norm1_g[l]), sh1, sc1)
        hc = modulate(rms_norm(xc, norm1_g[l]), csh1, csc1)
        px = hx @ w_in[l]
        if last:
            pc_kv = hc @ w_in[l][:, OFF_KV:OFF_F]
        else:
            pc = hc @ w_in[l]
            pc_kv = pc[..., OFF_KV:OFF_F]
        kn_c, kr_c, v_c = mla_keys_values(pc_kv, kv_norm_g[l], w_ukv[l], None)
        kn_x, kr_x, v_x = mla_keys_values(px[..., OFF_KV:OFF_F], kv_norm_g[l], w_ukv[l], rope)
        qn_x, qr_x = mla_queries(px, q_norm_g[l], w_uq[l], rope)
        att_x = mla_attention(qn_x, qr_x,
                              jnp.concatenate([kn_x, kn_c], axis=1),
                              jnp.concatenate([kr_x, kr_c], axis=1),
                              jnp.concatenate([v_x, v_c], axis=1))
        x = x + g1 * heads_out(att_x, px, hy, w_out[l])

        x = x + g2 * sq_relu_mlp(modulate(rms_norm(x, norm2_g[l]), sh2, sc2), w_mlp1[l], w_mlp2[l])

        if not last:
            qn_c, qr_c = mla_queries(pc, q_norm_g[l], w_uq[l], None)
            att_c = mla_attention(qn_c, qr_c, kn_c, kr_c, v_c)
            xc = xc + cg1 * heads_out(att_c, pc, hy, w_out[l])
            xc = xc + cg2 * sq_relu_mlp(modulate(rms_norm(xc, norm2_g[l]), csh2, csc2),
                                        w_mlp1[l], w_mlp2[l])
    return rms_norm(x, final_norm_g)


def setup_inputs(seed=0):
    out = dict(first_inputs(seed))
    for name, value in second_inputs(seed + 1).items():
        if name != "x":
            out[name + "_2"] = value
    return out


def reference(
    x, norm1_w, w_in, gla_w_a2, gla_b_a, gla_norm_w, w_out, norm2_w, w_ff1, w_ff2, rel_bias,
    final_norm_w, c_2, ctx_2, c_ctx_2, norm1_g_2, norm2_g_2, w_mod_2, b_mod_2, w_in_2,
    q_norm_g_2, kv_norm_g_2, w_uq_2, w_ukv_2, hy_conv_w_2, hy_conv_b_2, hy_w1_2, hy_b1_2,
    hy_freq_2, hy_w2_2, hy_b2_2, hy_w3_2, hy_d_2, w_out_2, w_mlp1_2, w_mlp2_2, final_norm_g_2,
):
    x = first_block(
        x, norm1_w, w_in, gla_w_a2, gla_b_a, gla_norm_w, w_out, norm2_w, w_ff1, w_ff2, rel_bias,
        final_norm_w,
    )
    return second_block(
        x, c_2, ctx_2, c_ctx_2, norm1_g_2, norm2_g_2, w_mod_2, b_mod_2, w_in_2, q_norm_g_2,
        kv_norm_g_2, w_uq_2, w_ukv_2, hy_conv_w_2, hy_conv_b_2, hy_w1_2, hy_b1_2, hy_freq_2,
        hy_w2_2, hy_b2_2, hy_w3_2, hy_d_2, w_out_2, w_mlp1_2, w_mlp2_2, final_norm_g_2,
    )


_drawn_inputs = setup_inputs


def setup_inputs(seed=0):
    import zlib

    import numpy as np

    out = dict(_drawn_inputs(seed))
    spreads = {}
    factors = {'norm1_w': 3.53,
     'gla_b_a': 3.81,
     'gla_norm_w': 8.0,
     'norm2_w': 3.112,
     'final_norm_w': 2.7,
     'ctx_2': 4.752,
     'norm1_g_2': 3.416,
     'q_norm_g_2': 8.0,
     'kv_norm_g_2': 8.0,
     'hy_conv_b_2': 8.0,
     'hy_b1_2': 7.602,
     'hy_freq_2': 8.0,
     'hy_b2_2': 5.654,
     'norm2_g_2': 4.334}
    for name, (base, spread) in spreads.items():
        noise = np.random.default_rng([zlib.crc32(name.encode()), seed]).standard_normal(out[name].shape)
        drawn = base * np.exp(spread * noise) if base else spread * noise
        out[name] = __import__('jax').numpy.asarray(drawn.astype(out[name].dtype))
    for name, factor in factors.items():
        out[name] = (out[name] * factor).astype(out[name].dtype)
    return out
```

```python
import math
from contextlib import ExitStack

import numpy as np

import concourse.bass as bass
from concourse import mybir

F32 = mybir.dt.float32
ALU = mybir.AluOpType
ACT = mybir.ActivationFunctionType
AX = mybir.AxisListType

P = 128
D = 1024
KT = D // P
S = 512
SC = 256
T2 = S + SC
DH = 64
EPS = 1e-6
A_HEADS = B_HEADS_ = 6
B_HEADS, B_DK, B_DV, B_RANK, B_CHUNK, B_TAU = 4, 32, 64, 16, 16, 16.0
C_HEADS = 6
NCHUNK = S // B_CHUNK
REL_BUCKETS, REL_MAX = 32, 2048
F = 4 * D
FT = F // P
HALF_FT = FT // 2
MH = 8
NOPE, ROPE = 64, 32
QL, KVL = 384, 256
HY = 256
SLOT = 1024
RING = 8
NEG = -1e30
STRIP = 640


def rel_bucket(n):
    n = np.maximum(n, 0)
    exact = REL_BUCKETS // 2
    logv = (np.log(np.maximum(n, 1).astype(np.float32) / exact) / np.float32(math.log(REL_MAX / exact)))
    large = np.minimum(exact + (logv * (REL_BUCKETS - exact)).astype(np.int32), REL_BUCKETS - 1)
    return np.where(n < exact, n, large)


def shape_constants():
    f64 = np.float64
    c = {}
    c["ident"] = np.eye(P)
    c["flip"] = np.eye(P)[::-1]
    c["ones"] = np.ones((P, P))
    two = (np.arange(P)[:, None] // 32 % 2) == (np.arange(P)[None, :] // 64)
    c["spread"] = two.astype(f64)
    c["mean64"] = (np.arange(P)[:, None] // 64 == np.arange(P)[None, :] // 64) / 64.0
    c["in_chunk"] = (np.arange(P)[:, None] // B_CHUNK == np.arange(P // B_CHUNK)[None, :]).astype(f64)
    c["not_first"] = np.tile((np.arange(S) % B_CHUNK != 0).astype(f64), (P, 1))
    dist = S - 1 - np.arange(STRIP)
    c["bucket_of"] = np.zeros((P, STRIP))
    c["bucket_of"][:REL_BUCKETS] = np.arange(REL_BUCKETS)[:, None] == rel_bucket(dist)[None, :]
    times = (dist <= 128) * 1.0 + (dist % 4 == 0) + (dist % 16 == 0)
    log_a = np.where((dist >= 0) & (times > 0), np.log(np.maximum(times, 1)), NEG)
    c["log_reach"] = np.zeros((P, STRIP))
    c["log_reach"][:A_HEADS] = log_a
    c["log_reach"][A_HEADS:A_HEADS + C_HEADS] = np.where(dist >= 0, 0.0, NEG)
    inv = (np.float32(10000.0) ** (-np.arange(0, 16, 2, dtype=np.float32) / 16)).astype(np.float32)
    tok = np.arange(S)
    ang = np.concatenate([(tok // 64).astype(np.float32)[:, None] * inv, (tok % 64).astype(np.float32)[:, None] * inv], 1)
    j = np.arange(ROPE)
    which = j // 16 * 8 + j % 8
    c["rope"] = np.zeros((P, S))
    c["rope"][64:96] = np.cos(ang)[:, which].T
    c["rope"][96:128] = (np.sin(ang)[:, which] * np.where(j % 16 < 8, -1.0, 1.0)).T
    g = np.arange(P)
    same = g[:, None] // 64 == g[None, :] // 64
    a = 2 * np.pi * ((g[:, None] % 64) * (g[None, :] % 64) % 64) / 64
    c["dft64"] = np.concatenate([np.cos(a) * same, np.sin(a) * same], 1)
    return {k: v.astype(np.float32) for k, v in c.items()}


CONSTS = ["ident", "flip", "ones", "spread", "mean64", "in_chunk", "not_first", "bucket_of", "log_reach", "rope", "dft64"]
CONST_W = {"ident": P, "flip": P, "ones": P, "spread": P, "mean64": P, "in_chunk": P // B_CHUNK, "not_first": S,
           "bucket_of": STRIP, "log_reach": STRIP, "rope": S, "dft64": 2 * P}


def slots_of(table):
    k, m = table.shape
    return np.ascontiguousarray(table.reshape(k // P, P, m).transpose(1, 0, 2).reshape(P, -1))


def sequence_tables():
    out = {}
    for L, name in ((S, "x"), (SC, "c")):
        t = np.arange(L)
        a = 2 * np.pi * (t[:, None] * t[None, :] % L) / L
        n = 1.0 / math.sqrt(L * 64)
        rows = [np.concatenate([np.cos(a[i:i + P]) * n, -np.sin(a[i:i + P]) * n], 1) for i in range(0, L, P)]
        out["fourier_" + name] = rows
        w = np.pi * (t[:, None] * (2 * t[None, :] + 1) % (4 * L)) / (2 * L) * 1.0
        w = 2 * np.pi * (t[:, None] * (2 * t[None, :] + 1) % (4 * L)) / (4 * L)
        out["fwd_" + name] = [np.concatenate([slots_of(np.cos(w[:, i:i + P])), slots_of(-np.sin(w[:, i:i + P]))], 1)
                              for i in range(0, L, P)]
        out["inv_" + name] = [np.concatenate([np.cos(w.T[i:i + P]) / L, -np.sin(w.T[i:i + P]) / L], 1)
                              for i in range(0, L, P)]
        pos = np.linspace(0.0, 1.0, L, dtype=np.float32)[:, None]
        fr = np.linspace(1e-4, 15, 16, dtype=np.float32)
        ang = (np.float32(2.0 * math.pi) * t.astype(np.float32)[:, None] / np.float32(L) * fr).astype(np.float32)
        z = np.concatenate([pos, np.cos(ang), -np.sin(ang)], 1)
        lo, hi = math.log(1e-2) / 1.5, math.log(1e-2) / 0.3
        deltas = np.abs(np.linspace(lo, hi, HY, dtype=np.float32))
        decay = np.exp(-pos * deltas)
        decay = np.concatenate([decay, decay], 1)
        decay[0, HY:] = 0.0
        decay = slots_of(decay)
        zt = np.zeros((P, L))
        zt[:33] = z.T
        out["emb_" + name] = [zt]
        out["decay_" + name] = [decay[:, i:i + SLOT] for i in range(0, decay.shape[1], SLOT)]
    flat, at = [], {}
    for k, rows in out.items():
        at[k] = (len(flat), len(rows), rows[0].shape[1])
        for r in rows:
            full = np.zeros((P, SLOT), np.float32)
            full[:, :r.shape[1]] = r
            flat.append(full)
    return np.stack(flat), at


def vec_plan():
    plan, at = {}, 0
    for name, n in [("norm1", 8), ("norm2", 8), ("final1", 8), ("gla_norm", 2), ("gla_b", 1), ("final2", 8)] + [
            (f"{name}{l}", n) for l in range(2) for name, n in (
                ("n1_", 8), ("n2_", 8), ("qn_", 3), ("kvn_", 2), ("bmod_", 48), ("cw_", 18), ("cb_", 6), ("hd_", 2),
                ("fb1_", 1), ("ffr_", 1), ("fb2_", 1))]:
        plan[name] = (at, n)
        at += n
    return plan, at


VEC, VECS = vec_plan()


class Lane:

    def __init__(self, sem):
        self.sem, self.count, self.queue, self.seen = sem, 0, [], {}

    def wait(self, *after):
        for mark in marks(after):
            sem, value = mark
            if self.seen.get(id(sem), 0) < value:
                self.seen[id(sem)] = value
                self.queue.append(lambda eng, sem=sem, value=value: eng.wait_ge(sem, value))

    def issue(self, instruction, *after, signal=True):
        self.wait(*after)
        if signal:
            self.count += 1
            self.queue.append(lambda eng: instruction(eng).then_inc(self.sem, 1))
        else:
            self.queue.append(instruction)
        return (self.sem, self.count)

    def dma(self, sem, total, instruction, *after):
        self.wait(*after)
        self.queue.append(lambda eng: instruction(eng).then_inc(sem, 16))
        return (sem, total)

    def now(self):
        return (self.sem, self.count) if self.count else None

    def run(self, eng):
        for instruction in self.queue:
            instruction(eng)


def marks(x):
    if x is None:
        return
    if isinstance(x, tuple) and len(x) == 2 and isinstance(x[1], int):
        yield x
        return
    for y in x:
        yield from marks(y)


def build(nc, dr, out_t, at):
    plan = at
    with ExitStack() as top:
        def sem(name):
            return top.enter_context(nc.semaphore(name))

        pe, dve, act, pool, sp = (Lane(sem(n)) for n in ("pe_step", "dve_step", "act_step", "pool_step", "sp_step"))
        lanes = [pe, dve, act, pool]

        def sb(scope, name, shape):
            return scope.enter_context(nc.sbuf_tensor(name, shape, F32))

        def fence():
            all_now = [lane.now() for lane in lanes]
            for lane in lanes:
                lane.wait(all_now)

        ring = sb(top, "weight_ring", [P, RING, SLOT])
        X = sb(top, "residual", [P, KT, T2])
        H = sb(top, "normed_or_mix", [P, KT, T2])
        C = {n: sb(top, "c_" + n, [P, CONST_W[n]]) for n in CONSTS if n not in ("bucket_of", "log_reach")}
        vecs = sb(top, "vecs", [P, VECS])
        R = sb(top, "inv_rms", [P, T2])
        SQ = sb(top, "squares", [P, 2, T2])
        MOD = sb(top, "modulation", [P, 2, 2, 48])
        GS = sb(top, "gain_scale", [P, 2, 2, 2, KT])
        psum = top.enter_context(nc.psum_tensor("psum", [P, 8, 512], F32))

        def vec(name, i=0, rows=P):
            return vecs[0:rows, VEC[name][0] + i:VEC[name][0] + i + 1]

        ring_sem = [sem(f"ring_{i}") for i in range(RING)]
        ring_free = [None] * RING
        ring_at = [0]

        def load(src, width=SLOT):
            i = ring_at[0]
            ring_at[0] += 1
            k = i % RING
            mark = sp.dma(ring_sem[k], 16 * (i // RING + 1),
                          lambda eng: eng.dma_start(ring[:, k, 0:width], src), ring_free[k])
            return k, mark

        def free_slot(k, mark):
            ring_free[k] = mark

        bank_free = [None] * 8
        next_bank = {1: 0, 2: 0}

        def take(n=1):
            if n == 2:
                b = 2 * (next_bank[2] % 4)
                next_bank[2] += 1
                next_bank[1] = b + 2
            else:
                b = next_bank[1] % 8
                next_bank[1] += 1
            return b

        def bank(b, w=512, n=1):
            if n == 1:
                return psum[:, b, 0:w]
            return psum[:, b:b + 2, :].rearrange("p b w -> p (b w)")[:, 0:w]

        def mm(out, lhsT, rhs, start, stop, *after, signal=False):
            return pe.issue(lambda eng: eng.matmul(out, lhsT, rhs, start=start, stop=stop), *after, signal=signal)

        side = [0]

        def copy(out, in_, *after):
            side[0] += 1
            if side[0] % 2:
                return act.issue(lambda eng: eng.copy(out, in_), *after)
            return dve.issue(lambda eng: eng.tensor_copy(out, in_), *after)

        def v_tt(out, a, b, op, *after, lane=None):
            return (lane or dve).issue(lambda eng: eng.tensor_tensor(out, a, b, op), *after)

        def v_ts(out, a, s1, s2, op0, op1, *after, lane=None):
            if s2 is None:
                return (lane or dve).issue(lambda eng: eng.tensor_scalar(out, a, s1, None, op0), *after)
            return (lane or dve).issue(lambda eng: eng.tensor_scalar(out, a, s1, s2, op0, op1), *after)

        def v_stt(out, a, s, b, op0, op1, *after):
            return dve.issue(lambda eng: eng.scalar_tensor_tensor(out=out, in0=a, scalar=s, in1=b, op0=op0, op1=op1), *after)

        def fn(out, in_, f, *after, **kw):
            return act.issue(lambda eng: eng.activation(out, in_, f, **kw), *after)

        def zero(lane, out, *after, value=0.0):
            return lane.issue(lambda eng: eng.memset(out, value), *after)

        def recip(out, in_, *after):
            return dve.issue(lambda eng: eng.reciprocal(out, in_), *after)

        def neg_rowmax(out, in_, *after):
            return dve.issue(lambda eng: eng.tensor_reduce(out, in_, AX.X, ALU.max, negate=True), *after)

        def turn(out, in_, *after, signal=True):
            return pe.issue(lambda eng: eng.transpose(out, in_, C["ident"][:, :]), *after, signal=signal)

        def copy_on(lane, out, in_, *after):
            if lane is act:
                return act.issue(lambda eng: eng.copy(out, in_), *after)
            return lane.issue(lambda eng: eng.tensor_copy(out, in_), *after)

        def scan(out, decay, add, *after):
            return dve.issue(lambda eng: eng.tensor_tensor_scan(out, decay, add, 0.0, ALU.mult, ALU.add), *after)

        def dot(scratch, a, b, out, *after):
            return dve.issue(lambda eng: eng.tensor_tensor_reduce(out=scratch, in0=a, in1=b, scale=1.0, scalar=0.0,
                                                                  op0=ALU.mult, op1=ALU.add, accum_out=out), *after)

        def dma(lane, sem_, total, dst, src, *after):
            return lane.dma(sem_, total, lambda eng: eng.dma_start(dst, src), *after)

        X1, XB = [(0, S)], [(0, S), (S, T2)]

        got = sem("small_inputs")
        n_got = [0]

        def fetch(dst, src):
            n_got[0] += 16
            return dma(act, got, n_got[0], dst, src)

        small = {}
        for name, rows, cols in (("w_a2", B_RANK, P), ("rel_bias", REL_BUCKETS, A_HEADS + C_HEADS),
                                 ("fw1", 33, 128), ("fw2", 64, 128), ("fw3", 64, 1024)):
            small[name] = sb(top, "s_" + name, [P, cols])
            fetch(small[name][0:rows, :], dr[name])
        for n in C:
            fetch(C[n][:, :], dr["c_" + n])
        fetch(vecs[:, :], dr["vecs"])
        fetch(X[:, :, 0:S], dr["x_t"])
        loaded = fetch(X[:, :, S:T2], dr["ctx_t"])
        for lane in lanes:
            lane.wait(loaded)

        def inv_rms(src, nt, ranges, n, ready, dst=None):
            dst = R if dst is None else dst
            lo, hi = ranges[0][0], ranges[-1][1]
            b = take(len(ranges))
            read = [None, None]
            last = None
            for t in range(nt):
                sq = fn(SQ[:, t % 2, lo:hi], src(t)[:, lo:hi], ACT.Square, ready[t] if isinstance(ready, list) else ready, read[t % 2],
                        [dve.now(), pe.now()] if t < 2 else None)
                for r, (a, z) in enumerate(ranges):
                    last = mm(bank(b + r, z - a), C["ones"][:, :], SQ[:, t % 2, a:z], t == 0, t == nt - 1,
                              sq, bank_free[b + r] if t == 0 else None, signal=r == len(ranges) - 1)
                read[t % 2] = last
            for r, (a, z) in enumerate(ranges):
                m = v_ts(dst[:, a:z], bank(b + r, z - a), 1.0 / n, EPS, ALU.mult, ALU.add, last)
                bank_free[b + r] = m
            m = fn(dst[:, lo:hi], dst[:, lo:hi], ACT.Sqrt, m)
            return recip(dst[:, lo:hi], dst[:, lo:hi], m)

        def normed(src, dst, nt, ranges, gain, ready, shift=None):
            out = []
            for t in range(nt):
                ms = []
                for r, (a, z) in enumerate(ranges):
                    m = v_stt(dst(t)[:, a:z], src(t)[:, a:z], gain(t, r), R[:, a:z], ALU.mult, ALU.mult, ready)
                    if shift is not None:
                        m = fn(dst(t)[:, a:z], dst(t)[:, a:z], ACT.Identity, m, bias=shift(t, r), scale=1.0)
                    ms.append(m)
                out.append(ms)
            return out

        def product(chunks, M, x, x_ready, ranges, take_out, rows=0):
            b = take(len(ranges))
            total = sum(c[1] for c in chunks)
            k, last = 0, None
            for src, nk in chunks:
                slot, landed = load(src, nk * M)
                for j in range(nk):
                    for r, (lo, hi) in enumerate(ranges):
                        last = mm(psum[rows:rows + M, b + r, 0:hi - lo], ring[:, slot, j * M:(j + 1) * M], x(k, lo, hi),
                                  k == 0, k == total - 1, landed, x_ready[k] if isinstance(x_ready, list) else x_ready,
                                  bank_free[b + r] if k == 0 else None,
                                  signal=(j == nk - 1 and r == len(ranges) - 1))
                    k += 1
                free_slot(slot, last)
            for r, (lo, hi) in enumerate(ranges):
                bank_free[b + r] = take_out(psum[rows:rows + M, b + r, 0:hi - lo], lo, hi, last)

        def mlp(w1, w2, ranges, x_ready, gate, next_mod):
            with ExitStack() as scope:
                G = sb(scope, f"hidden_{next_mod}", [P, HALF_FT, T2])
                side_work = iter(()) if next_mod is None else modulation(next_mod, scope)

                def filler():
                    next(side_work, None)
                filler()
                fence()
                lo, hi = ranges[0][0], ranges[-1][1]
                done = None
                for half in range(2):
                    g_ready = []
                    for m in range(HALF_FT):
                        ms = []

                        def relu(ps, a, z, mark, m=m, ms=ms, done=done):
                            got_it = fn(G[:, m, a:z], ps, ACT.Relu, mark, done)
                            ms.append(v_tt(G[:, m, a:z], G[:, m, a:z], G[:, m, a:z], ALU.mult, got_it, lane=pool))
                            return got_it
                        product([(w1[half * HALF_FT + m], KT)], P, lambda k, a, z: H[:, k, a:z], x_ready, ranges, relu)
                        g_ready.append(ms)
                        filler()
                    for m in range(KT):
                        def add(ps, a, z, mark, m=m):
                            if gate is None:
                                return v_tt(X[:, m, a:z], ps, X[:, m, a:z], ALU.add, mark)
                            return v_stt(X[:, m, a:z], ps, gate(m, a), X[:, m, a:z], ALU.mult, ALU.add, mark)
                        product([(w2[half, m, s], KT) for s in range(2)], P, lambda k, a, z: G[:, k, a:z], g_ready, ranges, add)
                        filler()
                    done = pe.now()
                for _ in side_work:
                    pass
                fence()

        def attention(scope, tag, units, scale, q_of, k_of, v_of, strip_of, put, kmax):
            NP = 3
            Pb = sb(scope, tag + "_prob", [P, NP, kmax])
            PT = sb(scope, tag + "_probT", [P, 2, kmax // P, S])
            st = sb(scope, tag + "_stat", [P, NP, 4])
            Dg = sb(scope, tag + "_diag", [P, NP, P])
            fence()
            items = [(u, i) for u, unit in enumerate(units) for i in range(len(unit[1]))]
            info = [dict() for _ in items]
            pt_read = [None, None]
            pt_done = {}

            def logits(n):
                u, i = items[n]
                head, qs, k0 = units[u]
                q0, w = qs[i]
                nb = 1 if w <= 512 else 2
                b = take(nb)
                for off in range(0, w, 512):
                    pw = min(512, w - off)
                    m = mm(psum[:, b + off // 512, 0:pw], q_of(head, q0, q0 + P), k_of(head, k0 + off, k0 + off + pw),
                           True, True, bank_free[b + off // 512], signal=off + 512 >= w)
                info[n].update(bank=b, nb=nb, w=w, head=head, q0=q0, logits=m)

            def exps(n):
                d = info[n]
                w, j = d["w"], n % NP
                s = bank(d["bank"], w, d["nb"])
                free = info[n - NP]["pt"] if n >= NP else None
                if strip_of is not None:
                    m = v_stt(Pb[:, j, 0:w], s, scale, strip_of(d["head"], d["q0"], w), ALU.mult, ALU.add, d["logits"], free)
                    bank_free[d["bank"]] = m
                    m = neg_rowmax(st[:, j, 0:1], Pb[:, j, 0:w], m)
                    m = fn(Pb[:, j, 0:w], Pb[:, j, 0:w], ACT.Exp, m, bias=st[:, j, 0:1], scale=1.0, accum_out=st[:, j, 1:2])
                else:
                    m = neg_rowmax(st[:, j, 2:3], s, d["logits"], free)
                    m = v_ts(st[:, j, 0:1], st[:, j, 2:3], scale, None, ALU.mult, None, m)
                    m = fn(Pb[:, j, 0:w], s, ACT.Exp, m, free, bias=st[:, j, 0:1], scale=scale, accum_out=st[:, j, 1:2])
                    for r in range(d["nb"]):
                        bank_free[d["bank"] + r] = m
                d["exp"] = m

            def diag(n):
                d = info[n]
                j = n % NP
                m = recip(st[:, j, 3:4], st[:, j, 1:2], d["exp"])
                d["diag"] = v_ts(Dg[:, j, :], C["ident"][:, :], st[:, j, 3:4], None, ALU.mult, None, m,
                                 info[n - NP]["pt"] if n >= NP else None)

            def turn_p(n):
                u, i = items[n]
                d = info[n]
                j = n % NP
                nk = d["w"] // P
                col = d["q0"] - units[u][1][0][0]
                last = None
                for g in range(0, nk, 4):
                    b = take(1)
                    gn = min(4, nk - g)
                    for t in range(gn):
                        last = mm(psum[:, b, t * P:(t + 1) * P], Pb[:, j, (g + t) * P:(g + t + 1) * P], Dg[:, j, :],
                                  True, True, d["exp"], d["diag"], bank_free[b] if t == 0 else None, signal=t == gn - 1)
                    m = copy(PT[:, u % 2, g:g + gn, col:col + P], psum[:, b, 0:gn * P].rearrange("p (t q) -> p t q", q=P),
                             last, pt_read[u % 2] if i == 0 else None)
                    bank_free[b] = m
                    pt_done.setdefault(u, []).append(m)
                d["pt"] = last
                if i == len(units[u][1]) - 1:
                    values(u)

            def values(u):
                head, qs, k0 = units[u]
                b = take(1)
                wq = P * len(qs)
                nk = max(w for _, w in qs) // P
                r0 = 64 * (head % 2)
                for t in range(nk):
                    first = next(i for i, (_, w) in enumerate(qs) if w > t * P) * P
                    m = mm(psum[r0:r0 + DH, b, first:wq], v_of(head, k0 // P + t), PT[:, u % 2, t, first:wq],
                           t == 0, t == nk - 1, pt_done[u], bank_free[b] if t == 0 else None, signal=t == nk - 1)
                pt_read[u % 2] = m
                bank_free[b] = put(head, psum[r0:r0 + DH, b, 0:wq], qs[0][0], qs[0][0] + wq, m)

            for n in range(-3, len(items)):
                if 0 <= n + 3 < len(items):
                    logits(n + 3)
                if 0 <= n + 2 < len(items):
                    exps(n + 2)
                if 0 <= n + 1 < len(items):
                    diag(n + 1)
                if n >= 0:
                    turn_p(n)

        mod_sem = [sem("mod_ring_0"), sem("mod_ring_1")]
        mod_cond = sem("mod_cond")
        ready_mod = {}

        def modulation(l, scope):
            CB = sb(scope, f"cond_all_partitions_{l}", [P, 2, D])
            junk = sb(scope, f"mod_scratch_{l}", [P, D])
            mod_ring = sb(scope, f"mod_ring_{l}", [P, 2, D])
            yield
            dma(pool, mod_cond, 32 * l + 16, CB[:, 0, :], dr["cond"][0:1, :].broadcast_to([P, D]))
            m = dma(pool, mod_cond, 32 * l + 32, CB[:, 1, :], dr["cond"][1:2, :].broadcast_to([P, D]))
            cond = None
            for v in range(2):
                m = fn(junk[:, :], CB[:, v, :], ACT.Exp, m, cond, scale=-1.0)
                m = v_ts(junk[:, :], junk[:, :], 1.0, None, ALU.add, None, m)
                m = recip(junk[:, :], junk[:, :], m)
                cond = v_tt(CB[:, v, :], CB[:, v, :], junk[:, :], ALU.mult, m)
            yield
            read = [None, None]
            m = cond
            for t in range(48):
                k = t % 2
                landed = dma(pool, mod_sem[k], 16 * (24 * l + t // 2 + 1),
                                  mod_ring[:, k, :], dr["w_mod"][l, t], read[k])
                for v in range(2 if l == 0 or t < 16 else 1):
                    m = dot(junk[:, :], mod_ring[:, k, :], CB[:, v, :], MOD[:, l, v, t:t + 1], landed, cond, m)
                read[k] = m
                yield
            b0 = VEC[f"bmod_{l}"][0]
            for v in range(2):
                n = 48 if l == 0 or v == 0 else 16
                m = v_tt(MOD[:, l, v, 0:n], MOD[:, l, v, 0:n], vecs[:, b0:b0 + n], ALU.add, m)
                for w in range(2):
                    if l == 1 and v == 1 and w == 1:
                        continue
                    n0 = VEC[f"n{w + 1}_{l}"][0]
                    sc = 24 * w + 8
                    m = v_stt(GS[:, l, w, v, :], MOD[:, l, v, sc:sc + 8], 1.0, vecs[:, n0:n0 + 8], ALU.add, ALU.mult, m)
            ready_mod[l] = m

        strips = ExitStack()
        bias_rows = sb(strips, "bias_rows", [P, STRIP])
        tab = {n: sb(strips, "c_" + n, [P, STRIP]) for n in ("bucket_of", "log_reach")}
        raw = sb(strips, "strip_raw", [P, 2, S])
        STR = nc.dram_tensor("bias_scratch", [A_HEADS + C_HEADS, STRIP], F32, kind="Internal").ap()
        SAVE = nc.dram_tensor("strip_scratch", [A_HEADS + C_HEADS, P, S], F32, kind="Internal").ap()
        fetch(tab["bucket_of"][:, :], dr["c_bucket_of"])
        t_in = fetch(tab["log_reach"][:, :], dr["c_log_reach"])
        NH = A_HEADS + C_HEADS
        b = take(2)
        m = mm(psum[0:NH, b, 0:512], small["rel_bias"][0:REL_BUCKETS, :], tab["bucket_of"][0:REL_BUCKETS, 0:512], True, True, t_in)
        m = mm(psum[0:NH, b + 1, 0:128], small["rel_bias"][0:REL_BUCKETS, :], tab["bucket_of"][0:REL_BUCKETS, 512:640], True, True, signal=True)
        m = v_tt(bias_rows[0:NH, :], bank(b, STRIP, 2)[0:NH, :], tab["log_reach"][0:NH, :], ALU.add, m, t_in)
        bank_free[b] = bank_free[b + 1] = m
        s_strip = sem("bias_strip")
        s_raw = [sem("strip_raw_0"), sem("strip_raw_1")]
        s_save = sem("strip_saved")
        m = dma(act, s_strip, 16, STR, bias_rows[0:NH, :], m)
        base = STR
        s_out = sb(strips, "strip_out", [P, 2, S])
        saved = [None, None]
        n_saved = 0
        s_save2 = [sem("strip_saved_0"), sem("strip_saved_1")]
        flipped = [None, None]
        for h in range(NH):
            k = h % 2
            src = bass.AP(tensor=base.tensor, offset=base.offset + h * STRIP, ap=[[1, P], [1, S]])
            got_raw = dma(act, s_raw[k], 16 * (h // 2 + 1), raw[:, k, :], src, m, flipped[k])
            b = take(1)
            fl = mm(bank(b), C["flip"][:, :], raw[:, k, :], True, True, got_raw, bank_free[b], signal=True)
            flipped[k] = fl
            cp = copy_on(dve, s_out[:, k, :], bank(b), fl, saved[k])
            bank_free[b] = cp
            saved[k] = dma(act, s_save2[k], 16 * (h // 2 + 1), SAVE[h], s_out[:, k, :], cp)
        strips_saved = list(saved)
        for lane in lanes:
            lane.wait(strips_saved)
        fence()
        strips.close()

        r = inv_rms(lambda t: X[:, t, :], KT, X1, D, None)
        h_ready = normed(lambda t: X[:, t, :], lambda t: H[:, t, :], KT, X1, lambda t, r: vec("norm1", t), r)

        block1 = ExitStack()
        V = sb(block1, "values", [P, S // P, D])
        B_ = sb(block1, "gla_in", [P, 5, S])
        qk = ExitStack()
        QK = sb(qk, "q_and_k", [P, 12, S])
        fence()
        proj = []

        def keep(dst):
            def f(ps, a, z, mark):
                m = copy(dst, ps, mark)
                proj.append(m)
                return m
            return f

        dsts = [QK[:, i, :] for i in range(6)] + [B_[:, i, :] for i in range(4)] + [QK[:, i, :] for i in range(6, 12)]
        for i, dst in enumerate(dsts):
            product([(dr["w_in1"][i], KT)], P, lambda k, a, z: H[:, k, a:z], h_ready, X1, keep(dst))
        product([(dr["w_ba"], KT)], B_RANK, lambda k, a, z: H[:, k, a:z], h_ready, X1, keep(B_[0:B_RANK, 4, :]))
        for half in range(2):
            bs = [take(1) for _ in range(4)]
            for s in range(4):
                slot, landed = load(dr["w_v1"][half, s])
                for j in range(2):
                    k = 2 * s + j
                    for t in range(4):
                        m = mm(bank(bs[t]), H[:, k, t * P:(t + 1) * P], ring[:, slot, j * 512:(j + 1) * 512], k == 0, k == KT - 1,
                               landed, bank_free[bs[t]] if k == 0 else None, signal=(j == 1 and t == 3))
                free_slot(slot, m)
            for t in range(4):
                c = copy(V[:, t, half * 512:(half + 1) * 512], bank(bs[t]), m)
                bank_free[bs[t]] = c
                proj.append(c)
        for lane in lanes:
            lane.wait(proj)
        fence()

        n_strip = [0]
        s_load = sem("strip_load")
        for g in range(2):
            with ExitStack() as scope:
                ST = sb(scope, f"strips_{g}", [P, 6, S])
                fence()
                act.wait([lane.now() for lane in lanes])
                m = dma(act, s_load, 16 * (g + 1), ST[:, :, :], SAVE[6 * g:6 * g + 6].rearrange("h p c -> p h c"))
                for lane in lanes:
                    lane.wait(m)
                o = 6 * g
                units = [(h, [(P * i, P * (i + 1)) for i in range(4)], 0) for h in range(6)]
                attention(scope, f"att{g}", units, DH ** -0.5,
                          lambda h, a, z: QK[64 * (h % 2):64 * (h % 2) + 64, o + h // 2, a:z],
                          lambda h, a, z: QK[64 * (h % 2):64 * (h % 2) + 64, o + 3 + h // 2, a:z],
                          lambda h, t: V[:, t, (640 if g else 0) + h * DH:(640 if g else 0) + (h + 1) * DH],
                          lambda h, q0, w: ST[:, h, 384 - q0:384 - q0 + w],
                          lambda h, ps, a, z, mark: copy(H[64 * (h % 2):64 * (h % 2) + 64, (5 if g else 0) + h // 2, a:z], ps, mark), S)
                fence()
        qk.close()

        with ExitStack() as scope:
            def buf(name, *shape):
                return sb(scope, "gla_" + name, [P, *shape])
            Bc, la, e1, qs, eb, kt = (buf(n, S) for n in ("b", "la", "e1", "qs", "eb", "kt"))
            Q, K_, G_ = B_[:, 0, :], B_[:, 1, :], B_[:, 4, :]
            VT = buf("vT", 2, S)
            ktok = buf("ktok", 4, P)
            vm = buf("vm", 2, 512)
            BX = buf("state_blocks", 2, DH, NCHUNK)
            dec = buf("dec", NCHUNK)
            ACC = buf("acc", 2, S)
            carried = ExitStack()
            UX, DX, SX = (sb(carried, "gla_" + n, [P, DH, NCHUNK]) for n in ("u", "dec_all", "state"))
            fence()

            def ch(x):
                return x.rearrange("p (n c) -> p n c", c=B_CHUNK)
            b = take(1)
            m = mm(bank(b), small["w_a2"][0:B_RANK, :], G_[0:B_RANK, :], True, True, bank_free[b], signal=True)
            z = v_ts(la[:, :], bank(b), vec("gla_b"), None, ALU.add, None, m)
            bank_free[b] = z
            m = fn(e1[:, :], la[:, :], ACT.Abs, z)
            m = fn(e1[:, :], e1[:, :], ACT.Exp, m, scale=-1.0)
            m = fn(e1[:, :], e1[:, :], ACT.Ln, m, bias=1.0)
            m = v_stt(la[:, :], la[:, :], 0.0, e1[:, :], ALU.min, ALU.subtract, m)
            m = v_ts(la[:, :], la[:, :], 1.0 / B_TAU, None, ALU.mult, None, m)
            b_ready = scan(Bc[:, :], C["not_first"][:, :], la[:, :], m)
            q_s = v_ts(qs[:, :], Q, B_DK ** -0.5, None, ALU.mult, None)
            last_b = ch(Bc[:, :])[:, :, B_CHUNK - 1:B_CHUNK].broadcast_to([P, NCHUNK, B_CHUNK])
            m = v_tt(ch(kt[:, :]), last_b, ch(Bc[:, :]), ALU.subtract, b_ready)
            m = fn(kt[:, :], kt[:, :], ACT.Exp, m)
            k_end = v_tt(kt[:, :], kt[:, :], K_, ALU.mult, m)
            m = fn(dec[:, :], ch(Bc[:, :])[:, :, B_CHUNK - 1], ACT.Exp, b_ready)
            z0 = v_ts(DX[:, :, :], dec[:, :].unsqueeze(1).broadcast_to([P, DH, NCHUNK]), 1.0, None, ALU.mult, None, m)
            z0 = zero(dve, DX[:, :, 0:1], z0)
            m = fn(eb[:, :], Bc[:, :], ACT.Exp, b_ready)
            q_in = v_tt(eb[:, :], eb[:, :], qs[:, :], ALU.mult, m, q_s)
            b = take(1)
            for t in range(4):
                m = turn(psum[:, b, t * P:(t + 1) * P], kt[:, t * P:(t + 1) * P], k_end, bank_free[b], signal=t == 3)
            k_tok = copy(ktok[:, :, :].rearrange("p t c -> p (t c)"), bank(b), m)
            bank_free[b] = k_tok
            vt = []
            for f in range(2):
                b = take(1)
                for t in range(4):
                    m = turn(
                        psum[:, b, t * P:(t + 1) * P], V[:, t, 384 + f * P:384 + (f + 1) * P], bank_free[b], signal=t == 3)
                vt.append(copy(VT[:, f, :], bank(b), m))
                bank_free[b] = vt[-1]
            mask = C["in_chunk"][:, :].unsqueeze(2).broadcast_to([P, P // B_CHUNK, DH])
            vm_read = [None, None]
            u_done = []
            i = 0
            for t in range(4):
                b = take(1)
                for h in range(B_HEADS):
                    src = V[:, t, 384 + h * DH:384 + (h + 1) * DH].unsqueeze(1).broadcast_to([P, P // B_CHUNK, DH])
                    m = v_tt(vm[:, i % 2, :].rearrange("p (n v) -> p n v", v=DH), src, mask, ALU.mult, vm_read[i % 2])
                    m = mm(psum[32 * h:32 * h + 32, b, :], ktok[:, t, 32 * h:32 * h + 32], vm[:, i % 2, :], True, True, m, k_tok,
                           bank_free[b] if h == 0 else None, signal=True)
                    vm_read[i % 2] = m
                    i += 1
                m = copy_on(act, UX[:, :, 8 * t:8 * t + 8].rearrange("p v n -> p n v"),
                                                            bank(b).rearrange("p (n v) -> p n v", v=DH), m)
                bank_free[b] = m
                u_done.append(m)
            m = scan(
                SX[:, :, :].rearrange("p v n -> p (v n)"), DX[:, :, :].rearrange("p v n -> p (v n)"),
                UX[:, :, :].rearrange("p v n -> p (v n)"), u_done, z0)
            z1 = zero(pool, BX[:, :, :, :])
            for h in range(B_HEADS):
                bx = copy_on(act, BX[32 * h:32 * h + 32, h % 2], SX[32 * h:32 * h + 32], m, z1)
            fence()
            carried.close()
            D1, D2, D3 = buf("d1", 2, S), buf("d2", 2, S), buf("d3", 2, S)
            E_, T_ = buf("mul", 2, S), None
            p_read = [None, None]
            e_read = [None, None]
            acc_done = None
            for s in range(B_CHUNK):
                j, w = s % 2, B_CHUNK - s
                n = NCHUNK * w

                def cut(x, w=w, n=n):
                    return x[:, 0:n].rearrange("p (c w) -> p c w", w=w)
                m = v_tt(cut(D1[:, j, :]), ch(Bc[:, :])[:, :, s:], ch(Bc[:, :])[:, :, 0:w], ALU.subtract, p_read[j], b_ready)
                m = fn(D1[:, j, 0:n], D1[:, j, 0:n], ACT.Exp, m)
                m2 = v_tt(cut(D2[:, j, :]), ch(qs[:, :])[:, :, s:], ch(K_)[:, :, 0:w], ALU.mult, q_s, p_read[j], lane=pool)
                ready = v_tt(D3[:, j, 0:n], D1[:, j, 0:n], D2[:, j, 0:n], ALU.mult, m, m2, p_read[j], lane=pool)
                for pr in range(2):
                    b = take(1)
                    m = mm(bank(b, n), C["spread"][64 * pr:64 * pr + 64, :], D3[64 * pr:64 * pr + 64, j, 0:n], True, True,
                           ready, bank_free[b], signal=True)
                    p_read[j] = [m, ready]
                    if s == 0:
                        a = v_tt(ACC[:, pr, :], bank(b), VT[:, pr, :], ALU.mult, m, vt)
                        bank_free[b] = a
                    else:
                        a = v_tt(cut(E_[:, pr, :]), bank(b, n).rearrange("p (c w) -> p c w", w=w), ch(VT[:, pr, :])[:, :, 0:w],
                                 ALU.mult, m, e_read[pr])
                        bank_free[b] = a
                        e_read[pr] = v_tt(ch(ACC[:, pr, :])[:, :, s:], ch(ACC[:, pr, :])[:, :, s:], cut(E_[:, pr, :]), ALU.add, a,
                                          acc_done)
                        acc_done = e_read[pr]
            for pr in range(2):
                b = take(1)
                for n in range(1, NCHUNK):
                    m = mm(psum[:, b, n * B_CHUNK:(n + 1) * B_CHUNK], BX[64 * pr:64 * pr + 64, :, :, n - 1],
                           eb[64 * pr:64 * pr + 64, n * B_CHUNK:(n + 1) * B_CHUNK], True, True, bx, q_in, bank_free[b],
                           signal=n == NCHUNK - 1)
                m = v_tt(ACC[:, pr, B_CHUNK:], psum[:, b, B_CHUNK:], ACC[:, pr, B_CHUNK:], ALU.add, m, acc_done)
                bank_free[b] = m
                sq = fn(e1[:, :], ACC[:, pr, :], ACT.Square, m, [dve.now(), pe.now()])
                b = take(1)
                m = mm(bank(b), C["mean64"][:, :], e1[:, :], True, True, sq, bank_free[b], signal=True)
                m = v_ts(la[:, :], bank(b), EPS, None, ALU.add, None, m)
                bank_free[b] = m
                m = fn(la[:, :], la[:, :], ACT.Sqrt, m)
                m = recip(la[:, :], la[:, :], m)
                m = v_stt(la[:, :], la[:, :], vec("gla_norm", pr), ACC[:, pr, :], ALU.mult, ALU.mult, m)
                rr = B_[:, 2 + pr, :]
                x = fn(e1[:, :], rr, ACT.Exp, m, pe.now(), scale=-1.0)
                x = v_ts(e1[:, :], e1[:, :], 1.0, None, ALU.add, None, x)
                x = recip(e1[:, :], e1[:, :], x)
                x = v_tt(e1[:, :], e1[:, :], rr, ALU.mult, x)
                m = v_tt(H[:, 3 + pr, 0:S], e1[:, :], la[:, :], ALU.mult, x, m)
            fence()
        block1.close()

        def add_x(m):
            return lambda ps, a, z, mark: v_tt(X[:, m, a:z], ps, X[:, m, a:z], ALU.add, mark)
        for m_ in range(KT):
            product([(dr["w_out1"][m_], KT)], P, lambda k, a, z: H[:, k, a:z], None, X1, add_x(m_))
        fence()
        r = inv_rms(lambda t: X[:, t, :], KT, X1, D, None)
        h_ready = normed(lambda t: X[:, t, :], lambda t: H[:, t, :], KT, X1, lambda t, r: vec("norm2", t), r)
        mlp(dr["w_ff1"], dr["w_ff2"], X1, h_ready, None, 0)
        r = inv_rms(lambda t: X[:, t, :], KT, X1, D, None)
        normed(lambda t: X[:, t, :], lambda t: X[:, t, :], KT, X1, lambda t, r: vec("final1", t), r)

        for l in range(2):
            last_layer = l == 1
            RG = X1 if last_layer else XB
            streams = [(0, S, "x")] if last_layer else [(0, S, "x"), (S, T2, "c")]
            fence()
            r = inv_rms(lambda t: X[:, t, :], KT, XB, D, None)
            h_ready = normed(lambda t: X[:, t, :], lambda t: H[:, t, :], KT, XB, lambda t, r: GS[:, l, 0, r, t:t + 1],
                             [r, ready_mod[l]], lambda t, r: MOD[:, l, r, t:t + 1])
            layer = ExitStack()
            LAT = sb(layer, f"latents_{l}", [P, 5, T2])
            KR = sb(layer, f"k_rope_{l}", [P, T2])
            tmp = sb(layer, f"rope_tmp_{l}", [P, 2, S])
            mixed = ExitStack()
            U = sb(mixed, f"conv_out_{l}", [P, 6, T2])
            early = ExitStack()
            FU = sb(early, f"fourier_in_{l}", [P, 2, T2])
            HU = sb(early, f"hyena_in_{l}", [P, 6, T2])
            fence()
            proj = []

            def keep2(dst):
                def f(ps, a, z, mark):
                    m = copy(dst[:, a:z], ps, mark)
                    proj.append(m)
                    return m
                return f

            def rotated(dst, ps, a, mark):
                m0 = v_tt(tmp[64:96, 0, :], ps[64:96], C["rope"][64:96, :], ALU.mult, mark, dve.now())
                m1 = v_tt(tmp[64:96, 1, :], ps[96:128], C["rope"][96:128, :], ALU.mult, mark, dve.now())
                m = v_tt(dst, tmp[64:96, 0, :], tmp[64:96, 1, :], ALU.add, m0, m1)
                return m, m1

            x_of = lambda k, a, z: H[:, k, a:z]
            for i in range(3):
                product([(dr["w_in2"][l, i], KT)], P, x_of, h_ready, RG, keep2(LAT[:, i, :]))
            for i in range(3, 5):
                product([(dr["w_in2"][l, i], KT)], P, x_of, h_ready, XB, keep2(LAT[:, i, :]))
            for i in range(2):
                product([(dr["w_in2"][l, 5 + i], KT)], P, x_of, h_ready, RG, keep2(FU[:, i, :]))
            for i in range(6):
                product([(dr["w_in2"][l, 7 + i], KT)], P, x_of, h_ready, RG, keep2(HU[:, i, :]))

            def kr_out(ps, a, z, mark):
                if a == 0:
                    full = psum[:, kr_bank[0], 0:S]
                    m, m1 = rotated(KR[64:96, a:z], full, a, mark)
                    proj.append(m)
                    return m
                m = copy(KR[64:96, a:z], ps[0:32], mark)
                proj.append(m)
                return m
            kr_bank = [2 * (next_bank[2] % 4)]
            product([(dr["w_kr"][l], KT)], 64, x_of, h_ready, XB, kr_out, rows=64)
            for lane in lanes:
                lane.wait(proj)
            fence()

            with ExitStack() as scope:
                A_ = sb(scope, f"fourier_mid_{l}", [P, 4, 512])
                for lo, hi, nm in streams:
                    nt = (hi - lo) // P
                    a_done = []
                    fence()
                    for t in range(nt):
                        b = take(1)
                        for f in range(2):
                            m = mm(psum[:, b, f * 256:(f + 1) * 256], FU[:, f, lo + t * P:lo + (t + 1) * P], C["dft64"][:, :],
                                   True, True, bank_free[b] if f == 0 else None, signal=f == 1)
                        m = copy(A_[:, t, :], bank(b), m)
                        bank_free[b] = m
                        a_done.append(m)
                    b = take(2)
                    i0, n_rows, wid = plan["fourier_" + nm]
                    L = hi - lo
                    for t in range(nt):
                        slot, landed = load(dr["tables"][i0 + t][:, 0:wid], wid)
                        for f in range(2):
                            for cs in range(2):
                                m = mm(psum[:, b + f, 0:L], A_[:, t, f * 256 + cs * P:f * 256 + (cs + 1) * P],
                                       ring[:, slot, cs * L:(cs + 1) * L], t == 0 and cs == 0, t == nt - 1 and cs == 1,
                                       landed, a_done[t], bank_free[b + f] if t == 0 and cs == 0 else None, signal=f == 1 and cs == 1)
                        free_slot(slot, m)
                    for f in range(2):
                        m2 = copy(H[:, 4 + f, lo:hi], psum[:, b + f, 0:L], m)
                        bank_free[b + f] = m2
                fence()

            with ExitStack() as scope:
                cw, cb = VEC[f"cw_{l}"][0], VEC[f"cb_{l}"][0]
                fence()
                hi_all = streams[-1][1]
                for i in range(6):
                    m = fn(U[:, i, 0:hi_all], HU[:, i, 0:hi_all], ACT.Identity, bias=vecs[:, cb + i:cb + i + 1],
                           scale=vecs[:, cw + 6 + i:cw + 7 + i])
                    for lo, hi, nm in streams:
                        m = v_stt(U[:, i, lo + 1:hi], HU[:, i, lo:hi - 1], vecs[:, cw + i:cw + i + 1], U[:, i, lo + 1:hi], ALU.mult, ALU.add, m)
                        m = v_stt(U[:, i, lo:hi - 1], HU[:, i, lo + 1:hi], vecs[:, cw + 12 + i:cw + 13 + i], U[:, i, lo:hi - 1], ALU.mult, ALU.add, m)
                for i in range(2):
                    zm = v_tt(U[:, 2 + i, 0:hi_all], U[:, 2 + i, 0:hi_all], U[:, 4 + i, 0:hi_all], ALU.mult, m)
                Z = lambda i: U[:, 2 + i, :]
                fence()
                early.close()
                for lo, hi, nm in streams:
                    with ExitStack() as one:
                        L = hi - lo
                        nt = L // P
                        h1 = sb(one, f"filt_h1_{l}{nm}", [P, S])
                        h2 = sb(one, f"filt_h2_{l}{nm}", [P, S])
                        rn = sb(one, f"filt_rn_{l}{nm}", [P, S])
                        HF = sb(one, f"filt_hf_{l}{nm}", [P, nt, 512])
                        HA = sb(one, f"filt_abs_{l}{nm}", [P, nt, 512])
                        ZU = sb(one, f"spec_in_cos_{l}{nm}", [P, nt, 512])
                        ZW = sb(one, f"spec_in_sin_{l}{nm}", [P, nt, 512])
                        RE = sb(one, f"spec_re_{l}{nm}", [P, 2, 512])
                        IM = sb(one, f"spec_im_{l}{nm}", [P, 2, 512])
                        Y = sb(one, f"spec_prod_{l}{nm}", [P, nt, 2, 256])
                        T0 = sb(one, f"spec_tmp_{l}{nm}", [P, 2, 256])
                        nrm = sb(one, f"filt_norm_{l}{nm}", [P, 2])
                        fence()

                        def sine(dst, ps, mark, bias_name):
                            d = dst[0:64, 0:L]
                            n_ = rn[0:64, 0:L]
                            a0 = v_ts(d, ps, vec(bias_name, 0, 64), vec(f"ffr_{l}", 0, 64), ALU.add, ALU.mult, mark)
                            magic = 1.5 * 2 ** 23
                            m = v_ts(n_, d, 1.0 / (2 * math.pi), magic, ALU.mult, ALU.add, a0)
                            m = v_ts(n_, n_, magic, None, ALU.subtract, None, m)
                            c1 = 6.28125
                            c2 = float(np.float32(np.round((2 * math.pi - c1) * 2 ** 22) / 2 ** 22))
                            c3 = 2 * math.pi - c1 - c2
                            for c in (c1, c2, c3):
                                m = v_stt(d, n_, -c, d, ALU.mult, ALU.add, m)
                            m = v_ts(d, d, 3.1415925, -3.1415925, ALU.min, ALU.max, m)
                            return a0, fn(d, d, ACT.Sin, m)

                        i0 = plan["emb_" + nm][0]
                        slot, landed = load(dr["tables"][i0][:, 0:L], L)
                        b = take(1)
                        m = mm(psum[0:64, b, 0:L], small["fw1"][0:33, 64 * l:64 * l + 64], ring[0:33, slot, 0:L], True, True,
                               landed, bank_free[b], signal=True)
                        free_slot(slot, m)
                        bank_free[b], m = sine(h1, psum[0:64, b, 0:L], m, f"fb1_{l}")
                        b = take(1)
                        m = mm(psum[0:64, b, 0:L], small["fw2"][0:64, 64 * l:64 * l + 64], h1[0:64, 0:L], True, True, m, bank_free[b], signal=True)
                        bank_free[b], h2_ready = sine(h2, psum[0:64, b, 0:L], m, f"fb2_{l}")
                        i0, n_rows, wid = plan["decay_" + nm]
                        hf = []
                        for t in range(nt):
                            if t % 2 == 0:
                                slot, landed = load(dr["tables"][i0 + t // 2])
                            b = take(1)
                            m = mm(bank(b), h2[0:64, t * P:(t + 1) * P], small["fw3"][0:64, 512 * l:512 * l + 512], True, True,
                                   h2_ready, bank_free[b], signal=True)
                            m = v_tt(HF[:, t, :], bank(b), ring[:, slot, (t % 2) * 512:(t % 2) * 512 + 512], ALU.mult, m, landed)
                            bank_free[b] = m
                            if t % 2:
                                free_slot(slot, m)
                            ab = fn(HA[:, t, :], HF[:, t, :], ACT.Abs, m)
                            u1 = v_tt(ZU[:, t, 256:512], HF[:, t, 0:256], HF[:, t, 256:512], ALU.add, m)
                            u2 = v_tt(ZW[:, t, 256:512], HF[:, t, 0:256], HF[:, t, 256:512], ALU.subtract, m, lane=pool)
                            hf.append([ab, u1, u2])
                        b = take(1)
                        for ct in range(2):
                            i = 0
                            for t in range(nt):
                                for side_ in range(2):
                                    m = mm(psum[:, b, ct:ct + 1], HA[:, t, side_ * 256 + ct * P:side_ * 256 + (ct + 1) * P], C["ones"][:, 0:1],
                                           i == 0, i == 2 * nt - 1, hf, bank_free[b], signal=i == 2 * nt - 1)
                                    i += 1
                        nm_ready = recip(nrm[:, :], psum[:, b, 0:2], m)
                        bank_free[b] = nm_ready
                        zt = []
                        for t in range(nt):
                            b = take(1)
                            for ct in range(2):
                                m = turn(
                                    psum[:, b, ct * P:(ct + 1) * P], Z(ct)[:, lo + t * P:lo + (t + 1) * P], zm, bank_free[b], signal=ct == 1)
                            m1 = copy_on(act, ZU[:, t, 0:256], psum[:, b, 0:256], m)
                            m2 = copy_on(dve, ZW[:, t, 0:256], psum[:, b, 0:256], m, m1)
                            bank_free[b] = m2
                            zt.append([m1, m2])
                        i0, n_rows, wid = plan["fwd_" + nm]
                        y_done = [None] * nt
                        for f in range(nt):
                            j = f % 2
                            slot, landed = load(dr["tables"][i0 + f][:, 0:wid], wid)
                            b = take(2)
                            for cs, src in enumerate((ZU, ZW)):
                                for t in range(nt):
                                    m = mm(bank(b + cs), ring[:, slot, cs * nt * P + t * P:cs * nt * P + (t + 1) * P], src[:, t, :],
                                           t == 0, t == nt - 1, landed, zt, hf, bank_free[b + cs] if t == 0 else None, signal=t == nt - 1)
                            free_slot(slot, m)
                            free = y_done[f - 2] if f >= 2 else None
                            re = copy_on(act, RE[:, j, :], bank(b), m, free)
                            im = copy_on(act, IM[:, j, :], bank(b + 1), m, free)
                            bank_free[b], bank_free[b + 1] = re, im
                            zr, kr, zi, ki = RE[:, j, 0:256], RE[:, j, 256:512], IM[:, j, 0:256], IM[:, j, 256:512]
                            p1 = v_tt(Y[:, f, 0, :], zr, kr, ALU.mult, im)
                            p2 = v_tt(T0[:, 0, :], zi, ki, ALU.mult, im, y_done[f - 1] if f else None)
                            p3 = v_tt(Y[:, f, 0, :], Y[:, f, 0, :], T0[:, 0, :], ALU.subtract, p1, p2)
                            q1 = v_tt(Y[:, f, 1, :], zr, ki, ALU.mult, im, lane=pool)
                            q2 = v_tt(T0[:, 1, :], zi, kr, ALU.mult, im, y_done[f - 1] if f else None, lane=pool)
                            q3 = v_tt(Y[:, f, 1, :], Y[:, f, 1, :], T0[:, 1, :], ALU.add, q1, q2, lane=pool)
                            y_done[f] = [p3, q3]
                        i0, n_rows, wid = plan["inv_" + nm]
                        b = take(2)
                        for f in range(nt):
                            slot, landed = load(dr["tables"][i0 + f][:, 0:wid], wid)
                            for ct in range(2):
                                for cs in range(2):
                                    m = mm(psum[:, b + ct, 0:L], Y[:, f, cs, ct * P:(ct + 1) * P], ring[:, slot, cs * L:(cs + 1) * L],
                                           f == 0 and cs == 0, f == nt - 1 and cs == 1, landed, y_done[f],
                                           bank_free[b + ct] if f == 0 and cs == 0 else None, signal=ct == 1 and cs == 1)
                            free_slot(slot, m)
                        for ct in range(2):
                            dz = v_ts(Z(ct)[:, lo:hi], Z(ct)[:, lo:hi], vec(f"hd_{l}", ct), None, ALU.mult, None, m)
                            y = v_stt(Z(ct)[:, lo:hi], psum[:, b + ct, 0:L], nrm[:, ct:ct + 1], Z(ct)[:, lo:hi], ALU.mult, ALU.add, dz, nm_ready)
                            bank_free[b + ct] = y
                            v_tt(H[:, 6 + ct, lo:hi], U[:, ct, lo:hi], Z(ct)[:, lo:hi], ALU.mult, y)
                        fence()
                fence()
            mixed.close()

            with ExitStack() as scope:
                VH = sb(scope, f"v_heads_{l}", [P, T2 // P, MH * DH])
                fence()
                r = inv_rms(lambda t: LAT[:, t, :], 3, RG, QL, None)
                q_ready = normed(lambda t: LAT[:, t, :], lambda t: LAT[:, t, :], 3, RG, lambda t, r: vec(f"qn_{l}", t), r)
                r = inv_rms(lambda t: LAT[:, 3 + t, :], 2, XB, KVL, None)
                kv_ready = normed(lambda t: LAT[:, 3 + t, :], lambda t: LAT[:, 3 + t, :], 2, XB, lambda t, r: vec(f"kvn_{l}", t), r)
                v_made = []
                slot, landed = load(dr["w_uv"][l])
                for t in range(T2 // P):
                    b = take(1)
                    for k in range(2):
                        m = mm(bank(b), LAT[:, 3 + k, t * P:(t + 1) * P], ring[:, slot, k * 512:(k + 1) * 512], k == 0, k == 1,
                               landed, kv_ready[k], bank_free[b] if k == 0 else None, signal=k == 1)
                    m6 = copy(VH[:, t, :], bank(b), m)
                    bank_free[b] = m6
                    v_made.append(m6)
                free_slot(slot, m)
                for g in range(2):
                    half = ExitStack()
                    QH = sb(half, f"q_heads_{l}_{g}", [P, 4, T2])
                    KH = sb(half, f"k_heads_{l}_{g}", [P, 4, T2])
                    fence()
                    rope_k = copy_on(pool, KH[64:96, :, :], KR[64:96, :].unsqueeze(1).broadcast_to([32, 4, T2]))
                    made = [rope_k, v_made]
                    for h in range(4):
                        b = take(len(RG))
                        if h % 2 == 0:
                            slot, landed = load(dr["w_uq"][l, 2 * g + h // 2], 2 * 3 * P)
                        for k in range(3):
                            for r_, (lo, hi) in enumerate(RG):
                                m = mm(psum[:, b + r_, 0:hi - lo], ring[:, slot, ((h % 2) * 3 + k) * P:((h % 2) * 3 + k + 1) * P], LAT[:, k, lo:hi],
                                       k == 0, k == 2, landed, q_ready[k], bank_free[b + r_] if k == 0 else None,
                                       signal=k == 2 and r_ == len(RG) - 1)
                        if h % 2:
                            free_slot(slot, m)
                        m1, m2 = rotated(QH[64:96, h, 0:S], psum[:, b, 0:S], 0, m)
                        m3 = copy_on(act, QH[0:64, h, 0:S], psum[0:64, b, 0:S], m, m2)
                        bank_free[b] = m3
                        made += [m1, m3]
                        if not last_layer:
                            m4 = copy(QH[0:96, h, S:T2], psum[0:96, b + 1, 0:SC], m)
                            bank_free[b + 1] = m4
                            made.append(m4)
                    slot, landed = load(dr["w_uk"][l, :, 512 * g:512 * g + 512], 512)
                    for mt in range(2):
                        b = take(2)
                        for k in range(2):
                            for r_, (lo, hi) in enumerate(XB):
                                m = mm(psum[:, b + r_, 0:hi - lo], ring[:, slot, (mt * 2 + k) * P:(mt * 2 + k + 1) * P], LAT[:, 3 + k, lo:hi],
                                       k == 0, k == 1, landed, kv_ready[k], bank_free[b + r_] if k == 0 else None, signal=k == 1 and r_ == 1)
                        for j in range(2):
                            m5 = copy_on((dve, act)[j], 
                                KH[0:64, 2 * mt + j, :], bank(b, T2, 2)[64 * j:64 * j + 64, :], m, m5 if j else None)
                            made.append(m5)
                        bank_free[b] = bank_free[b + 1] = made[-2:]
                    free_slot(slot, m)
                    for lane in lanes:
                        lane.wait(made)
                    units = []
                    for h in range(4):
                        units.append((h, [(P * i, T2) for i in range(4)], 0))
                        if not last_layer:
                            units.append((h, [(S + P * i, SC) for i in range(2)], S))
                    attention(half, f"mla{l}_{g}", units, 1.0 / math.sqrt(NOPE + ROPE),
                              lambda h, a, z: QH[0:96, h, a:z], lambda h, a, z: KH[0:96, h, a:z],
                              lambda h, t: VH[:, t, (4 * g + h) * DH:(4 * g + h + 1) * DH], None,
                              lambda h, ps, a, z, mark: copy(H[64 * (h % 2):64 * (h % 2) + 64, 2 * g + h // 2, a:z], ps, mark), T2)
                    fence()
                    half.close()
            layer.close()

            def gate(comp):
                return lambda m, a: MOD[:, l, 0 if a == 0 else 1, comp * 8 + m:comp * 8 + m + 1]
            for m_ in range(KT):
                product([(dr["w_out2"][l, m_], KT)], P, x_of, None, RG,
                        lambda ps, a, z, mark, m_=m_: v_stt(X[:, m_, a:z], ps, gate(2)(m_, a), X[:, m_, a:z], ALU.mult, ALU.add, mark))
            fence()
            r = inv_rms(lambda t: X[:, t, :], KT, RG, D, None)
            h_ready = normed(lambda t: X[:, t, :], lambda t: H[:, t, :], KT, RG, lambda t, r: GS[:, l, 1, r, t:t + 1], r,
                             lambda t, r: MOD[:, l, r, 24 + t:25 + t])
            mlp(dr["w_mlp1"][l], dr["w_mlp2"][l], RG, h_ready, gate(5), None if last_layer else 1)

        r = inv_rms(lambda t: X[:, t, :], KT, X1, D, None)
        done = normed(lambda t: X[:, t, :], lambda t: H[:, t, :], KT, X1, lambda t, r: vec("final2", t), r)
        stored = sem("stored")
        for t in range(KT):
            m = dma(sp, stored, 16 * (t + 1), out_t[:, t, :], H[:, t, 0:S], done[t])
        sp.wait(m)

        with nc.Block() as block:
            @block.tensor
            def _(eng):
                pe.run(eng)

            @block.vector
            def _(eng):
                dve.run(eng)

            @block.scalar
            def _(eng):
                act.run(eng)

            @block.gpsimd
            def _(eng):
                pool.run(eng)

            @block.sync
            def _(eng):
                sp.run(eng)


def tiles(w, cols):
    return slots_of(w[:, cols])


def lay_out(a):
    d = {}
    fm = lambda v: np.ascontiguousarray(v.reshape(-1, P).T)
    cols = lambda m: [slice(i * P, (i + 1) * P) for i in range(m)]
    d["x_t"] = np.ascontiguousarray(a["x"][0].T.reshape(KT, P, S).transpose(1, 0, 2))
    d["ctx_t"] = np.ascontiguousarray(a["ctx_2"][0].T.reshape(KT, P, SC).transpose(1, 0, 2))
    w = a["w_in"][0]
    AQ, AK, AV, BQ, BK, BV, BR, BA, CQ, CK, CV, _ = np.cumsum([0, 384, 384, 384, 128, 128, 256, 256, 16, 384, 384, 384])
    starts = [AQ + P * i for i in range(3)] + [AK + P * i for i in range(3)] + [BQ, BK, BR, BR + P]
    starts += [CQ + P * i for i in range(3)] + [CK + P * i for i in range(3)]
    d["w_in1"] = np.stack([tiles(w, slice(s, s + P)) for s in starts])
    d["w_ba"] = tiles(w, slice(BA, BA + B_RANK))
    wv = np.concatenate([w[:, AV:AV + 384], w[:, BV:BV + 256], w[:, CV:CV + 384]], 1)
    d["w_v1"] = np.ascontiguousarray(wv.reshape(4, 2, P, 2, 512).transpose(3, 0, 2, 1, 4).reshape(2, 4, P, 1024))
    d["w_out1"] = np.stack([tiles(a["w_out"][0], c) for c in cols(KT)])

    def ff2(w):
        return np.ascontiguousarray(w.reshape(2, 2, KT, P, KT, P).transpose(0, 4, 1, 3, 2, 5).reshape(2, KT, 2, P, KT * P))
    d["w_ff1"] = np.stack([tiles(a["w_ff1"][0], c) for c in cols(FT)])
    d["w_ff2"] = ff2(a["w_ff2"][0])
    j = np.arange(ROPE)
    swap = np.where(j % 16 < 8, j + 8, j - 8)
    w2 = a["w_in_2"]
    off_kr, off_f = QL + KVL, QL + KVL + ROPE
    st = [P * i for i in range(5)] + [off_f + P * i for i in range(8)]
    d["w_in2"] = np.stack([np.stack([tiles(w2[l], slice(s, s + P)) for s in st]) for l in range(2)])
    d["w_kr"] = np.stack([tiles(w2[l], np.concatenate([off_kr + j, off_kr + swap])) for l in range(2)])
    uq = a["w_uq_2"]
    head = lambda h: np.concatenate([96 * h + np.arange(64), 96 * h + 64 + j, 96 * h + 64 + swap])
    d["w_uq"] = np.stack([np.stack([np.concatenate([tiles(uq[l], head(2 * p)), tiles(uq[l], head(2 * p + 1))], 1)
                                    for p in range(4)]) for l in range(2)])
    ukv = a["w_ukv_2"]
    nope = lambda p: np.concatenate([128 * (2 * p + i) + np.arange(64) for i in range(2)])
    vals = np.concatenate([128 * h + 64 + np.arange(64) for h in range(MH)])
    d["w_uk"] = np.stack([np.concatenate([tiles(ukv[l], nope(p)) for p in range(4)], 1) for l in range(2)])
    d["w_uv"] = np.stack([tiles(ukv[l], vals) for l in range(2)])
    d["w_out2"] = np.stack([np.stack([tiles(a["w_out_2"][l], c) for c in cols(KT)]) for l in range(2)])
    d["w_mlp1"] = np.stack([np.stack([tiles(a["w_mlp1_2"][l], c) for c in cols(FT)]) for l in range(2)])
    d["w_mlp2"] = np.stack([ff2(a["w_mlp2_2"][l]) for l in range(2)])
    d["w_mod"] = np.ascontiguousarray(a["w_mod_2"].transpose(0, 2, 1).reshape(2, 48, P, D))
    d["cond"] = np.stack([a["c_2"][0], a["c_ctx_2"]])
    d["w_a2"] = np.ascontiguousarray(a["gla_w_a2"][0])
    d["rel_bias"] = np.ascontiguousarray(a["rel_bias"])
    d["fw1"] = np.ascontiguousarray(np.concatenate([a["hy_w1_2"][l] for l in range(2)], 1))
    d["fw2"] = np.ascontiguousarray(np.concatenate([a["hy_w2_2"][l] for l in range(2)], 1))
    d["fw3"] = np.ascontiguousarray(np.concatenate([a["hy_w3_2"][l] for l in range(2)], 1))
    v = np.zeros((P, VECS), np.float32)

    def put(name, x):
        at, n = VEC[name]
        v[0:x.shape[0], at:at + n] = x
    put("norm1", fm(a["norm1_w"][0])); put("norm2", fm(a["norm2_w"][0])); put("final1", fm(a["final_norm_w"]))
    put("gla_norm", fm(a["gla_norm_w"][0])); put("gla_b", fm(a["gla_b_a"][0])); put("final2", fm(a["final_norm_g_2"]))
    for l in range(2):
        put(f"n1_{l}", fm(a["norm1_g_2"][l])); put(f"n2_{l}", fm(a["norm2_g_2"][l]))
        put(f"qn_{l}", fm(a["q_norm_g_2"][l])); put(f"kvn_{l}", fm(a["kv_norm_g_2"][l]))
        put(f"bmod_{l}", fm(a["b_mod_2"][l])); put(f"cw_{l}", fm(a["hy_conv_w_2"][l].reshape(-1)))
        put(f"cb_{l}", fm(a["hy_conv_b_2"][l])); put(f"hd_{l}", fm(a["hy_d_2"][l]))
        put(f"fb1_{l}", a["hy_b1_2"][l][:, None]); put(f"ffr_{l}", a["hy_freq_2"][l][:, None])
        put(f"fb2_{l}", a["hy_b2_2"][l][:, None])
    d["vecs"] = v
    for n, t in shape_constants().items():
        d["c_" + n] = t
    d["tables"], at = sequence_tables()
    return d, at


def kernel(**inputs):
    import concourse.bacc as bacc
    from concourse.bass_utils import run_bass_kernel_spmd as run

    arrays, at = lay_out({k: np.asarray(v) for k, v in inputs.items()})
    nc = bacc.Bacc("TRN2", target_bir_lowering=False, num_devices=1)
    dr = {n: nc.dram_tensor("in_" + n, a.shape, F32, kind="ExternalInput").ap() for n, a in arrays.items()}
    out_t = nc.dram_tensor("out_t", (P, KT, S), F32, kind="ExternalOutput").ap()
    build(nc, dr, out_t, at)
    r = run(nc, [{"in_" + n: np.ascontiguousarray(a) for n, a in arrays.items()}], core_ids=[0])
    o = np.asarray(r.results[0]["out_t"])
    return np.ascontiguousarray(o.transpose(1, 0, 2).reshape(D, S).T)[None]
```

```python
import math
from contextlib import ExitStack

import numpy as np

import concourse.bass as bass
from concourse import mybir

F32 = mybir.dt.float32
F32R = mybir.dt.float32r
ALU = mybir.AluOpType
ACT = mybir.ActivationFunctionType
AX = mybir.AxisListType

P = 128
D = 1024
KT = D // P
S = 512
SC = 256
T2 = S + SC
DH = 64
EPS = 1e-6
A_HEADS = B_HEADS_ = 6
B_HEADS, B_DK, B_DV, B_RANK, B_CHUNK, B_TAU = 4, 32, 64, 16, 16, 16.0
C_HEADS = 6
NCHUNK = S // B_CHUNK
REL_BUCKETS, REL_MAX = 32, 2048
F = 4 * D
FT = F // P
MH = 8
NOPE, ROPE = 64, 32
QL, KVL = 384, 256
HY = 256
SLOT = 1024
RING = 5
SPLIT_RING = 4
AHEAD = 2
GROUP = 4
NGROUP = 32 // GROUP
NEG = -1e30
STRIP = 640


def rel_bucket(n):
    n = np.maximum(n, 0)
    exact = REL_BUCKETS // 2
    logv = (np.log(np.maximum(n, 1).astype(np.float32) / exact) / np.float32(math.log(REL_MAX / exact)))
    large = np.minimum(exact + (logv * (REL_BUCKETS - exact)).astype(np.int32), REL_BUCKETS - 1)
    return np.where(n < exact, n, large)


def shape_constants():
    f64 = np.float64
    c = {}
    c["ident"] = np.eye(P)
    c["flip"] = np.eye(P)[::-1]
    c["ones"] = np.ones((P, P))
    two = (np.arange(P)[:, None] // 32 % 2) == (np.arange(P)[None, :] // 64)
    c["spread"] = two.astype(f64)
    c["mean64"] = (np.arange(P)[:, None] // 64 == np.arange(P)[None, :] // 64) / 64.0
    c["in_chunk"] = (np.arange(P)[:, None] // B_CHUNK == np.arange(P // B_CHUNK)[None, :]).astype(f64)
    c["not_first"] = np.tile((np.arange(S) % B_CHUNK != 0).astype(f64), (P, 1))
    dist = S - 1 - np.arange(STRIP)
    c["bucket_of"] = np.zeros((P, STRIP))
    c["bucket_of"][:REL_BUCKETS] = np.arange(REL_BUCKETS)[:, None] == rel_bucket(dist)[None, :]
    times = (dist <= 128) * 1.0 + (dist % 4 == 0) + (dist % 16 == 0)
    log_a = np.where((dist >= 0) & (times > 0), np.log(np.maximum(times, 1)), NEG)
    c["log_reach"] = np.zeros((P, STRIP))
    c["log_reach"][:A_HEADS] = log_a
    c["log_reach"][A_HEADS:A_HEADS + C_HEADS] = np.where(dist >= 0, 0.0, NEG)
    inv = (np.float32(10000.0) ** (-np.arange(0, 16, 2, dtype=np.float32) / 16)).astype(np.float32)
    tok = np.arange(S)
    ang = np.concatenate([(tok // 64).astype(np.float32)[:, None] * inv, (tok % 64).astype(np.float32)[:, None] * inv], 1)
    j = np.arange(ROPE)
    which = j // 16 * 8 + j % 8
    c["rope"] = np.zeros((P, S))
    c["rope"][64:96] = np.cos(ang)[:, which].T
    c["rope"][96:128] = (np.sin(ang)[:, which] * np.where(j % 16 < 8, -1.0, 1.0)).T
    g = np.arange(P)
    same = g[:, None] // 64 == g[None, :] // 64
    a = 2 * np.pi * ((g[:, None] % 64) * (g[None, :] % 64) % 64) / 64
    c["dft64"] = np.concatenate([np.cos(a) * same, np.sin(a) * same], 1)
    return {k: v.astype(np.float32) for k, v in c.items()}


CONSTS = ["ident", "flip", "ones", "spread", "mean64", "in_chunk", "not_first", "bucket_of", "log_reach", "rope", "dft64"]
CONST_W = {"ident": P, "flip": P, "ones": P, "spread": P, "mean64": P, "in_chunk": P // B_CHUNK, "not_first": S,
           "bucket_of": STRIP, "log_reach": STRIP, "rope": S, "dft64": 2 * P}


def slots_of(table):
    k, m = table.shape
    return np.ascontiguousarray(table.reshape(k // P, P, m).transpose(1, 0, 2).reshape(P, -1))


def sequence_tables():
    out = {}
    for L, name in ((S, "x"), (SC, "c")):
        t = np.arange(L)
        a = 2 * np.pi * (t[:, None] * t[None, :] % L) / L
        n = 1.0 / math.sqrt(L * 64)
        rows = [np.concatenate([np.cos(a[i:i + P]) * n, -np.sin(a[i:i + P]) * n], 1) for i in range(0, L, P)]
        out["fourier_" + name] = rows
        w = np.pi * (t[:, None] * (2 * t[None, :] + 1) % (4 * L)) / (2 * L) * 1.0
        w = 2 * np.pi * (t[:, None] * (2 * t[None, :] + 1) % (4 * L)) / (4 * L)
        out["fwd_" + name] = [np.concatenate([slots_of(np.cos(w[:, i:i + P])), slots_of(-np.sin(w[:, i:i + P]))], 1)
                              for i in range(0, L, P)]
        out["inv_" + name] = [np.concatenate([np.cos(w.T[i:i + P]) / L, -np.sin(w.T[i:i + P]) / L], 1)
                              for i in range(0, L, P)]
        pos = np.linspace(0.0, 1.0, L, dtype=np.float32)[:, None]
        fr = np.linspace(1e-4, 15, 16, dtype=np.float32)
        ang = (np.float32(2.0 * math.pi) * t.astype(np.float32)[:, None] / np.float32(L) * fr).astype(np.float32)
        z = np.concatenate([pos, np.cos(ang), -np.sin(ang)], 1)
        lo, hi = math.log(1e-2) / 1.5, math.log(1e-2) / 0.3
        deltas = np.abs(np.linspace(lo, hi, HY, dtype=np.float32))
        decay = np.exp(-pos * deltas)
        decay = np.concatenate([decay, decay], 1)
        decay[0, HY:] = 0.0
        decay = slots_of(decay)
        zt = np.zeros((P, L))
        zt[:33] = z.T
        out["emb_" + name] = [zt]
        out["decay_" + name] = [decay[:, i:i + SLOT] for i in range(0, decay.shape[1], SLOT)]
    flat, at = [], {}
    for k, rows in out.items():
        at[k] = (len(flat), len(rows), rows[0].shape[1])
        for r in rows:
            full = np.zeros((P, SLOT), np.float32)
            full[:, :r.shape[1]] = r
            flat.append(full)
    return np.stack(flat), at


def vec_plan():
    plan, at = {}, 0
    for name, n in [("norm1", 8), ("norm2", 8), ("final1", 8), ("gla_norm", 2), ("gla_b", 1), ("final2", 8)] + [
            (f"{name}{l}", n) for l in range(2) for name, n in (
                ("n1_", 8), ("n2_", 8), ("qn_", 3), ("kvn_", 2), ("bmod_", 48), ("cw_", 18), ("cb_", 6), ("hd_", 2),
                ("fb1_", 1), ("ffr_", 1), ("fb2_", 1))]:
        plan[name] = (at, n)
        at += n
    return plan, at


VEC, VECS = vec_plan()


class Lane:

    def __init__(self, sem):
        self.sem, self.count, self.queue, self.seen = sem, 0, [], {}

    def wait(self, *after):
        for mark in marks(after):
            sem, value = mark
            if self.seen.get(id(sem), 0) < value:
                self.seen[id(sem)] = value
                self.queue.append(lambda eng, sem=sem, value=value: eng.wait_ge(sem, value))

    def issue(self, instruction, *after, signal=True):
        self.wait(*after)
        if signal:
            self.count += 1
            self.queue.append(lambda eng: instruction(eng).then_inc(self.sem, 1))
        else:
            self.queue.append(instruction)
        return (self.sem, self.count)

    def dma(self, sem, total, instruction, *after):
        self.wait(*after)
        self.queue.append(lambda eng: instruction(eng).then_inc(sem, 16))
        return (sem, total)

    def now(self):
        return (self.sem, self.count) if self.count else None

    def run(self, eng):
        for instruction in self.queue:
            instruction(eng)


def marks(x):
    if x is None:
        return
    if isinstance(x, tuple) and len(x) == 2 and isinstance(x[1], int):
        yield x
        return
    for y in x:
        yield from marks(y)


def build(nc, dr, out_t, at, order):
    plan = at
    with ExitStack() as top:
        def sem(name):
            return top.enter_context(nc.semaphore(name))

        pe, dve, act, pool, sp = (Lane(sem(n)) for n in ("pe_step", "dve_step", "act_step", "pool_step", "sp_step"))
        lanes = [pe, dve, act, pool]

        holes = [[nc.sbuf_base + 31 & ~31, nc.sbuf_usable_end & ~31, []]]

        def sb(scope, name, shape, dtype=F32, high=False):
            size = 4 * int(np.prod(shape[1:])) + 31 & ~31
            got = next((h for h in (holes[::-1] if high else holes) if h[1] - h[0] >= size), None)
            if got is None:
                raise MemoryError(f"{name} {size}: {[(h[0], h[1] - h[0]) for h in holes]}")
            at, since = got[1] - size if high else got[0], got[2]
            got[0 if not high else 1] += -size if high else size
            if got[0] == got[1]:
                holes.remove(got)
            for lane in lanes:
                lane.wait(since)
            scope.callback(give_back, at, size)
            return nc.alloc_sbuf_tensor_at(name, shape, dtype, offset=at)

        def give_back(at, size):
            now = [lane.now() for lane in lanes]
            holes.append([at, at + size, now])
            holes.sort(key=lambda h: h[0])
            i = 0
            while i + 1 < len(holes):
                a, b = holes[i], holes[i + 1]
                if a[1] == b[0]:
                    latest = {}
                    for m_sem, value in marks([a[2], b[2]]):
                        old = latest.get(id(m_sem))
                        latest[id(m_sem)] = (m_sem, max(value, old[1] if old else 0))
                    holes[i:i + 2] = [[a[0], b[1], list(latest.values())]]
                else:
                    i += 1

        def fence():
            all_now = [lane.now() for lane in lanes]
            for lane in lanes:
                lane.wait(all_now)

        ring = sb(top, "weight_ring", [P, RING, SLOT])
        WS = sb(top, "weight_split", [P, SPLIT_RING, 2, SLOT], F32R)
        SQ = sb(top, "squares", [P, 2, T2])
        X = sb(top, "residual", [P, KT, T2])
        C = {n: sb(top, "c_" + n, [P, CONST_W[n]]) for n in CONSTS if n not in ("bucket_of", "log_reach", "flip")}
        vecs = sb(top, "vecs", [P, VECS])
        MOD = sb(top, "modulation", [P, 2, 2, 48])
        GS = sb(top, "gain_scale", [P, 2, 2, 2, KT])
        rs = sb(top, "row_stats", [P, 6])
        psum = top.enter_context(nc.psum_tensor("psum", [P, 8, 512], F32))

        def vec(name, i=0, rows=P):
            return vecs[0:rows, VEC[name][0] + i:VEC[name][0] + i + 1]

        ring_sem = [sem(f"ring_{i}") for i in range(RING)]
        ring_free = {}
        used = []
        queued = [0]
        landed_at = {}
        split_free = [None] * SPLIT_RING
        split_mark, split_of = {}, {}
        n_split, n_split_used = [0], [0]

        def queue_loads(upto):
            while queued[0] <= upto and queued[0] < len(used if order is None else order):
                i = queued[0]
                if i >= RING and i - RING not in ring_free:
                    break
                name, index, width, _ = (used if order is None else order)[i]
                src = dr[name][index] if width == SLOT else dr[name][index][:, 0:width]
                landed_at[i] = dma(sp, ring_sem[i % RING], 16 * (i // RING + 1), ring[:, i % RING, 0:width], src,
                                   ring_free.get(i - RING))
                queued[0] += 1

        def load(name, index, width=SLOT, split=False):
            i = len(used)
            used.append((name, index, width, split))
            if order is not None:
                assert order[i] == used[i]
            queue_loads(i + RING - 1)
            return i, landed_at[i]

        def free_slot(i, mark):
            ring_free[i] = mark

        def split_ahead(upto):
            while n_split[0] <= upto and n_split[0] < len(used if order is None else order):
                i = n_split[0]
                name, index, width, split = order[i] if order is not None else used[i]
                if split:
                    if order is not None:
                        queue_loads(i)
                    if i not in landed_at:
                        break
                    j = n_split_used[0]
                    k = j % SPLIT_RING
                    src = ring[:, i % RING, 0:width]
                    hi = act.issue(lambda eng, k=k, src=src, width=width: eng.copy(WS[:, k, 0, 0:width], src),
                                   landed_at[i], split_free[k])
                    lo = v_tt(WS[:, k, 1, 0:width], src, WS[:, k, 0, 0:width].bitcast(F32), ALU.subtract, hi, split_free[k],
                              lane=pool if j % 3 == 2 else dve)
                    ring_free[i] = lo
                    split_mark[i], split_of[i] = lo, k
                    n_split_used[0] += 1
                n_split[0] += 1

        def load_split(name, index, width=SLOT):
            i, _ = load(name, index, width, True)
            split_ahead(i + AHEAD if order is not None else i)
            return split_of[i], split_mark[i]

        bank_free = [None] * 8
        next_bank = {"pair": 0, "one": 0, "turn": 0}
        PAIRS, ONES, TURN = [0, 2, 4, 6], [0, 1, 2, 3, 4, 5, 6, 7], [6, 7]

        def take(n=1, pool_=None):
            kind, banks = (pool_, {"turn": TURN, "logits": [0, 2, 4]}[pool_]) if pool_ else ("pair", PAIRS) if n == 2 else ("one", ONES)
            b = banks[next_bank.get(kind, 0) % len(banks)]
            next_bank[kind] = next_bank.get(kind, 0) + 1
            if pool_ is None:
                next_bank["one" if n == 2 else "pair"] = (b + n) % 8 if n == 2 else (b // 2 + 1) % 4
            return b

        def bank(b, w=512, n=1):
            if n == 1:
                return psum[:, b, 0:w]
            return psum[:, b:b + 2, :].rearrange("p b w -> p (b w)")[:, 0:w]

        def mm(out, lhsT, rhs, start, stop, *after, signal=False):
            return pe.issue(lambda eng: eng.matmul(out, lhsT, rhs, start=start, stop=stop), *after, signal=signal)

        side = [0]

        def copy(out, in_, *after):
            side[0] += 1
            if side[0] % 2:
                return act.issue(lambda eng: eng.copy(out, in_), *after)
            return dve.issue(lambda eng: eng.tensor_copy(out, in_), *after)

        def v_tt(out, a, b, op, *after, lane=None):
            return (lane or dve).issue(lambda eng: eng.tensor_tensor(out, a, b, op), *after)

        def v_ts(out, a, s1, s2, op0, op1, *after, lane=None):
            if s2 is None:
                return (lane or dve).issue(lambda eng: eng.tensor_scalar(out, a, s1, None, op0), *after)
            return (lane or dve).issue(lambda eng: eng.tensor_scalar(out, a, s1, s2, op0, op1), *after)

        def v_stt(out, a, s, b, op0, op1, *after):
            return dve.issue(lambda eng: eng.scalar_tensor_tensor(out=out, in0=a, scalar=s, in1=b, op0=op0, op1=op1), *after)

        def fn(out, in_, f, *after, **kw):
            return act.issue(lambda eng: eng.activation(out, in_, f, **kw), *after)

        def zero(lane, out, *after, value=0.0):
            return lane.issue(lambda eng: eng.memset(out, value), *after)

        def recip(out, in_, *after):
            return dve.issue(lambda eng: eng.reciprocal(out, in_), *after)

        def neg_rowmax(out, in_, *after):
            return dve.issue(lambda eng: eng.tensor_reduce(out, in_, AX.X, ALU.max, negate=True), *after)

        def turn(out, in_, *after, signal=True):
            return pe.issue(lambda eng: eng.transpose(out, in_, C["ident"][:, :]), *after, signal=signal)

        def copy_on(lane, out, in_, *after):
            if lane is act:
                return act.issue(lambda eng: eng.copy(out, in_), *after)
            return lane.issue(lambda eng: eng.tensor_copy(out, in_), *after)

        def scan(out, decay, add, *after):
            return dve.issue(lambda eng: eng.tensor_tensor_scan(out, decay, add, 0.0, ALU.mult, ALU.add), *after)

        def dot(scratch, a, b, out, *after):
            return dve.issue(lambda eng: eng.tensor_tensor_reduce(out=scratch, in0=a, in1=b, scale=1.0, scalar=0.0,
                                                                  op0=ALU.mult, op1=ALU.add, accum_out=out), *after)

        def dma(lane, sem_, total, dst, src, *after):
            return lane.dma(sem_, total, lambda eng: eng.dma_start(dst, src), *after)

        X1, XB = [(0, S)], [(0, S), (S, T2)]

        got = sem("small_inputs")
        n_got = [0]

        def fetch(dst, src):
            n_got[0] += 16
            return dma(act, got, n_got[0], dst, src)

        small = {}
        for name, rows, cols in (("w_a2", B_RANK, P), ("rel_bias", REL_BUCKETS, A_HEADS + C_HEADS),
                                 ("fw1", 33, 128), ("fw2", 64, 128), ("fw3", 64, 1024)):
            small[name] = sb(top, "s_" + name, [P, cols])
            fetch(small[name][0:rows, :], dr[name])
        for n in C:
            fetch(C[n][:, :], dr["c_" + n])
        fetch(vecs[:, :], dr["vecs"])
        fetch(X[:, :, 0:S], dr["x_t"])
        loaded = fetch(X[:, :, S:T2], dr["ctx_t"])
        for lane in lanes:
            lane.wait(loaded)

        class SquareSum:

            def __init__(self, ranges):
                self.lo, self.hi, self.n, self.mark = ranges[0][0], ranges[-1][1], 0, None
                self.since = [lane.now() for lane in lanes]

            def add(self, src, ready):
                a, z = self.lo, self.hi
                if self.n == 0:
                    self.mark = fn(SQ[:, 0, a:z], src[:, a:z], ACT.Square, ready, self.since)
                else:
                    m = fn(SQ[:, 1, a:z], src[:, a:z], ACT.Square, ready, self.mark)
                    self.mark = v_tt(SQ[:, 0, a:z], SQ[:, 0, a:z], SQ[:, 1, a:z], ALU.add, m)
                self.n += 1

            def inverse(self, n):
                nt = (self.hi - self.lo) // P
                b = take(1)
                for t in range(nt):
                    m = mm(psum[:, b, t:t + 1], SQ[:, 0, self.lo + t * P:self.lo + (t + 1) * P], C["ones"][:, 0:1], True, True,
                           self.mark, bank_free[b], signal=t == nt - 1)
                m = v_ts(rs[:, 0:nt], psum[:, b, 0:nt], 1.0 / n, EPS, ALU.mult, ALU.add, m)
                bank_free[b] = m
                m = fn(rs[:, 0:nt], rs[:, 0:nt], ACT.Sqrt, m)
                m = recip(rs[:, 0:nt], rs[:, 0:nt], m)
                dg = SQ[:, 1, 0:nt * P].rearrange("p (t q) -> p t q", q=P)
                m = v_tt(dg, C["ident"][:, :].unsqueeze(1).broadcast_to([P, nt, P]),
                         rs[:, 0:nt].unsqueeze(2).broadcast_to([P, nt, P]), ALU.mult, m)
                b = take(2)
                m2 = mm(bank(b, min(nt, 4) * P), C["ones"][:, :], SQ[:, 1, 0:min(nt, 4) * P], True, True, m, bank_free[b],
                        bank_free[b + 1], signal=True)
                if nt > 4:
                    m2 = mm(bank(b + 1, (nt - 4) * P), C["ones"][:, :], SQ[:, 1, 4 * P:nt * P], True, True, signal=True)
                return b, m2

        def all_squares(src, nt, ranges, ready):
            sums = SquareSum(ranges)
            for t in range(nt):
                sums.add(src(t), ready[t] if isinstance(ready, list) else ready)
            return sums

        def normed(sums, n, src, dst, nt, ranges, gain):
            b, ready = sums.inverse(n)
            out = []
            for t in range(nt):
                ms = []
                for r, (a, z) in enumerate(ranges):
                    ms.append(v_stt(dst(t)[:, a:z], src(t)[:, a:z], gain(t, r), bank(b + r, z - a), ALU.mult, ALU.mult, ready))
                out.append(ms)
            bank_free[b] = bank_free[b + 1] = ms
            return out

        def normed_split(sums, n, HS, ranges, gain, shift=None):
            b, ready = sums.inverse(n)
            out = []
            last = [None, None]
            for t in range(KT):
                ms, tm = [], []
                for r, (a, z) in enumerate(ranges):
                    m = v_stt(SQ[:, t % 2, a:z], X[:, t, a:z], gain(t, r), bank(b + r, z - a), ALU.mult, ALU.mult, ready, last[t % 2])
                    tm.append(m)
                    tmp, hi, lo = SQ[:, t % 2, a:z], HS[:, 0, t, a:z], HS[:, 1, t, a:z]
                    if shift is None:
                        m = act.issue(lambda eng, hi=hi, tmp=tmp: eng.copy(hi, tmp), m)
                        m = v_tt(lo, tmp, hi.bitcast(F32), ALU.subtract, m, lane=pool)
                    else:
                        m = fn(hi, tmp, ACT.Identity, m, bias=shift(t, r), scale=1.0)
                        m = v_stt(lo, tmp, shift(t, r), hi.bitcast(F32), ALU.add, ALU.subtract, m)
                    ms.append(m)
                last[t % 2] = ms
                out.append(ms)
            bank_free[b] = bank_free[b + 1] = tm
            return out

        def split_mix(HS, MIX, ranges):
            lo, hi = ranges[0][0], ranges[-1][1]
            out = []
            for t in range(KT):
                m = copy_on(act, HS[:, 0, t, lo:hi], MIX[:, t, lo:hi])
                out.append(v_tt(HS[:, 1, t, lo:hi], MIX[:, t, lo:hi], HS[:, 0, t, lo:hi].bitcast(F32), ALU.subtract, m,
                                lane=pool if t % 2 else dve))
            return out

        def products(b, ranges, w_hi, w_lo, x, k, n, ready, signal):
            for w, part in ((w_hi, 0), (w_hi, 1), (w_lo, 0)):
                for r, (lo, hi) in enumerate(ranges):
                    m = mm(psum[:, b + r, 0:hi - lo], w, x(part, k, lo, hi), k == 0 and w is w_hi and part == 0,
                           k == n - 1 and w is w_lo, ready, bank_free[b + r] if k == 0 and w is w_hi and part == 0 else None,
                           signal=signal and w is w_lo and r == len(ranges) - 1)
            return m

        def product(chunks, x, x_ready, ranges, take_out):
            b = take(2)
            total = sum(c[2] for c in chunks)
            k = 0
            for name, index, nk in chunks:
                slot, ready = load_split(name, index, nk * P)
                for j in range(nk):
                    last = products(b, ranges, WS[:, slot, 0, j * P:(j + 1) * P], WS[:, slot, 1, j * P:(j + 1) * P], x, k, total,
                                    [ready, x_ready[k] if isinstance(x_ready, list) else x_ready], j == nk - 1)
                    k += 1
                split_free[slot] = last
            for r, (lo, hi) in enumerate(ranges):
                bank_free[b + r] = take_out(psum[:, b + r, 0:hi - lo], lo, hi, last)

        def mlp(layer, w1, w2, HS, ranges, x_ready, gate, work):
            with ExitStack() as scope:
                width = ranges[-1][1]
                G = sb(scope, f"hidden_{layer}", [P, 2, 2 * GROUP, width], F32R)
                act_tmp = sb(scope, f"hidden_tmp_{layer}", [P, 2, width])
                g_ready, g_read, tmp_read = {}, [None] * (2 * GROUP), [None, None]
                sums = SquareSum(ranges)
                x_of = lambda part, k, a, z: HS[:, part, k, a:z]
                lo, hi = ranges[0][0], ranges[-1][1]

                def up(f):
                    k, j = f % (2 * GROUP), f % 2
                    ms = []

                    def relu(ps, a, z, mark):
                        r = act_tmp[:, j, a:z]
                        got_it = fn(r, ps, ACT.Relu, mark, tmp_read[j])
                        h = fn(G[:, 0, k, a:z], r, ACT.Square, got_it, g_read[k])
                        sq = v_tt(r, r, r, ALU.mult, h, lane=pool)
                        ms.append(v_tt(G[:, 1, k, a:z], r, G[:, 0, k, a:z].bitcast(F32), ALU.subtract, sq, g_read[k]))
                        return got_it
                    product([w1(f)], x_of, x_ready, ranges, relu)
                    g_ready[f] = tmp_read[j] = ms
                    next(work, None)

                def down(g):
                    for m in range(0, KT, 2):
                        slot, ready = load_split(*w2(g, m // 2))
                        for i in range(2):
                            b = take(2)
                            for j in range(GROUP):
                                f = g * GROUP + j
                                k = f % (2 * GROUP)
                                w = WS[:, slot, :, (i * GROUP + j) * P:(i * GROUP + j + 1) * P]
                                last = products(b, ranges, w[:, 0, :], w[:, 1, :], lambda part, _, a, z, k=k: G[:, part, k, a:z], j, GROUP,
                                                [ready, g_ready[f]], j == GROUP - 1)
                            ms = []
                            for r, (a, z) in enumerate(ranges):
                                x, ps = X[:, m + i, a:z], psum[:, b + r, 0:z - a]
                                if gate is None:
                                    bank_free[b + r] = v_tt(x, ps, x, ALU.add, last)
                                else:
                                    bank_free[b + r] = v_stt(x, ps, gate(m + i, a), x, ALU.mult, ALU.add, last)
                                ms.append(bank_free[b + r])
                            if g == NGROUP - 1:
                                sums.add(X[:, m + i, :], ms)
                        split_free[slot] = last
                        next(work, None)
                    for j in range(GROUP):
                        g_read[(g * GROUP + j) % (2 * GROUP)] = last

                for g in range(NGROUP + 1):
                    if g < NGROUP:
                        for j in range(GROUP):
                            up(g * GROUP + j)
                    if g > 0:
                        down(g - 1)
                for _ in work:
                    pass
            return sums

        def attention(scope, tag, units, scale, q_of, k_of, v_of, strip_of, put, kmax):
            NP, NPT = 3, 2 if kmax == S else 1
            Pb = sb(scope, tag + "_prob", [P, NP, kmax])
            PT = sb(scope, tag + "_probT", [P, NPT, kmax // P, S])
            st = sb(scope, tag + "_stat", [P, NP, 4])
            items = [(u, i) for u, unit in enumerate(units) for i in range(len(unit[1]))]
            info = [dict() for _ in items]
            pt_read = [None] * NPT
            pt_done = {}

            def logits(n):
                u, i = items[n]
                head, qs, k0 = units[u]
                q0, w = qs[i]
                nb = 1 if w <= 512 else 2
                b = take(2, "logits")
                for off in range(0, w, 512):
                    pw = min(512, w - off)
                    m = mm(psum[:, b + off // 512, 0:pw], q_of(head, q0, q0 + P), k_of(head, k0 + off, k0 + off + pw),
                           True, True, bank_free[b + off // 512], signal=off + 512 >= w)
                info[n].update(bank=b, nb=nb, w=w, head=head, q0=q0, logits=m)

            def exps(n):
                d = info[n]
                w, j = d["w"], n % NP
                s = bank(d["bank"], w, d["nb"])
                free = info[n - NP]["pt"] if n >= NP else None
                if strip_of is not None:
                    m = v_stt(Pb[:, j, 0:w], s, scale, strip_of(d["head"], d["q0"], w), ALU.mult, ALU.add, d["logits"], free)
                    bank_free[d["bank"]] = m
                    m = neg_rowmax(st[:, j, 0:1], Pb[:, j, 0:w], m)
                    m = fn(Pb[:, j, 0:w], Pb[:, j, 0:w], ACT.Exp, m, bias=st[:, j, 0:1], scale=1.0, accum_out=st[:, j, 1:2])
                else:
                    m = neg_rowmax(st[:, j, 2:3], s, d["logits"], free)
                    m = v_ts(st[:, j, 0:1], st[:, j, 2:3], scale, None, ALU.mult, None, m)
                    m = fn(Pb[:, j, 0:w], s, ACT.Exp, m, free, bias=st[:, j, 0:1], scale=scale, accum_out=st[:, j, 1:2])
                    for r in range(d["nb"]):
                        bank_free[d["bank"] + r] = m
                d["exp"] = m

            def diag(n):
                d = info[n]
                j = n % NP
                m = recip(st[:, j, 3:4], st[:, j, 1:2], d["exp"])
                d["prob"] = v_ts(Pb[:, j, 0:d["w"]], Pb[:, j, 0:d["w"]], st[:, j, 3:4], None, ALU.mult, None, m)

            def turn_p(n):
                u, i = items[n]
                d = info[n]
                j = n % NP
                nk = d["w"] // P
                col = d["q0"] - units[u][1][0][0]
                last = None
                for g in range(0, nk, 4):
                    b = take(1, "turn")
                    gn = min(4, nk - g)
                    for t in range(gn):
                        last = turn(psum[:, b, t * P:(t + 1) * P], Pb[:, j, (g + t) * P:(g + t + 1) * P],
                                    d["prob"], bank_free[b] if t == 0 else None, signal=t == gn - 1)
                    m = copy(PT[:, u % NPT, g:g + gn, col:col + P], psum[:, b, 0:gn * P].rearrange("p (t q) -> p t q", q=P),
                             last, pt_read[u % NPT] if i == 0 else None)
                    bank_free[b] = m
                    pt_done.setdefault(u, []).append(m)
                d["pt"] = last
                if i == len(units[u][1]) - 1:
                    values(u)

            def values(u):
                head, qs, k0 = units[u]
                b = take(1, "turn")
                wq = P * len(qs)
                nk = max(w for _, w in qs) // P
                r0 = 64 * (head % 2)
                for t in range(nk):
                    first = next(i for i, (_, w) in enumerate(qs) if w > t * P) * P
                    m = mm(psum[r0:r0 + DH, b, first:wq], v_of(head, k0 // P + t), PT[:, u % NPT, t, first:wq],
                           t == 0, t == nk - 1, pt_done[u], bank_free[b] if t == 0 else None, signal=t == nk - 1)
                pt_read[u % NPT] = m
                bank_free[b] = put(head, psum[r0:r0 + DH, b, 0:wq], qs[0][0], qs[0][0] + wq, m)

            for n in range(-3, len(items)):
                if 0 <= n + 3 < len(items):
                    logits(n + 3)
                if 0 <= n + 2 < len(items):
                    exps(n + 2)
                if 0 <= n + 1 < len(items):
                    diag(n + 1)
                if n >= 0:
                    turn_p(n)

        mod_sem = [sem("mod_ring_0"), sem("mod_ring_1")]
        mod_cond = sem("mod_cond")
        ready_mod = {}

        def modulation(scope):
            CB = sb(scope, "cond_all_partitions", [P, 2, D])
            junk = sb(scope, "mod_scratch", [P, D])
            mod_ring = sb(scope, "mod_ring", [P, 2, D])
            dma(pool, mod_cond, 16, CB[:, 0, :], dr["cond"][0:1, :].broadcast_to([P, D]))
            m = dma(pool, mod_cond, 32, CB[:, 1, :], dr["cond"][1:2, :].broadcast_to([P, D]))
            cond = None
            for v in range(2):
                m = fn(junk[:, :], CB[:, v, :], ACT.Exp, m, cond, scale=-1.0)
                m = v_ts(junk[:, :], junk[:, :], 1.0, None, ALU.add, None, m)
                m = recip(junk[:, :], junk[:, :], m)
                cond = v_tt(CB[:, v, :], CB[:, v, :], junk[:, :], ALU.mult, m)
            yield
            read = [None, None]
            m = cond
            i = 0
            for l in range(2):
                for t in range(48):
                    k = i % 2
                    landed = dma(pool, mod_sem[k], 16 * (i // 2 + 1), mod_ring[:, k, :], dr["w_mod"][l, t], read[k])
                    for v in range(2 if l == 0 or t < 16 else 1):
                        m = dot(junk[:, :], mod_ring[:, k, :], CB[:, v, :], MOD[:, l, v, t:t + 1], landed, cond, m)
                    read[k] = m
                    i += 1
                    if t % 2:
                        yield
                b0 = VEC[f"bmod_{l}"][0]
                for v in range(2):
                    n = 48 if l == 0 or v == 0 else 16
                    m = v_tt(MOD[:, l, v, 0:n], MOD[:, l, v, 0:n], vecs[:, b0:b0 + n], ALU.add, m)
                    for w in range(2):
                        if l == 1 and v == 1 and w == 1:
                            continue
                        n0 = VEC[f"n{w + 1}_{l}"][0]
                        sc = 24 * w + 8
                        m = v_stt(GS[:, l, w, v, :], MOD[:, l, v, sc:sc + 8], 1.0, vecs[:, n0:n0 + 8], ALU.add, ALU.mult, m)

        strips = ExitStack()
        bias_rows = sb(strips, "bias_rows", [P, STRIP])
        tab = {n: sb(strips, "c_" + n, [P, STRIP]) for n in ("bucket_of", "log_reach")}
        flip = sb(strips, "c_flip", [P, P])
        fetch(flip[:, :], dr["c_flip"])
        raw = sb(strips, "strip_raw", [P, 2, S])
        STR = nc.dram_tensor("bias_scratch", [A_HEADS + C_HEADS, STRIP], F32, kind="Internal").ap()
        SAVE = nc.dram_tensor("strip_scratch", [A_HEADS + C_HEADS, P, S], F32, kind="Internal").ap()
        fetch(tab["bucket_of"][:, :], dr["c_bucket_of"])
        t_in = fetch(tab["log_reach"][:, :], dr["c_log_reach"])
        NH = A_HEADS + C_HEADS
        b = take(2)
        m = mm(psum[0:NH, b, 0:512], small["rel_bias"][0:REL_BUCKETS, :], tab["bucket_of"][0:REL_BUCKETS, 0:512], True, True, t_in)
        m = mm(psum[0:NH, b + 1, 0:128], small["rel_bias"][0:REL_BUCKETS, :], tab["bucket_of"][0:REL_BUCKETS, 512:640], True, True, signal=True)
        m = v_tt(bias_rows[0:NH, :], bank(b, STRIP, 2)[0:NH, :], tab["log_reach"][0:NH, :], ALU.add, m, t_in)
        bank_free[b] = bank_free[b + 1] = m
        s_strip = sem("bias_strip")
        s_raw = [sem("strip_raw_0"), sem("strip_raw_1")]
        s_save = sem("strip_saved")
        m = dma(act, s_strip, 16, STR, bias_rows[0:NH, :], m)
        base = STR
        s_out = sb(strips, "strip_out", [P, 2, S])
        saved = [None, None]
        n_saved = 0
        s_save2 = [sem("strip_saved_0"), sem("strip_saved_1")]
        flipped = [None, None]
        for h in range(NH):
            k = h % 2
            src = bass.AP(tensor=base.tensor, offset=base.offset + h * STRIP, ap=[[1, P], [1, S]])
            got_raw = dma(act, s_raw[k], 16 * (h // 2 + 1), raw[:, k, :], src, m, flipped[k])
            b = take(1)
            fl = mm(bank(b), flip[:, :], raw[:, k, :], True, True, got_raw, bank_free[b], signal=True)
            flipped[k] = fl
            cp = copy_on(dve, s_out[:, k, :], bank(b), fl, saved[k])
            bank_free[b] = cp
            saved[k] = dma(act, s_save2[k], 16 * (h // 2 + 1), SAVE[h], s_out[:, k, :], cp)
        strips_saved = list(saved)
        for lane in lanes:
            lane.wait(strips_saved)
        fence()
        strips.close()

        block1 = ExitStack()
        V = sb(block1, "values", [P, S // P, D])
        B_ = sb(block1, "gla_in", [P, 5, S])
        qk = ExitStack()
        QK = sb(qk, "q_and_k", [P, 12, S])
        HS_1 = ExitStack()
        HS = sb(HS_1, "normed_1", [P, 2, KT, S], F32R)
        h_ready = normed_split(all_squares(lambda t: X[:, t, :], KT, X1, None), D, HS, X1, lambda t, r: vec("norm1", t))
        x_of = lambda part, k, a, z: HS[:, part, k, a:z]
        proj = []

        def keep(dst):
            def f(ps, a, z, mark):
                m = copy(dst, ps, mark)
                proj.append(m)
                return m
            return f

        dsts = [QK[:, i, :] for i in range(6)] + [B_[:, i, :] for i in range(4)] + [QK[:, i, :] for i in range(6, 12)]
        for i, dst in enumerate(dsts):
            product([("w_in1", i, KT)], x_of, h_ready, X1, keep(dst))
        product([("w_in1", 16, KT)], x_of, h_ready, X1, keep(B_[:, 4, :]))
        for half in range(2):
            bs = [take(1) for _ in range(4)]
            for s in range(4):
                slot, ready = load_split("w_v1", (half, s))
                for j in range(2):
                    k = 2 * s + j
                    for part, w in ((0, 0), (1, 0), (0, 1)):
                        for t in range(4):
                            m = mm(bank(bs[t]), HS[:, part, k, t * P:(t + 1) * P], WS[:, slot, w, j * 512:(j + 1) * 512],
                                   k == 0 and part + w == 0, k == KT - 1 and w == 1, ready,
                                   bank_free[bs[t]] if k == 0 and part + w == 0 else None, signal=(j == 1 and t == 3 and w == 1))
                split_free[slot] = m
            for t in range(4):
                c = copy(V[:, t, half * 512:(half + 1) * 512], bank(bs[t]), m)
                bank_free[bs[t]] = c
                proj.append(c)
        for lane in lanes:
            lane.wait(proj)
        fence()
        HS_1.close()
        mix1 = ExitStack()
        H = sb(mix1, "mix_1", [P, KT, S], high=True)

        n_strip = [0]
        s_load = sem("strip_load")
        for g in range(2):
            with ExitStack() as scope:
                ST = sb(scope, f"strips_{g}", [P, 6, S])
                fence()
                act.wait([lane.now() for lane in lanes])
                m = dma(act, s_load, 16 * (g + 1), ST[:, :, :], SAVE[6 * g:6 * g + 6].rearrange("h p c -> p h c"))
                for lane in lanes:
                    lane.wait(m)
                o = 6 * g
                units = [(h, [(P * i, P * (i + 1)) for i in range(4)], 0) for h in range(6)]
                attention(scope, f"att{g}", units, DH ** -0.5,
                          lambda h, a, z: QK[64 * (h % 2):64 * (h % 2) + 64, o + h // 2, a:z],
                          lambda h, a, z: QK[64 * (h % 2):64 * (h % 2) + 64, o + 3 + h // 2, a:z],
                          lambda h, t: V[:, t, (640 if g else 0) + h * DH:(640 if g else 0) + (h + 1) * DH],
                          lambda h, q0, w: ST[:, h, 384 - q0:384 - q0 + w],
                          lambda h, ps, a, z, mark: copy(H[64 * (h % 2):64 * (h % 2) + 64, (5 if g else 0) + h // 2, a:z], ps, mark), S)
                fence()
        qk.close()

        with ExitStack() as scope:
            def buf(name, *shape):
                return sb(scope, "gla_" + name, [P, *shape])
            Bc, la, e1, qs, eb, kt = (buf(n, S) for n in ("b", "la", "e1", "qs", "eb", "kt"))
            Q, K_, G_ = B_[:, 0, :], B_[:, 1, :], B_[:, 4, :]
            VT = buf("vT", 2, S)
            ktok = buf("ktok", 4, P)
            vm = buf("vm", 2, 512)
            BX = buf("state_blocks", 2, DH, NCHUNK)
            dec = buf("dec", NCHUNK)
            ACC = buf("acc", 2, S)
            carried = ExitStack()
            UX, DX, SX = (sb(carried, "gla_" + n, [P, DH, NCHUNK]) for n in ("u", "dec_all", "state"))
            fence()

            def ch(x):
                return x.rearrange("p (n c) -> p n c", c=B_CHUNK)
            b = take(1)
            m = mm(bank(b), small["w_a2"][0:B_RANK, :], G_[0:B_RANK, :], True, True, bank_free[b], signal=True)
            z = v_ts(la[:, :], bank(b), vec("gla_b"), None, ALU.add, None, m)
            bank_free[b] = z
            m = fn(e1[:, :], la[:, :], ACT.Abs, z)
            m = fn(e1[:, :], e1[:, :], ACT.Exp, m, scale=-1.0)
            m = fn(e1[:, :], e1[:, :], ACT.Ln, m, bias=1.0)
            m = v_stt(la[:, :], la[:, :], 0.0, e1[:, :], ALU.min, ALU.subtract, m)
            m = v_ts(la[:, :], la[:, :], 1.0 / B_TAU, None, ALU.mult, None, m)
            b_ready = scan(Bc[:, :], C["not_first"][:, :], la[:, :], m)
            q_s = v_ts(qs[:, :], Q, B_DK ** -0.5, None, ALU.mult, None)
            last_b = ch(Bc[:, :])[:, :, B_CHUNK - 1:B_CHUNK].broadcast_to([P, NCHUNK, B_CHUNK])
            m = v_tt(ch(kt[:, :]), last_b, ch(Bc[:, :]), ALU.subtract, b_ready)
            m = fn(kt[:, :], kt[:, :], ACT.Exp, m)
            k_end = v_tt(kt[:, :], kt[:, :], K_, ALU.mult, m)
            m = fn(dec[:, :], ch(Bc[:, :])[:, :, B_CHUNK - 1], ACT.Exp, b_ready)
            z0 = v_ts(DX[:, :, :], dec[:, :].unsqueeze(1).broadcast_to([P, DH, NCHUNK]), 1.0, None, ALU.mult, None, m)
            z0 = zero(dve, DX[:, :, 0:1], z0)
            m = fn(eb[:, :], Bc[:, :], ACT.Exp, b_ready)
            q_in = v_tt(eb[:, :], eb[:, :], qs[:, :], ALU.mult, m, q_s)
            b = take(1)
            for t in range(4):
                m = turn(psum[:, b, t * P:(t + 1) * P], kt[:, t * P:(t + 1) * P], k_end, bank_free[b], signal=t == 3)
            k_tok = copy(ktok[:, :, :].rearrange("p t c -> p (t c)"), bank(b), m)
            bank_free[b] = k_tok
            vt = []
            for f in range(2):
                b = take(1)
                for t in range(4):
                    m = turn(
                        psum[:, b, t * P:(t + 1) * P], V[:, t, 384 + f * P:384 + (f + 1) * P], bank_free[b], signal=t == 3)
                vt.append(copy(VT[:, f, :], bank(b), m))
                bank_free[b] = vt[-1]
            mask = C["in_chunk"][:, :].unsqueeze(2).broadcast_to([P, P // B_CHUNK, DH])
            vm_read = [None, None]
            u_done = []
            i = 0
            for t in range(4):
                b = take(1)
                for h in range(B_HEADS):
                    src = V[:, t, 384 + h * DH:384 + (h + 1) * DH].unsqueeze(1).broadcast_to([P, P // B_CHUNK, DH])
                    m = v_tt(vm[:, i % 2, :].rearrange("p (n v) -> p n v", v=DH), src, mask, ALU.mult, vm_read[i % 2])
                    m = mm(psum[32 * h:32 * h + 32, b, :], ktok[:, t, 32 * h:32 * h + 32], vm[:, i % 2, :], True, True, m, k_tok,
                           bank_free[b] if h == 0 else None, signal=True)
                    vm_read[i % 2] = m
                    i += 1
                m = copy_on(act, UX[:, :, 8 * t:8 * t + 8].rearrange("p v n -> p n v"),
                                                            bank(b).rearrange("p (n v) -> p n v", v=DH), m)
                bank_free[b] = m
                u_done.append(m)
            m = scan(
                SX[:, :, :].rearrange("p v n -> p (v n)"), DX[:, :, :].rearrange("p v n -> p (v n)"),
                UX[:, :, :].rearrange("p v n -> p (v n)"), u_done, z0)
            z1 = zero(pool, BX[:, :, :, :])
            for h in range(B_HEADS):
                bx = copy_on(act, BX[32 * h:32 * h + 32, h % 2], SX[32 * h:32 * h + 32], m, z1)
            fence()
            carried.close()
            D1, D2, D3 = buf("d1", 2, S), buf("d2", 2, S), buf("d3", 2, S)
            E_, T_ = buf("mul", 2, S), None
            p_read = [None, None]
            e_read = [None, None]
            acc_done = None
            for s in range(B_CHUNK):
                j, w = s % 2, B_CHUNK - s
                n = NCHUNK * w

                def cut(x, w=w, n=n):
                    return x[:, 0:n].rearrange("p (c w) -> p c w", w=w)
                m = v_tt(cut(D1[:, j, :]), ch(Bc[:, :])[:, :, s:], ch(Bc[:, :])[:, :, 0:w], ALU.subtract, p_read[j], b_ready)
                m = fn(D1[:, j, 0:n], D1[:, j, 0:n], ACT.Exp, m)
                m2 = v_tt(cut(D2[:, j, :]), ch(qs[:, :])[:, :, s:], ch(K_)[:, :, 0:w], ALU.mult, q_s, p_read[j], lane=pool)
                ready = v_tt(D3[:, j, 0:n], D1[:, j, 0:n], D2[:, j, 0:n], ALU.mult, m, m2, p_read[j], lane=pool)
                for pr in range(2):
                    b = take(1)
                    m = mm(bank(b, n), C["spread"][64 * pr:64 * pr + 64, :], D3[64 * pr:64 * pr + 64, j, 0:n], True, True,
                           ready, bank_free[b], signal=True)
                    p_read[j] = [m, ready]
                    if s == 0:
                        a = v_tt(ACC[:, pr, :], bank(b), VT[:, pr, :], ALU.mult, m, vt)
                        bank_free[b] = a
                    else:
                        a = v_tt(cut(E_[:, pr, :]), bank(b, n).rearrange("p (c w) -> p c w", w=w), ch(VT[:, pr, :])[:, :, 0:w],
                                 ALU.mult, m, e_read[pr])
                        bank_free[b] = a
                        e_read[pr] = v_tt(ch(ACC[:, pr, :])[:, :, s:], ch(ACC[:, pr, :])[:, :, s:], cut(E_[:, pr, :]), ALU.add, a,
                                          acc_done)
                        acc_done = e_read[pr]
            for pr in range(2):
                b = take(1)
                for n in range(1, NCHUNK):
                    m = mm(psum[:, b, n * B_CHUNK:(n + 1) * B_CHUNK], BX[64 * pr:64 * pr + 64, :, :, n - 1],
                           eb[64 * pr:64 * pr + 64, n * B_CHUNK:(n + 1) * B_CHUNK], True, True, bx, q_in, bank_free[b],
                           signal=n == NCHUNK - 1)
                m = v_tt(ACC[:, pr, B_CHUNK:], psum[:, b, B_CHUNK:], ACC[:, pr, B_CHUNK:], ALU.add, m, acc_done)
                bank_free[b] = m
                sq = fn(e1[:, :], ACC[:, pr, :], ACT.Square, m, [dve.now(), pe.now()])
                b = take(1)
                m = mm(bank(b), C["mean64"][:, :], e1[:, :], True, True, sq, bank_free[b], signal=True)
                m = v_ts(la[:, :], bank(b), EPS, None, ALU.add, None, m)
                bank_free[b] = m
                m = fn(la[:, :], la[:, :], ACT.Sqrt, m)
                m = recip(la[:, :], la[:, :], m)
                m = v_stt(la[:, :], la[:, :], vec("gla_norm", pr), ACC[:, pr, :], ALU.mult, ALU.mult, m)
                rr = B_[:, 2 + pr, :]
                x = fn(e1[:, :], rr, ACT.Exp, m, pe.now(), scale=-1.0)
                x = v_ts(e1[:, :], e1[:, :], 1.0, None, ALU.add, None, x)
                x = recip(e1[:, :], e1[:, :], x)
                x = v_tt(e1[:, :], e1[:, :], rr, ALU.mult, x)
                m = v_tt(H[:, 3 + pr, 0:S], e1[:, :], la[:, :], ALU.mult, x, m)
            fence()
        block1.close()

        with ExitStack() as tail:
            HS = sb(tail, "mix_split_1", [P, 2, KT, S], F32R)
            ready = split_mix(HS, H, X1)
            sums = SquareSum(X1)
            for m_ in range(KT):
                def add_x(ps, a, z, mark, m_=m_):
                    done = v_tt(X[:, m_, a:z], ps, X[:, m_, a:z], ALU.add, mark)
                    sums.add(X[:, m_, :], done)
                    return done
                product([("w_out1", m_, KT)], lambda part, k, a, z: HS[:, part, k, a:z], ready, X1, add_x)
            fence()
            mix1.close()
            h_ready = normed_split(sums, D, HS, X1, lambda t, r: vec("norm2", t))
            with ExitStack() as scope:
                sums = mlp("1", lambda f: ("w_ff1", f, KT), lambda g, m: ("w_ff2", (g, m)), HS, X1, h_ready, None, modulation(scope))
        fence()
        normed(sums, D, lambda t: X[:, t, :], lambda t: X[:, t, :], KT, X1, lambda t, r: vec("final1", t))
        fence()

        for l in range(2):
            last_layer = l == 1
            RG = X1 if last_layer else XB
            streams = [(0, S, "x")] if last_layer else [(0, S, "x"), (S, T2, "c")]
            norm_in = ExitStack()
            layer = ExitStack()
            LAT = sb(layer, f"latents_{l}", [P, 5, T2])
            KR = sb(layer, f"k_rope_{l}", [P, T2])
            tmp = SQ
            mixed = ExitStack()
            early = ExitStack()
            FU = sb(early, f"fourier_in_{l}", [P, 2, T2])
            HU = sb(early, f"hyena_in_{l}", [P, 6, T2])
            HS = sb(norm_in, f"normed_in_{l}", [P, 2, KT, T2], F32R)
            fence()
            h_ready = normed_split(all_squares(lambda t: X[:, t, :], KT, XB, None), D, HS, XB, lambda t, r: GS[:, l, 0, r, t:t + 1],
                                   lambda t, r: MOD[:, l, r, t:t + 1])
            proj = []

            def keep2(dst):
                def f(ps, a, z, mark):
                    m = copy(dst[:, a:z], ps, mark)
                    proj.append(m)
                    return m
                return f

            def rotated(dst, ps, a, mark):
                m0 = v_tt(tmp[64:96, 0, 0:S], ps[64:96], C["rope"][64:96, :], ALU.mult, mark, dve.now())
                m1 = v_tt(tmp[64:96, 1, 0:S], ps[96:128], C["rope"][96:128, :], ALU.mult, mark, dve.now())
                m = v_tt(dst, tmp[64:96, 0, 0:S], tmp[64:96, 1, 0:S], ALU.add, m0, m1)
                return m, m1

            x_of = lambda part, k, a, z: HS[:, part, k, a:z]
            for i in range(3):
                product([("w_in2", (l, i), KT)], x_of, h_ready, RG, keep2(LAT[:, i, :]))
            for i in range(3, 5):
                product([("w_in2", (l, i), KT)], x_of, h_ready, XB, keep2(LAT[:, i, :]))
            for i in range(2):
                product([("w_in2", (l, 5 + i), KT)], x_of, h_ready, RG, keep2(FU[:, i, :]))
            for i in range(6):
                product([("w_in2", (l, 7 + i), KT)], x_of, h_ready, RG, keep2(HU[:, i, :]))

            def kr_out(ps, a, z, mark):
                if a == 0:
                    m, m1 = rotated(KR[64:96, a:z], ps, a, mark)
                    proj.append(m)
                    return m
                m = copy(KR[64:96, a:z], ps[64:96], mark)
                proj.append(m)
                return m
            product([("w_in2", (l, 13), KT)], x_of, h_ready, XB, kr_out)
            for lane in lanes:
                lane.wait(proj)
            fence()
            norm_in.close()
            mix2 = ExitStack()
            H = sb(mix2, f"mix_2_{l}", [P, KT, T2], high=True)
            U = sb(mixed, f"conv_out_{l}", [P, 6, T2])

            with ExitStack() as scope:
                A_ = sb(scope, f"fourier_mid_{l}", [P, 4, 512])
                for lo, hi, nm in streams:
                    nt = (hi - lo) // P
                    a_done = []
                    fence()
                    for t in range(nt):
                        b = take(1)
                        for f in range(2):
                            m = mm(psum[:, b, f * 256:(f + 1) * 256], FU[:, f, lo + t * P:lo + (t + 1) * P], C["dft64"][:, :],
                                   True, True, bank_free[b] if f == 0 else None, signal=f == 1)
                        m = copy(A_[:, t, :], bank(b), m)
                        bank_free[b] = m
                        a_done.append(m)
                    b = take(2)
                    i0, n_rows, wid = plan["fourier_" + nm]
                    L = hi - lo
                    for t in range(nt):
                        slot, landed = load("tables", i0 + t, wid)
                        for f in range(2):
                            for cs in range(2):
                                m = mm(psum[:, b + f, 0:L], A_[:, t, f * 256 + cs * P:f * 256 + (cs + 1) * P],
                                       ring[:, slot % RING, cs * L:(cs + 1) * L], t == 0 and cs == 0, t == nt - 1 and cs == 1,
                                       landed, a_done[t], bank_free[b + f] if t == 0 and cs == 0 else None, signal=f == 1 and cs == 1)
                        free_slot(slot, m)
                    for f in range(2):
                        m2 = copy(H[:, 4 + f, lo:hi], psum[:, b + f, 0:L], m)
                        bank_free[b + f] = m2
                fence()

            with ExitStack() as scope:
                cw, cb = VEC[f"cw_{l}"][0], VEC[f"cb_{l}"][0]
                fence()
                hi_all = streams[-1][1]
                for i in range(6):
                    m = fn(U[:, i, 0:hi_all], HU[:, i, 0:hi_all], ACT.Identity, bias=vecs[:, cb + i:cb + i + 1],
                           scale=vecs[:, cw + 6 + i:cw + 7 + i])
                    for lo, hi, nm in streams:
                        m = v_stt(U[:, i, lo + 1:hi], HU[:, i, lo:hi - 1], vecs[:, cw + i:cw + i + 1], U[:, i, lo + 1:hi], ALU.mult, ALU.add, m)
                        m = v_stt(U[:, i, lo:hi - 1], HU[:, i, lo + 1:hi], vecs[:, cw + 12 + i:cw + 13 + i], U[:, i, lo:hi - 1], ALU.mult, ALU.add, m)
                for i in range(2):
                    zm = v_tt(U[:, 2 + i, 0:hi_all], U[:, 2 + i, 0:hi_all], U[:, 4 + i, 0:hi_all], ALU.mult, m)
                Z = lambda i: U[:, 2 + i, :]
                fence()
                early.close()
                for lo, hi, nm in streams:
                    with ExitStack() as one:
                        L = hi - lo
                        nt = L // P
                        h1 = sb(one, f"filt_h1_{l}{nm}", [P, S])
                        h2 = sb(one, f"filt_h2_{l}{nm}", [P, S])
                        rn = sb(one, f"filt_rn_{l}{nm}", [P, S])
                        HF = sb(one, f"filt_hf_{l}{nm}", [P, nt, 512])
                        ZU = sb(one, f"spec_in_cos_{l}{nm}", [P, nt, 512])
                        ZW = sb(one, f"spec_in_sin_{l}{nm}", [P, nt, 512])
                        RE = sb(one, f"spec_re_{l}{nm}", [P, 2, 512])
                        IM = sb(one, f"spec_im_{l}{nm}", [P, 2, 512])
                        Y = sb(one, f"spec_prod_{l}{nm}", [P, nt, 2, 256])
                        T0 = sb(one, f"spec_tmp_{l}{nm}", [P, 2, 256])
                        nrm = sb(one, f"filt_norm_{l}{nm}", [P, 2])
                        fence()

                        def sine(dst, ps, mark, bias_name):
                            d = dst[0:64, 0:L]
                            n_ = rn[0:64, 0:L]
                            a0 = v_ts(d, ps, vec(bias_name, 0, 64), vec(f"ffr_{l}", 0, 64), ALU.add, ALU.mult, mark)
                            magic = 1.5 * 2 ** 23
                            m = v_ts(n_, d, 1.0 / (2 * math.pi), magic, ALU.mult, ALU.add, a0)
                            m = v_ts(n_, n_, magic, None, ALU.subtract, None, m)
                            c1 = 6.28125
                            c2 = float(np.float32(np.round((2 * math.pi - c1) * 2 ** 22) / 2 ** 22))
                            c3 = 2 * math.pi - c1 - c2
                            for c in (c1, c2, c3):
                                m = v_stt(d, n_, -c, d, ALU.mult, ALU.add, m)
                            m = v_ts(d, d, 3.1415925, -3.1415925, ALU.min, ALU.max, m)
                            return a0, fn(d, d, ACT.Sin, m)

                        i0 = plan["emb_" + nm][0]
                        slot, landed = load("tables", i0, L)
                        b = take(1)
                        m = mm(psum[0:64, b, 0:L], small["fw1"][0:33, 64 * l:64 * l + 64], ring[0:33, slot % RING, 0:L], True, True,
                               landed, bank_free[b], signal=True)
                        free_slot(slot, m)
                        bank_free[b], m = sine(h1, psum[0:64, b, 0:L], m, f"fb1_{l}")
                        b = take(1)
                        m = mm(psum[0:64, b, 0:L], small["fw2"][0:64, 64 * l:64 * l + 64], h1[0:64, 0:L], True, True, m, bank_free[b], signal=True)
                        bank_free[b], h2_ready = sine(h2, psum[0:64, b, 0:L], m, f"fb2_{l}")
                        i0, n_rows, wid = plan["decay_" + nm]
                        hf = []
                        for t in range(nt):
                            if t % 2 == 0:
                                slot, landed = load("tables", i0 + t // 2)
                            b = take(1)
                            m = mm(bank(b), h2[0:64, t * P:(t + 1) * P], small["fw3"][0:64, 512 * l:512 * l + 512], True, True,
                                   h2_ready, bank_free[b], signal=True)
                            m = v_tt(HF[:, t, :], bank(b), ring[:, slot % RING, (t % 2) * 512:(t % 2) * 512 + 512], ALU.mult, m, landed)
                            bank_free[b] = m
                            if t % 2:
                                free_slot(slot, m)
                            u1 = v_tt(ZU[:, t, 256:512], HF[:, t, 0:256], HF[:, t, 256:512], ALU.add, m)
                            u2 = v_tt(ZW[:, t, 256:512], HF[:, t, 0:256], HF[:, t, 256:512], ALU.subtract, m, lane=pool)
                            ab = fn(HF[:, t, :], HF[:, t, :], ACT.Abs, u1, u2)
                            hf.append([ab, u1, u2])
                        b = take(1)
                        for ct in range(2):
                            i = 0
                            for t in range(nt):
                                for side_ in range(2):
                                    m = mm(psum[:, b, ct:ct + 1], HF[:, t, side_ * 256 + ct * P:side_ * 256 + (ct + 1) * P], C["ones"][:, 0:1],
                                           i == 0, i == 2 * nt - 1, hf, bank_free[b], signal=i == 2 * nt - 1)
                                    i += 1
                        nm_ready = recip(nrm[:, :], psum[:, b, 0:2], m)
                        bank_free[b] = nm_ready
                        zt = []
                        for t in range(nt):
                            b = take(1)
                            for ct in range(2):
                                m = turn(
                                    psum[:, b, ct * P:(ct + 1) * P], Z(ct)[:, lo + t * P:lo + (t + 1) * P], zm, bank_free[b], signal=ct == 1)
                            m1 = copy_on(act, ZU[:, t, 0:256], psum[:, b, 0:256], m)
                            m2 = copy_on(dve, ZW[:, t, 0:256], psum[:, b, 0:256], m, m1)
                            bank_free[b] = m2
                            zt.append([m1, m2])
                        i0, n_rows, wid = plan["fwd_" + nm]
                        y_done = [None] * nt
                        for f in range(nt):
                            j = f % 2
                            slot, landed = load("tables", i0 + f, wid)
                            b = take(2)
                            for cs, src in enumerate((ZU, ZW)):
                                for t in range(nt):
                                    m = mm(bank(b + cs), ring[:, slot % RING, cs * nt * P + t * P:cs * nt * P + (t + 1) * P], src[:, t, :],
                                           t == 0, t == nt - 1, landed, zt, hf, bank_free[b + cs] if t == 0 else None, signal=t == nt - 1)
                            free_slot(slot, m)
                            free = y_done[f - 2] if f >= 2 else None
                            re = copy_on(act, RE[:, j, :], bank(b), m, free)
                            im = copy_on(act, IM[:, j, :], bank(b + 1), m, free)
                            bank_free[b], bank_free[b + 1] = re, im
                            zr, kr, zi, ki = RE[:, j, 0:256], RE[:, j, 256:512], IM[:, j, 0:256], IM[:, j, 256:512]
                            p1 = v_tt(Y[:, f, 0, :], zr, kr, ALU.mult, im)
                            p2 = v_tt(T0[:, 0, :], zi, ki, ALU.mult, im, y_done[f - 1] if f else None)
                            p3 = v_tt(Y[:, f, 0, :], Y[:, f, 0, :], T0[:, 0, :], ALU.subtract, p1, p2)
                            q1 = v_tt(Y[:, f, 1, :], zr, ki, ALU.mult, im, lane=pool)
                            q2 = v_tt(T0[:, 1, :], zi, kr, ALU.mult, im, y_done[f - 1] if f else None, lane=pool)
                            q3 = v_tt(Y[:, f, 1, :], Y[:, f, 1, :], T0[:, 1, :], ALU.add, q1, q2, lane=pool)
                            y_done[f] = [p3, q3]
                        i0, n_rows, wid = plan["inv_" + nm]
                        b = take(2)
                        for f in range(nt):
                            slot, landed = load("tables", i0 + f, wid)
                            for ct in range(2):
                                for cs in range(2):
                                    m = mm(psum[:, b + ct, 0:L], Y[:, f, cs, ct * P:(ct + 1) * P], ring[:, slot % RING, cs * L:(cs + 1) * L],
                                           f == 0 and cs == 0, f == nt - 1 and cs == 1, landed, y_done[f],
                                           bank_free[b + ct] if f == 0 and cs == 0 else None, signal=ct == 1 and cs == 1)
                            free_slot(slot, m)
                        for ct in range(2):
                            dz = v_ts(Z(ct)[:, lo:hi], Z(ct)[:, lo:hi], vec(f"hd_{l}", ct), None, ALU.mult, None, m)
                            y = v_stt(Z(ct)[:, lo:hi], psum[:, b + ct, 0:L], nrm[:, ct:ct + 1], Z(ct)[:, lo:hi], ALU.mult, ALU.add, dz, nm_ready)
                            bank_free[b + ct] = y
                            v_tt(H[:, 6 + ct, lo:hi], U[:, ct, lo:hi], Z(ct)[:, lo:hi], ALU.mult, y)
                        fence()
                fence()
            mixed.close()

            with ExitStack() as scope:
                VH = sb(scope, f"v_heads_{l}", [P, T2 // P, MH * DH])
                fence()
                sums = all_squares(lambda t: LAT[:, t, :], 3, RG, None)
                q_ready = normed(sums, QL, lambda t: LAT[:, t, :], lambda t: LAT[:, t, :], 3, RG, lambda t, r: vec(f"qn_{l}", t))
                sums = all_squares(lambda t: LAT[:, 3 + t, :], 2, XB, None)
                kv_ready = normed(sums, KVL, lambda t: LAT[:, 3 + t, :], lambda t: LAT[:, 3 + t, :], 2, XB, lambda t, r: vec(f"kvn_{l}", t))
                v_made = []
                slot, landed = load("w_uv", l)
                for t in range(T2 // P):
                    b = take(1)
                    for k in range(2):
                        m = mm(bank(b), LAT[:, 3 + k, t * P:(t + 1) * P], ring[:, slot % RING, k * 512:(k + 1) * 512], k == 0, k == 1,
                               landed, kv_ready[k], bank_free[b] if k == 0 else None, signal=k == 1)
                    m6 = copy(VH[:, t, :], bank(b), m)
                    bank_free[b] = m6
                    v_made.append(m6)
                free_slot(slot, m)
                for g in range(2):
                    half = ExitStack()
                    QH = sb(half, f"q_heads_{l}_{g}", [P, 4, T2])
                    KH = sb(half, f"k_heads_{l}_{g}", [P, 4, T2])
                    fence()
                    rope_k = copy_on(pool, KH[64:96, :, :], KR[64:96, :].unsqueeze(1).broadcast_to([32, 4, T2]))
                    made = [rope_k, v_made]
                    for h in range(4):
                        b = take(len(RG))
                        if h % 2 == 0:
                            slot, landed = load("w_uq", (l, 2 * g + h // 2), 2 * 3 * P)
                        for k in range(3):
                            for r_, (lo, hi) in enumerate(RG):
                                m = mm(psum[:, b + r_, 0:hi - lo], ring[:, slot % RING, ((h % 2) * 3 + k) * P:((h % 2) * 3 + k + 1) * P], LAT[:, k, lo:hi],
                                       k == 0, k == 2, landed, q_ready[k], bank_free[b + r_] if k == 0 else None,
                                       signal=k == 2 and r_ == len(RG) - 1)
                        if h % 2:
                            free_slot(slot, m)
                        m1, m2 = rotated(QH[64:96, h, 0:S], psum[:, b, 0:S], 0, m)
                        m3 = copy_on(act, QH[0:64, h, 0:S], psum[0:64, b, 0:S], m, m2)
                        bank_free[b] = m3
                        made += [m1, m3]
                        if not last_layer:
                            m4 = copy(QH[0:96, h, S:T2], psum[0:96, b + 1, 0:SC], m)
                            bank_free[b + 1] = m4
                            made.append(m4)
                    slot, landed = load("w_uk", (l, g), 512)
                    for mt in range(2):
                        b = take(2)
                        for k in range(2):
                            for r_, (lo, hi) in enumerate(XB):
                                m = mm(psum[:, b + r_, 0:hi - lo], ring[:, slot % RING, (mt * 2 + k) * P:(mt * 2 + k + 1) * P], LAT[:, 3 + k, lo:hi],
                                       k == 0, k == 1, landed, kv_ready[k], bank_free[b + r_] if k == 0 else None, signal=k == 1 and r_ == 1)
                        for j in range(2):
                            m5 = copy_on((dve, act)[j], 
                                KH[0:64, 2 * mt + j, :], bank(b, T2, 2)[64 * j:64 * j + 64, :], m, m5 if j else None)
                            made.append(m5)
                        bank_free[b] = bank_free[b + 1] = made[-2:]
                    free_slot(slot, m)
                    for lane in lanes:
                        lane.wait(made)
                    units = []
                    for h in range(4):
                        units.append((h, [(P * i, T2) for i in range(4)], 0))
                        if not last_layer:
                            units.append((h, [(S + P * i, SC) for i in range(2)], S))
                    attention(half, f"mla{l}_{g}", units, 1.0 / math.sqrt(NOPE + ROPE),
                              lambda h, a, z: QH[0:96, h, a:z], lambda h, a, z: KH[0:96, h, a:z],
                              lambda h, t: VH[:, t, (4 * g + h) * DH:(4 * g + h + 1) * DH], None,
                              lambda h, ps, a, z, mark: copy(H[64 * (h % 2):64 * (h % 2) + 64, 2 * g + h // 2, a:z], ps, mark), T2)
                    fence()
                    half.close()
            layer.close()

            def gate(comp):
                return lambda m, a: MOD[:, l, 0 if a == 0 else 1, comp * 8 + m:comp * 8 + m + 1]
            with ExitStack() as tail:
                HS = sb(tail, f"mix_split_2_{l}", [P, 2, KT, T2], F32R)
                ready = split_mix(HS, H, RG)
                sums = SquareSum(RG)
                x_of = lambda part, k, a, z: HS[:, part, k, a:z]
                for m_ in range(KT):
                    ms = []

                    def add_x(ps, a, z, mark, m_=m_, ms=ms):
                        ms.append(v_stt(X[:, m_, a:z], ps, gate(2)(m_, a), X[:, m_, a:z], ALU.mult, ALU.add, mark))
                        if z == RG[-1][1]:
                            sums.add(X[:, m_, :], ms)
                        return ms[-1]
                    product([("w_out2", (l, m_), KT)], x_of, ready, RG, add_x)
                fence()
                mix2.close()
                h_ready = normed_split(sums, D, HS, RG, lambda t, r: GS[:, l, 1, r, t:t + 1], lambda t, r: MOD[:, l, r, 24 + t:25 + t])
                sums = mlp(f"2_{l}", lambda f: ("w_mlp1", (l, f), KT), lambda g, m: ("w_mlp2", (l, g, m)), HS, RG, h_ready, gate(5), iter(()))
            fence()

        done = normed(sums, D, lambda t: X[:, t, :], lambda t: X[:, t, :], KT, X1, lambda t, r: vec("final2", t))
        stored = sem("stored")
        for t in range(KT):
            m = dma(sp, stored, 16 * (t + 1), out_t[:, t, :], X[:, t, 0:S], done[t])
        sp.wait(m)

        if order is None:
            return used
        with nc.Block() as block:
            @block.tensor
            def _(eng):
                pe.run(eng)

            @block.vector
            def _(eng):
                dve.run(eng)

            @block.scalar
            def _(eng):
                act.run(eng)

            @block.gpsimd
            def _(eng):
                pool.run(eng)

            @block.sync
            def _(eng):
                sp.run(eng)


def tiles(w, cols):
    return slots_of(w[:, cols])


def lay_out(a):
    d = {}
    fm = lambda v: np.ascontiguousarray(v.reshape(-1, P).T)
    cols = lambda m: [slice(i * P, (i + 1) * P) for i in range(m)]
    d["x_t"] = np.ascontiguousarray(a["x"][0].T.reshape(KT, P, S).transpose(1, 0, 2))
    d["ctx_t"] = np.ascontiguousarray(a["ctx_2"][0].T.reshape(KT, P, SC).transpose(1, 0, 2))
    w = a["w_in"][0]
    AQ, AK, AV, BQ, BK, BV, BR, BA, CQ, CK, CV, _ = np.cumsum([0, 384, 384, 384, 128, 128, 256, 256, 16, 384, 384, 384])
    starts = [AQ + P * i for i in range(3)] + [AK + P * i for i in range(3)] + [BQ, BK, BR, BR + P]
    starts += [CQ + P * i for i in range(3)] + [CK + P * i for i in range(3)]
    ba = np.concatenate([w[:, BA:BA + B_RANK], np.zeros((D, P - B_RANK), np.float32)], 1)
    d["w_in1"] = np.stack([tiles(w, slice(s, s + P)) for s in starts] + [slots_of(ba)])
    wv = np.concatenate([w[:, AV:AV + 384], w[:, BV:BV + 256], w[:, CV:CV + 384]], 1)
    d["w_v1"] = np.ascontiguousarray(wv.reshape(4, 2, P, 2, 512).transpose(3, 0, 2, 1, 4).reshape(2, 4, P, 1024))
    d["w_out1"] = np.stack([tiles(a["w_out"][0], c) for c in cols(KT)])

    def ff2(w):
        return np.ascontiguousarray(w.reshape(NGROUP, GROUP, P, KT // 2, 2, P).transpose(0, 3, 2, 4, 1, 5).reshape(NGROUP, KT // 2, P, SLOT))
    d["w_ff1"] = np.stack([tiles(a["w_ff1"][0], c) for c in cols(FT)])
    d["w_ff2"] = ff2(a["w_ff2"][0])
    j = np.arange(ROPE)
    swap = np.where(j % 16 < 8, j + 8, j - 8)
    w2 = a["w_in_2"]
    off_kr, off_f = QL + KVL, QL + KVL + ROPE
    st = [P * i for i in range(5)] + [off_f + P * i for i in range(8)]
    pad = np.zeros((D, 64), np.float32)
    kr = [slots_of(np.concatenate([pad, w2[l][:, off_kr + j], w2[l][:, off_kr + swap]], 1)) for l in range(2)]
    d["w_in2"] = np.stack([np.stack([tiles(w2[l], slice(s, s + P)) for s in st] + [kr[l]]) for l in range(2)])
    uq = a["w_uq_2"]
    head = lambda h: np.concatenate([96 * h + np.arange(64), 96 * h + 64 + j, 96 * h + 64 + swap])
    d["w_uq"] = np.stack([np.stack([np.concatenate([tiles(uq[l], head(2 * p)), tiles(uq[l], head(2 * p + 1))], 1)
                                    for p in range(4)]) for l in range(2)])
    ukv = a["w_ukv_2"]
    nope = lambda p: np.concatenate([128 * (2 * p + i) + np.arange(64) for i in range(2)])
    vals = np.concatenate([128 * h + 64 + np.arange(64) for h in range(MH)])
    d["w_uk"] = np.stack([np.stack([np.concatenate([tiles(ukv[l], nope(p)) for p in (2 * g, 2 * g + 1)], 1)
                                    for g in range(2)]) for l in range(2)])
    d["w_uv"] = np.stack([tiles(ukv[l], vals) for l in range(2)])
    d["w_out2"] = np.stack([np.stack([tiles(a["w_out_2"][l], c) for c in cols(KT)]) for l in range(2)])
    d["w_mlp1"] = np.stack([np.stack([tiles(a["w_mlp1_2"][l], c) for c in cols(FT)]) for l in range(2)])
    d["w_mlp2"] = np.stack([ff2(a["w_mlp2_2"][l]) for l in range(2)])
    d["w_mod"] = np.ascontiguousarray(a["w_mod_2"].transpose(0, 2, 1).reshape(2, 48, P, D))
    d["cond"] = np.stack([a["c_2"][0], a["c_ctx_2"]])
    d["w_a2"] = np.ascontiguousarray(a["gla_w_a2"][0])
    d["rel_bias"] = np.ascontiguousarray(a["rel_bias"])
    d["fw1"] = np.ascontiguousarray(np.concatenate([a["hy_w1_2"][l] for l in range(2)], 1))
    d["fw2"] = np.ascontiguousarray(np.concatenate([a["hy_w2_2"][l] for l in range(2)], 1))
    d["fw3"] = np.ascontiguousarray(np.concatenate([a["hy_w3_2"][l] for l in range(2)], 1))
    v = np.zeros((P, VECS), np.float32)

    def put(name, x):
        at, n = VEC[name]
        v[0:x.shape[0], at:at + n] = x
    put("norm1", fm(a["norm1_w"][0])); put("norm2", fm(a["norm2_w"][0])); put("final1", fm(a["final_norm_w"]))
    put("gla_norm", fm(a["gla_norm_w"][0])); put("gla_b", fm(a["gla_b_a"][0])); put("final2", fm(a["final_norm_g_2"]))
    for l in range(2):
        put(f"n1_{l}", fm(a["norm1_g_2"][l])); put(f"n2_{l}", fm(a["norm2_g_2"][l]))
        put(f"qn_{l}", fm(a["q_norm_g_2"][l])); put(f"kvn_{l}", fm(a["kv_norm_g_2"][l]))
        put(f"bmod_{l}", fm(a["b_mod_2"][l])); put(f"cw_{l}", fm(a["hy_conv_w_2"][l].reshape(-1)))
        put(f"cb_{l}", fm(a["hy_conv_b_2"][l])); put(f"hd_{l}", fm(a["hy_d_2"][l]))
        put(f"fb1_{l}", a["hy_b1_2"][l][:, None]); put(f"ffr_{l}", a["hy_freq_2"][l][:, None])
        put(f"fb2_{l}", a["hy_b2_2"][l][:, None])
    d["vecs"] = v
    for n, t in shape_constants().items():
        d["c_" + n] = t
    d["tables"], at = sequence_tables()
    return d, at


def kernel(**inputs):
    import concourse.bacc as bacc
    from concourse.bass_utils import run_bass_kernel_spmd as run

    arrays, at = lay_out({k: np.asarray(v) for k, v in inputs.items()})
    def blank():
        nc = bacc.Bacc("TRN2", target_bir_lowering=False, num_devices=1)
        dr = {n: nc.dram_tensor("in_" + n, a.shape, F32, kind="ExternalInput").ap() for n, a in arrays.items()}
        return nc, dr, nc.dram_tensor("out_t", (P, KT, S), F32, kind="ExternalOutput").ap()

    order = build(*blank(), at, None)
    nc, dr, out_t = blank()
    build(nc, dr, out_t, at, order)
    r = run(nc, [{"in_" + n: np.ascontiguousarray(a) for n, a in arrays.items()}], core_ids=[0])
    o = np.asarray(r.results[0]["out_t"])
    return np.ascontiguousarray(o.transpose(1, 0, 2).reshape(D, S).T)[None]
```

```python
import math
from contextlib import ExitStack

import numpy as np

import concourse.bass as bass
from concourse import mybir

F32 = mybir.dt.float32
F32R = mybir.dt.float32r
ALU = mybir.AluOpType
ACT = mybir.ActivationFunctionType
AX = mybir.AxisListType

P = 128
D = 1024
KT = D // P
S = 512
SC = 256
T2 = S + SC
DH = 64
EPS = 1e-6
A_HEADS = 6
B_HEADS, B_DK, B_DV, B_RANK, B_CHUNK, B_TAU = 4, 32, 64, 16, 16, 16.0
C_HEADS = 6
NCHUNK = S // B_CHUNK
REL_BUCKETS, REL_MAX = 32, 2048
F = 4 * D
FT = F // P
MH = 8
NOPE, ROPE = 64, 32
QL, KVL = 384, 256
HY = 256
SLOT = 1024
RING = 5
SPLIT_RING = 4
AHEAD = 2
GROUP = 4
NGROUP = 32 // GROUP
MOD_FIRST = 28
NEG = -1e30
STRIP = 640


def rel_bucket(n):
    n = np.maximum(n, 0)
    exact = REL_BUCKETS // 2
    logv = (np.log(np.maximum(n, 1).astype(np.float32) / exact) / np.float32(math.log(REL_MAX / exact)))
    large = np.minimum(exact + (logv * (REL_BUCKETS - exact)).astype(np.int32), REL_BUCKETS - 1)
    return np.where(n < exact, n, large)


def shape_constants():
    f64 = np.float64
    c = {}
    c["ident"] = np.eye(P)
    c["flip"] = np.eye(P)[::-1]
    c["ones"] = np.ones((P, P))
    two = (np.arange(P)[:, None] // 32 % 2) == (np.arange(P)[None, :] // 64)
    c["spread"] = two.astype(f64)
    c["mean64"] = (np.arange(P)[:, None] // 64 == np.arange(P)[None, :] // 64) / 64.0
    c["in_chunk"] = (np.arange(P)[:, None] // B_CHUNK == np.arange(P // B_CHUNK)[None, :]).astype(f64)
    c["not_first"] = np.tile((np.arange(S) % B_CHUNK != 0).astype(f64), (P, 1))
    dist = S - 1 - np.arange(STRIP)
    c["bucket_of"] = np.zeros((P, STRIP))
    c["bucket_of"][:REL_BUCKETS] = np.arange(REL_BUCKETS)[:, None] == rel_bucket(dist)[None, :]
    times = (dist <= 128) * 1.0 + (dist % 4 == 0) + (dist % 16 == 0)
    log_a = np.where((dist >= 0) & (times > 0), np.log(np.maximum(times, 1)), NEG)
    c["log_reach"] = np.zeros((P, STRIP))
    c["log_reach"][:A_HEADS] = log_a
    c["log_reach"][A_HEADS:A_HEADS + C_HEADS] = np.where(dist >= 0, 0.0, NEG)
    inv = (np.float32(10000.0) ** (-np.arange(0, 16, 2, dtype=np.float32) / 16)).astype(np.float32)
    tok = np.arange(S)
    ang = np.concatenate([(tok // 64).astype(np.float32)[:, None] * inv, (tok % 64).astype(np.float32)[:, None] * inv], 1)
    j = np.arange(ROPE)
    which = j // 16 * 8 + j % 8
    c["rope"] = np.zeros((P, S))
    c["rope"][64:96] = np.cos(ang)[:, which].T
    c["rope"][96:128] = (np.sin(ang)[:, which] * np.where(j % 16 < 8, -1.0, 1.0)).T
    g = np.arange(P)
    same = g[:, None] // 64 == g[None, :] // 64
    a = 2 * np.pi * ((g[:, None] % 64) * (g[None, :] % 64) % 64) / 64
    c["dft64"] = np.concatenate([np.cos(a) * same, np.sin(a) * same], 1)
    return {k: v.astype(np.float32) for k, v in c.items()}


CONSTS = ["ident", "flip", "ones", "spread", "mean64", "in_chunk", "not_first", "bucket_of", "log_reach", "rope", "dft64"]
CONST_W = {"ident": P, "flip": P, "ones": P, "spread": P, "mean64": P, "in_chunk": P // B_CHUNK, "not_first": S,
           "bucket_of": STRIP, "log_reach": STRIP, "rope": S, "dft64": 2 * P}


def slots_of(table):
    k, m = table.shape
    return np.ascontiguousarray(table.reshape(k // P, P, m).transpose(1, 0, 2).reshape(P, -1))


def sequence_tables():
    out = {}
    for L, name in ((S, "x"), (SC, "c")):
        t = np.arange(L)
        a = 2 * np.pi * (t[:, None] * t[None, :] % L) / L
        n = 1.0 / math.sqrt(L * 64)
        rows = [np.concatenate([np.cos(a[i:i + P]) * n, -np.sin(a[i:i + P]) * n], 1) for i in range(0, L, P)]
        out["fourier_" + name] = rows
        w = 2 * np.pi * (t[:, None] * (2 * t[None, :] + 1) % (4 * L)) / (4 * L)
        out["fwd_" + name] = [np.concatenate([slots_of(np.cos(w[:, i:i + P])), slots_of(-np.sin(w[:, i:i + P]))], 1)
                              for i in range(0, L, P)]
        out["inv_" + name] = [np.concatenate([np.cos(w.T[i:i + P]) / L, -np.sin(w.T[i:i + P]) / L], 1)
                              for i in range(0, L, P)]
        pos = np.linspace(0.0, 1.0, L, dtype=np.float32)[:, None]
        fr = np.linspace(1e-4, 15, 16, dtype=np.float32)
        ang = (np.float32(2.0 * math.pi) * t.astype(np.float32)[:, None] / np.float32(L) * fr).astype(np.float32)
        z = np.concatenate([pos, np.cos(ang), -np.sin(ang)], 1)
        lo, hi = math.log(1e-2) / 1.5, math.log(1e-2) / 0.3
        deltas = np.abs(np.linspace(lo, hi, HY, dtype=np.float32))
        decay = np.exp(-pos * deltas)
        decay = np.concatenate([decay, decay], 1)
        decay[0, HY:] = 0.0
        decay = slots_of(decay)
        zt = np.zeros((P, L))
        zt[:33] = z.T
        out["emb_" + name] = [zt]
        out["decay_" + name] = [decay[:, i:i + SLOT] for i in range(0, decay.shape[1], SLOT)]
    flat, at = [], {}
    for k, rows in out.items():
        at[k] = (len(flat), len(rows), rows[0].shape[1])
        for r in rows:
            full = np.zeros((P, SLOT), np.float32)
            full[:, :r.shape[1]] = r
            flat.append(full)
    return np.stack(flat), at


def vec_plan():
    plan, at = {}, 0
    for name, n in [("norm1", 8), ("norm2", 8), ("final1", 8), ("gla_norm", 2), ("gla_b", 1), ("final2", 8)] + [
            (f"{name}{l}", n) for l in range(2) for name, n in (
                ("n1_", 8), ("n2_", 8), ("qn_", 3), ("kvn_", 2), ("bmod_", 48), ("cw_", 18), ("cb_", 6), ("hd_", 2),
                ("fb1_", 1), ("ffr_", 1), ("fb2_", 1))]:
        plan[name] = (at, n)
        at += n
    return plan, at


VEC, VECS = vec_plan()


class Lane:

    def __init__(self, sem):
        self.sem, self.count, self.queue, self.seen = sem, 0, [], {}

    def wait(self, *after):
        for mark in marks(after):
            sem, value = mark
            if self.seen.get(id(sem), 0) < value:
                self.seen[id(sem)] = value
                self.queue.append(lambda eng, sem=sem, value=value: eng.wait_ge(sem, value))

    def issue(self, instruction, *after, signal=True):
        self.wait(*after)
        if signal:
            self.count += 1
            self.queue.append(lambda eng: instruction(eng).then_inc(self.sem, 1))
        else:
            self.queue.append(instruction)
        return (self.sem, self.count)

    def dma(self, sem, total, instruction, *after):
        self.wait(*after)
        self.queue.append(lambda eng: instruction(eng).then_inc(sem, 16))
        return (sem, total)

    def now(self):
        return (self.sem, self.count) if self.count else None

    def run(self, eng):
        for instruction in self.queue:
            instruction(eng)


def marks(x):
    if x is None:
        return
    if isinstance(x, tuple) and len(x) == 2 and isinstance(x[1], int):
        yield x
        return
    for y in x:
        yield from marks(y)


def build(nc, dr, out_t, at, order):
    plan = at
    with ExitStack() as top:
        def sem(name):
            return top.enter_context(nc.semaphore(name))

        pe, dve, act, pool, sp = (Lane(sem(n)) for n in ("pe_step", "dve_step", "act_step", "pool_step", "sp_step"))
        lanes = [pe, dve, act, pool]

        holes = [[nc.sbuf_base + 31 & ~31, nc.sbuf_usable_end & ~31, []]]

        def sb(scope, name, shape, dtype=F32, high=False):
            size = 4 * int(np.prod(shape[1:])) + 31 & ~31
            got = next((h for h in (holes[::-1] if high else holes) if h[1] - h[0] >= size), None)
            if got is None:
                raise MemoryError(f"{name} {size}: {[(h[0], h[1] - h[0]) for h in holes]}")
            at, since = got[1] - size if high else got[0], got[2]
            got[0 if not high else 1] += -size if high else size
            if got[0] == got[1]:
                holes.remove(got)
            for lane in lanes:
                lane.wait(since)
            scope.callback(give_back, at, size)
            return nc.alloc_sbuf_tensor_at(name, shape, dtype, offset=at)

        def give_back(at, size):
            now = [lane.now() for lane in lanes]
            holes.append([at, at + size, now])
            holes.sort(key=lambda h: h[0])
            i = 0
            while i + 1 < len(holes):
                a, b = holes[i], holes[i + 1]
                if a[1] == b[0]:
                    latest = {}
                    for m_sem, value in marks([a[2], b[2]]):
                        old = latest.get(id(m_sem))
                        latest[id(m_sem)] = (m_sem, max(value, old[1] if old else 0))
                    holes[i:i + 2] = [[a[0], b[1], list(latest.values())]]
                else:
                    i += 1

        def fence():
            all_now = [lane.now() for lane in lanes]
            for lane in lanes:
                lane.wait(all_now)

        ring = sb(top, "weight_ring", [P, RING, SLOT])
        WS = sb(top, "weight_split", [P, SPLIT_RING, 2, SLOT], F32R)
        SQ = sb(top, "squares", [P, 2, T2])
        SQF = sb(top, "shifted", [P, T2])
        X = sb(top, "residual", [P, KT, T2])
        C = {n: sb(top, "c_" + n, [P, CONST_W[n]]) for n in CONSTS if n not in ("bucket_of", "log_reach", "flip")}
        vecs = sb(top, "vecs", [P, VECS])
        MOD = sb(top, "modulation", [P, 2, 2, 48])
        GS = sb(top, "gain_scale", [P, 2, 2, 2, KT])
        gain_12 = sb(top, "gain_of_both_norms", [P, KT])
        rs = sb(top, "row_stats", [P, 12])
        psum = top.enter_context(nc.psum_tensor("psum", [P, 8, 512], F32))

        def vec(name, i=0, rows=P):
            return vecs[0:rows, VEC[name][0] + i:VEC[name][0] + i + 1]

        ring_sem = [sem(f"ring_{i}") for i in range(RING)]
        ring_free = {}
        used = []
        queued = [0]
        landed_at = {}
        split_free = [None] * SPLIT_RING
        split_mark, split_of = {}, {}
        n_split, n_split_used = [0], [0]

        def queue_loads(upto):
            while queued[0] <= upto and queued[0] < len(used if order is None else order):
                i = queued[0]
                if i >= RING and i - RING not in ring_free:
                    break
                name, index, width, _ = (used if order is None else order)[i]
                src = dr[name][index] if width == SLOT else dr[name][index][:, 0:width]
                landed_at[i] = dma(sp, ring_sem[i % RING], 16 * (i // RING + 1), ring[:, i % RING, 0:width], src,
                                   ring_free.get(i - RING))
                queued[0] += 1

        def load(name, index, width=SLOT, split=False):
            i = len(used)
            used.append((name, index, width, split))
            if order is not None:
                assert order[i] == used[i]
            queue_loads(i + RING - 1)
            return i, landed_at[i]

        def free_slot(i, mark):
            ring_free[i] = mark

        def split_ahead(upto):
            while n_split[0] <= upto and n_split[0] < len(used if order is None else order):
                i = n_split[0]
                name, index, width, split = order[i] if order is not None else used[i]
                if split:
                    if order is not None:
                        queue_loads(i)
                    if i not in landed_at:
                        break
                    j = n_split_used[0]
                    k = j % SPLIT_RING
                    src = ring[:, i % RING, 0:width]
                    hi = act.issue(lambda eng, k=k, src=src, width=width: eng.copy(WS[:, k, 0, 0:width], src),
                                   landed_at[i], split_free[k])
                    lo = v_tt(WS[:, k, 1, 0:width], src, WS[:, k, 0, 0:width].bitcast(F32), ALU.subtract, hi, split_free[k],
                              lane=pool if j % 3 == 2 else dve)
                    ring_free[i] = lo
                    split_mark[i], split_of[i] = lo, k
                    n_split_used[0] += 1
                n_split[0] += 1

        def split_next_two():
            if order is not None:
                split_ahead(len(used) + 1)

        def load_split(name, index, width=SLOT):
            i, _ = load(name, index, width, True)
            split_ahead(i + AHEAD if order is not None else i)
            return split_of[i], split_mark[i]

        bank_free = [None] * 8
        next_bank = {"pair": 0, "one": 0, "turn": 0}
        PAIRS, ONES, TURN = [0, 2, 4, 6], [0, 1, 2, 3, 4, 5, 6, 7], [4, 5, 6, 7]

        def take(n=1, pool_=None):
            kind, banks = (pool_, {"turn": TURN, "logits": [0, 2], "row": [0, 1, 2, 3]}[pool_]) if pool_ else ("pair", PAIRS) if n == 2 else ("one", ONES)
            b = banks[next_bank.get(kind, 0) % len(banks)]
            next_bank[kind] = next_bank.get(kind, 0) + 1
            if pool_ is None:
                next_bank["one" if n == 2 else "pair"] = (b + n) % 8 if n == 2 else (b // 2 + 1) % 4
            return b

        def bank(b, w=512, n=1):
            if n == 1:
                return psum[:, b, 0:w]
            return psum[:, b:b + 2, :].rearrange("p b w -> p (b w)")[:, 0:w]

        def mm(out, lhsT, rhs, start, stop, *after, signal=False):
            return pe.issue(lambda eng: eng.matmul(out, lhsT, rhs, start=start, stop=stop), *after, signal=signal)

        side = [0]

        def copy(out, in_, *after):
            side[0] += 1
            if side[0] % 2:
                return act.issue(lambda eng: eng.copy(out, in_), *after)
            return dve.issue(lambda eng: eng.tensor_copy(out, in_), *after)

        def v_tt(out, a, b, op, *after, lane=None):
            return (lane or dve).issue(lambda eng: eng.tensor_tensor(out, a, b, op), *after)

        def v_ts(out, a, s1, s2, op0, op1, *after, lane=None):
            if s2 is None:
                return (lane or dve).issue(lambda eng: eng.tensor_scalar(out, a, s1, None, op0), *after)
            return (lane or dve).issue(lambda eng: eng.tensor_scalar(out, a, s1, s2, op0, op1), *after)

        def v_stt(out, a, s, b, op0, op1, *after):
            return dve.issue(lambda eng: eng.scalar_tensor_tensor(out=out, in0=a, scalar=s, in1=b, op0=op0, op1=op1), *after)

        def fn(out, in_, f, *after, **kw):
            return act.issue(lambda eng: eng.activation(out, in_, f, **kw), *after)

        def zero(lane, out, *after, value=0.0):
            return lane.issue(lambda eng: eng.memset(out, value), *after)

        def recip(out, in_, *after):
            return dve.issue(lambda eng: eng.reciprocal(out, in_), *after)

        def neg_rowmax(out, in_, *after):
            return dve.issue(lambda eng: eng.tensor_reduce(out, in_, AX.X, ALU.max, negate=True), *after)

        def turn(out, in_, *after, signal=True):
            return pe.issue(lambda eng: eng.transpose(out, in_, C["ident"][:, :]), *after, signal=signal)

        def copy_on(lane, out, in_, *after):
            if lane is act:
                return act.issue(lambda eng: eng.copy(out, in_), *after)
            return lane.issue(lambda eng: eng.tensor_copy(out, in_), *after)

        def scan(out, decay, add, *after):
            return dve.issue(lambda eng: eng.tensor_tensor_scan(out, decay, add, 0.0, ALU.mult, ALU.add), *after)

        def dot(scratch, a, b, out, *after):
            return dve.issue(lambda eng: eng.tensor_tensor_reduce(out=scratch, in0=a, in1=b, scale=1.0, scalar=0.0,
                                                                  op0=ALU.mult, op1=ALU.add, accum_out=out), *after)

        def dma(lane, sem_, total, dst, src, *after):
            return lane.dma(sem_, total, lambda eng: eng.dma_start(dst, src), *after)

        X1, XB = [(0, S)], [(0, S), (S, T2)]

        got = {name: [sem("inputs_" + name), 0] for name in ("first", "rest", "strips", "context")}

        def fetch(dst, src, group="rest"):
            got[group][1] += 16
            return dma(act, got[group][0], got[group][1], dst, src)

        x_sem = [sem(f"x_{i}") for i in range(4)]
        x_landed = [dma(sp, x_sem[i], 16, X[:, 2 * i:2 * i + 2, 0:S], dr["x_t"][:, 2 * i:2 * i + 2, :]) for i in range(4)]
        for n in ("ident", "ones"):
            fetch(C[n][:, :], dr["c_" + n], "first")
        first_loaded = fetch(vecs[:, :], dr["vecs"], "first")
        small = {}
        for name, rows, cols in (("rel_bias", REL_BUCKETS, A_HEADS + C_HEADS), ("w_a2", B_RANK, P),
                                 ("fw1", 33, 128), ("fw2", 64, 128), ("fw3", 64, 1024)):
            small[name] = sb(top, "s_" + name, [P, cols])
            fetch(small[name][0:rows, :], dr[name])
        for n in C:
            if n not in ("ident", "ones"):
                loaded = fetch(C[n][:, :], dr["c_" + n])
        for lane in lanes:
            lane.wait(first_loaded)

        class SquareSum:

            def __init__(self, ranges, buf=None, spare=None):
                self.lo, self.hi, self.n, self.mark = ranges[0][0], ranges[-1][1], 0, None
                self.buf = SQ if buf is None else buf
                self.since = [lane.now() for lane in lanes]
                self.tmp = [self.buf[:, 1, :]] + ([] if spare is None else [spare])
                self.tmp_read = [None] * len(self.tmp)

            def add(self, src, ready, gain=1.0):
                a, z, buf = self.lo, self.hi, self.buf
                if self.n == 0:
                    self.mark = fn(buf[:, 0, a:z], src[:, a:z], ACT.Square, ready, self.since, scale=gain)
                else:
                    j = self.n % len(self.tmp)
                    m = fn(self.tmp[j][:, a:z], src[:, a:z], ACT.Square, ready, self.tmp_read[j], self.since, scale=gain)
                    self.mark = v_tt(buf[:, 0, a:z], buf[:, 0, a:z], self.tmp[j][:, a:z], ALU.add, m, self.mark)
                    self.tmp_read[j] = self.mark
                self.n += 1

        def column_sums(sums):
            b, c = take(1), 0
            for s_ in sums:
                nt = (s_.hi - s_.lo) // P
                for t in range(nt):
                    m = mm(psum[:, b, c:c + 1], s_.buf[:, 0, s_.lo + t * P:s_.lo + (t + 1) * P], C["ones"][:, 0:1], True, True,
                           s_.mark, bank_free[b], signal=s_ is sums[-1] and t == nt - 1)
                    c += 1
            return b, m, c

        def inverse_root(out, mean_eps):
            return recip(out, out, fn(out, out, ACT.Sqrt, mean_eps))

        def on_all_partitions(out, values, diagonal, *after):
            nt = values.shape[1]
            m = v_tt(diagonal.rearrange("p (t q) -> p t q", q=P), C["ident"][:, :].unsqueeze(1).broadcast_to([P, nt, P]),
                     values.unsqueeze(2).broadcast_to([P, nt, P]), ALU.mult, *after)
            for a in range(0, nt * P, 512):
                z = min(a + 512, nt * P)
                m = mm(out[:, a:z], C["ones"][:, :], diagonal[:, a:z], True, True, m, signal=True)
            return m

        def inverse_narrow(sums, n):
            b, m, nt = column_sums([sums])
            m = v_ts(rs[:, 0:nt], psum[:, b, 0:nt], 1.0 / n, EPS, ALU.mult, ALU.add, m)
            bank_free[b] = m
            return nt, inverse_root(rs[:, 0:nt], m)

        def inverse_spread(nt, m):
            b = take(2)
            return b, on_all_partitions(bank(b, nt * P, 2), rs[:, 0:nt], SQ[:, 1, 0:nt * P], m, bank_free[b], bank_free[b + 1])

        def inverse(sums, n):
            return inverse_spread(*inverse_narrow(sums, n))

        def all_squares(src, nt, ranges, ready):
            sums = SquareSum(ranges, spare=SQF)
            for t in range(nt):
                sums.add(src(t), ready[t] if isinstance(ready, list) else ready)
            return sums

        def normed(spread, src, dst, nt, ranges, gain):
            b, ready = spread
            out = []
            for t in range(nt):
                ms = []
                for r, (a, z) in enumerate(ranges):
                    ms.append(v_stt(dst(t)[:, a:z], src(t)[:, a:z], gain(t, r), bank(b + r, z - a), ALU.mult, ALU.mult, ready))
                out.append(ms)
            bank_free[b] = bank_free[b + 1] = ms
            return out

        def normed_split(spread, HS, ranges, gain, shift=None):
            b, ready = spread
            out, tmp_made, split = [], {}, {}
            last = [None, None]
            full = SQF[:, :]
            full_read = None

            def scaled(t):
                tmp_made[t] = [v_stt(SQ[:, t % 2, a:z], X[:, t, a:z], gain(t, r), bank(b + r, z - a), ALU.mult, ALU.mult, ready, last[t % 2])
                               for r, (a, z) in enumerate(ranges)]
            scaled(0)
            for t in range(KT):
                if t + 1 < KT:
                    scaled(t + 1)
                ms = []
                for r, (a, z) in enumerate(ranges):
                    m = tmp_made[t][r]
                    tmp, hi, lo = SQ[:, t % 2, a:z], HS[:, 0, t, a:z], HS[:, 1, t, a:z]
                    if shift is None:
                        m = copy_on(act, hi, tmp, m)
                        m = v_tt(lo, tmp, hi.bitcast(F32), ALU.subtract, m, lane=pool if t % 2 else dve)
                    elif t % 2:
                        h = fn(hi, tmp, ACT.Identity, m, bias=shift(t, r), scale=1.0)
                        m = fn(full[:, a:z], tmp, ACT.Identity, m, full_read, bias=shift(t, r), scale=1.0)
                        m = v_tt(lo, full[:, a:z], hi.bitcast(F32), ALU.subtract, m, h, lane=pool)
                    else:
                        m = fn(hi, tmp, ACT.Identity, m, bias=shift(t, r), scale=1.0)
                        m = v_stt(lo, tmp, shift(t, r), hi.bitcast(F32), ALU.add, ALU.subtract, m)
                    ms.append(m)
                last[t % 2] = ms
                if t % 2:
                    full_read = ms
                out.append(ms)
            bank_free[b] = bank_free[b + 1] = tmp_made[KT - 1]
            return out

        def split_mix(HS, MIX, ranges):
            lo, hi = ranges[0][0], ranges[-1][1]
            out = []
            for t in range(KT):
                m = copy_on(act, HS[:, 0, t, lo:hi], MIX[:, t, lo:hi])
                out.append(v_tt(HS[:, 1, t, lo:hi], MIX[:, t, lo:hi], HS[:, 0, t, lo:hi].bitcast(F32), ALU.subtract, m,
                                lane=pool if t % 2 else dve))
            return out

        def products(b, ranges, w_hi, w_lo, x, k, n, ready, signal):
            for w, part in ((w_hi, 0), (w_hi, 1), (w_lo, 0)):
                for r, (lo, hi) in enumerate(ranges):
                    m = mm(psum[:, b + r, 0:hi - lo], w, x(part, k, lo, hi), k == 0 and w is w_hi and part == 0,
                           k == n - 1 and w is w_lo, ready, bank_free[b + r] if k == 0 and w is w_hi and part == 0 else None,
                           signal=signal and w is w_lo and r == len(ranges) - 1)
            return m

        def product(weights, x, x_ready, ranges, take_outs):
            bs = [take(2) for _ in weights]
            slots = [load_split(*w) for w in weights]
            for k in range(KT):
                for i, (b, (slot, ready)) in enumerate(zip(bs, slots)):
                    last = products(b, ranges, WS[:, slot, 0, k * P:(k + 1) * P], WS[:, slot, 1, k * P:(k + 1) * P], x, k, KT,
                                    [ready, x_ready[k] if isinstance(x_ready, list) else x_ready], k == KT - 1)
                    if k == KT - 1:
                        split_free[slot] = last
                        for r, (lo, hi) in enumerate(ranges):
                            bank_free[b + r] = take_outs[i](psum[:, b + r, 0:hi - lo], lo, hi, last)

        def mlp(layer, w1, w2, HS, ranges, x_ready, gate, work, gained=None):
            with ExitStack() as scope:
                width = ranges[-1][1]
                G = sb(scope, f"hidden_{layer}", [P, 2, 2 * GROUP, width], F32R)
                act_tmp = sb(scope, f"hidden_tmp_{layer}", [P, 2, width])
                g_ready, g_read, tmp_read = {}, [None] * (2 * GROUP), [None, None]
                sums = SquareSum(ranges)
                x_of = lambda part, k, a, z: HS[:, part, k, a:z]
                lo, hi = ranges[0][0], ranges[-1][1]

                def up(*fs):
                    def relu_of(f):
                        k, j = f % (2 * GROUP), f % 2
                        before, ms = tmp_read[j], []
                        g_ready[f] = tmp_read[j] = ms

                        def relu(ps, a, z, mark):
                            r = act_tmp[:, j, a:z]
                            got_it = fn(r, ps, ACT.Relu, mark, before)
                            h = fn(G[:, 0, k, a:z], r, ACT.Square, got_it, g_read[k])
                            sq = v_tt(r, r, r, ALU.mult, h, lane=pool)
                            ms.append(v_tt(G[:, 1, k, a:z], r, G[:, 0, k, a:z].bitcast(F32), ALU.subtract, sq, g_read[k]))
                            return got_it
                        return relu
                    product([w1(f) for f in fs], x_of, x_ready, ranges, [relu_of(f) for f in fs])
                    for _ in fs:
                        next(work, None)

                def down(g):
                    for m in range(0, KT, 2):
                        slot, ready = load_split(*w2(g, m // 2))
                        for i in range(2):
                            b = take(2)
                            for j in range(GROUP):
                                f = g * GROUP + j
                                k = f % (2 * GROUP)
                                w = WS[:, slot, :, (i * GROUP + j) * P:(i * GROUP + j + 1) * P]
                                last = products(b, ranges, w[:, 0, :], w[:, 1, :], lambda part, _, a, z, k=k: G[:, part, k, a:z], j, GROUP,
                                                [ready, g_ready[f]], j == GROUP - 1)
                            ms = []
                            for r, (a, z) in enumerate(ranges):
                                x, ps = X[:, m + i, a:z], psum[:, b + r, 0:z - a]
                                if gate is None:
                                    bank_free[b + r] = v_tt(x, ps, x, ALU.add, last)
                                else:
                                    bank_free[b + r] = v_stt(x, ps, gate(m + i, a), x, ALU.mult, ALU.add, last)
                                ms.append(bank_free[b + r])
                            if g == NGROUP - 1:
                                sums.add(X[:, m + i, :], ms)
                                if gained is not None:
                                    gained[0].add(X[:, m + i, :], ms, gained[1](m + i))
                        split_free[slot] = last
                        next(work, None)
                        if m % 4 == 0:
                            next(work, None)
                    for j in range(GROUP):
                        g_read[(g * GROUP + j) % (2 * GROUP)] = last

                for g in range(NGROUP + 1):
                    if g < NGROUP:
                        if g == 0:
                            up(0, 1)
                        for j in range(2 if g == 0 else 0, GROUP):
                            up(g * GROUP + j)
                    if g > 0:
                        down(g - 1)
                for _ in work:
                    pass
            return sums

        def attention(scope, tag, units, scale, q_of, k_of, v_of, strip_of, put, kmax, work=iter(()), strips=None, heads=None):
            one = kmax <= 512
            AHEAD_L, AHEAD_E = (5, 3) if one else (3, 2)
            NP, NPT = AHEAD_E + 1, 2
            Pb = sb(scope, tag + "_prob", [P, NP, kmax])
            PT = sb(scope, tag + "_probT", [P, NPT, kmax // P, S])
            st = sb(scope, tag + "_stat", [P, NP, 4])
            items = [(u, i) for u, unit in enumerate(units) for i in range(len(unit[1]))]
            info = [dict() for _ in items]
            pt_read = [None] * NPT
            pt_done = {}

            def logits(n):
                u, i = items[n]
                head, qs, k0 = units[u]
                q0, w = qs[i]
                if heads is not None:
                    heads[0](head, k0 == 0 and i == 0)
                nb = 1 if w <= 512 else 2
                b = take(1, "row") if one else take(2, "logits")
                for off in range(0, w, 512):
                    pw = min(512, w - off)
                    m = mm(psum[:, b + off // 512, 0:pw], q_of(head, q0, q0 + P), k_of(head, k0 + off, k0 + off + pw),
                           True, True, bank_free[b + off // 512], heads[1][head] if heads else None, signal=off + 512 >= w)
                if heads is not None:
                    heads[2][head] = m
                info[n].update(bank=b, nb=nb, w=w, head=head, q0=q0, logits=m)

            def exps(n):
                d = info[n]
                w, j = d["w"], n % NP
                s = bank(d["bank"], w, d["nb"])
                free = info[n - NP]["pt"] if n >= NP else None
                if strip_of is not None:
                    m = v_stt(Pb[:, j, 0:w], s, scale, strip_of(d["head"], d["q0"], w), ALU.mult, ALU.add, d["logits"], free,
                              strips[0][d["head"]])
                    if items[n][1] == 3:
                        strips[1][d["head"]] = m
                        if d["head"] + 2 < 6:
                            strips[2](d["head"] + 2)
                    bank_free[d["bank"]] = m
                    m = neg_rowmax(st[:, j, 0:1], Pb[:, j, 0:w], m)
                    m = fn(Pb[:, j, 0:w], Pb[:, j, 0:w], ACT.Exp, m, bias=st[:, j, 0:1], scale=1.0, accum_out=st[:, j, 1:2])
                else:
                    m = neg_rowmax(st[:, j, 0:1], s, d["logits"], free)
                    m = fn(Pb[:, j, 0:w], s, ACT.Exp, m, free, bias=st[:, j, 0:1], scale=1.0, accum_out=st[:, j, 1:2])
                    for r in range(d["nb"]):
                        bank_free[d["bank"] + r] = m
                d["exp"] = m

            def diag(n):
                d = info[n]
                j = n % NP
                m = recip(st[:, j, 3:4], st[:, j, 1:2], d["exp"])
                d["prob"] = fn(Pb[:, j, 0:d["w"]], Pb[:, j, 0:d["w"]], ACT.Identity, m, scale=st[:, j, 3:4])

            def turn_p(n):
                u, i = items[n]
                d = info[n]
                j = n % NP
                nk = d["w"] // P
                col = d["q0"] - units[u][1][0][0]
                last = None
                for g in range(0, nk, 4):
                    b = take(1, "turn")
                    gn = min(4, nk - g)
                    for t in range(gn):
                        last = turn(psum[:, b, t * P:(t + 1) * P], Pb[:, j, (g + t) * P:(g + t + 1) * P],
                                    d["prob"], bank_free[b] if t == 0 else None, signal=t == gn - 1)
                    m = copy(PT[:, u % NPT, g:g + gn, col:col + P], psum[:, b, 0:gn * P].rearrange("p (t q) -> p t q", q=P),
                             last, pt_read[u % NPT] if i == 0 else None)
                    bank_free[b] = m
                    pt_done.setdefault(u, []).append(m)
                d["pt"] = last
                if waiting[0] is not None:
                    values(waiting[0])
                    waiting[0] = None
                if i == len(units[u][1]) - 1:
                    waiting[0] = u

            def values(u):
                head, qs, k0 = units[u]
                b = take(1, "turn")
                wq = P * len(qs)
                nk = max(w for _, w in qs) // P
                r0 = 64 * (head % 2)
                for t in range(nk):
                    first = next(i for i, (_, w) in enumerate(qs) if w > t * P) * P
                    m = mm(psum[r0:r0 + DH, b, first:wq], v_of(head, k0 // P + t), PT[:, u % NPT, t, first:wq],
                           t == 0, t == nk - 1, pt_done[u], bank_free[b] if t == 0 else None, signal=t == nk - 1)
                pt_read[u % NPT] = m
                bank_free[b] = put(head, psum[r0:r0 + DH, b, 0:wq], qs[0][0], qs[0][0] + wq, m)

            waiting = [None]
            for n in range(-AHEAD_L, len(items)):
                if 0 <= n + AHEAD_L < len(items):
                    logits(n + AHEAD_L)
                if 0 <= n + AHEAD_E < len(items):
                    exps(n + AHEAD_E)
                if 0 <= n + 1 < len(items):
                    diag(n + 1)
                if n >= 0:
                    turn_p(n)
                next(work, None)
            values(waiting[0])
            for _ in work:
                pass

        mod_sem = [sem("mod_ring_0"), sem("mod_ring_1")]
        mod_cond = sem("mod_cond")
        ready_mod = {}

        cond_of = lambda v: X[:, 4 * v:4 * v + 4, S:T2]
        mod_conditions = [0]
        mod_loads = [0]

        def modulation(scope, tag, tiles_of):
            junk = sb(scope, "mod_scratch" + tag, [P, 4, D // 4])
            mod_ring = sb(scope, "mod_ring" + tag, [P, 2, 4, D // 4])
            cond = None
            if mod_conditions[0] == 0:
                for v in range(2):
                    mod_conditions[0] += 16
                    m = dma(pool, mod_cond, mod_conditions[0], cond_of(v),
                            dr["cond"][v:v + 1, :].broadcast_to([P, D]).rearrange("p (t c) -> p t c", t=4))
                yield
                for v in range(2):
                    m = fn(junk[:, :, :], cond_of(v), ACT.Exp, m, cond, scale=-1.0)
                    m = fn(junk[:, :, :], junk[:, :, :], ACT.Ln, m, bias=1.0)
                    m = fn(junk[:, :, :], junk[:, :, :], ACT.Exp, m, scale=-1.0)
                    cond = v_tt(cond_of(v), cond_of(v), junk[:, :, :], ALU.mult, m)
            yield
            read = [None, None]
            m = cond
            first = mod_loads[0]

            def fetch_tile(i):
                l, t = tiles_of[i]
                k = (first + i) % 2
                mod_loads[0] += 1
                return dma(pool, mod_sem[k], 16 * ((first + i) // 2 + 1), mod_ring[:, k, :, :],
                           dr["w_mod"][l, t].rearrange("p (t c) -> p t c", t=4), read[k])
            landed = {0: fetch_tile(0)}
            for i, (l, t) in enumerate(tiles_of):
                if i + 1 < len(tiles_of):
                    landed[i + 1] = fetch_tile(i + 1)
                yield
                k = (first + i) % 2
                for v in range(2 if l == 0 or t < 16 else 1):
                    m = dot(junk[:, :, :], mod_ring[:, k, :, :], cond_of(v), MOD[:, l, v, t:t + 1], landed[i], m)
                read[k] = m
                if t < 47:
                    continue
                b0 = VEC[f"bmod_{l}"][0]
                for v in range(2):
                    n = 48 if l == 0 or v == 0 else 16
                    m = v_tt(MOD[:, l, v, 0:n], MOD[:, l, v, 0:n], vecs[:, b0:b0 + n], ALU.add, m)
                    for w in range(2):
                        if l == 1 and v == 1 and w == 1:
                            continue
                        n0 = VEC[f"n{w + 1}_{l}"][0]
                        sc = 24 * w + 8
                        m = v_stt(GS[:, l, w, v, :], MOD[:, l, v, sc:sc + 8], 1.0, vecs[:, n0:n0 + 8], ALU.add, ALU.mult, m)

        block1 = ExitStack()
        V = sb(block1, "values", [P, S // P, D])
        B_ = sb(block1, "gla_in", [P, 5, S])
        qk = [ExitStack(), ExitStack()]
        QK = [sb(qk[1 - g], f"q_and_k_{1 - g}", [P, 6, S]) for g in range(2)][::-1]
        HS_1 = ExitStack()
        HS = sb(HS_1, "normed_1", [P, 2, KT, S], F32R)
        spread = inverse(all_squares(lambda t: X[:, t, :], KT, X1, [x_landed[t // 2] for t in range(KT)]), D)
        split_next_two()
        h_ready = normed_split(spread, HS, X1, lambda t, r: vec("norm1", t))
        x_of = lambda part, k, a, z: HS[:, part, k, a:z]
        proj = []

        def keep(dst):
            def f(ps, a, z, mark):
                m = copy(dst, ps, mark)
                proj.append(m)
                return m
            return f

        NH = A_HEADS + C_HEADS
        ROWS = nc.dram_tensor("bias_scratch", [NH, STRIP], F32, kind="Internal").ap()
        STRIPS = nc.dram_tensor("strip_scratch", [NH, P, S], F32, kind="Internal").ap()
        strip_saved = [None, None]

        def make_strips(scope):
            s_rows = sem("bias_rows_saved")
            s_raw = [sem("strip_raw_0"), sem("strip_raw_1")]
            s_saved = [sem("strip_saved_0"), sem("strip_saved_1")]
            flip = sb(scope, "c_flip", [P, P])
            with ExitStack() as rows:
                bias_rows = sb(rows, "bias_rows", [P, STRIP])
                bucket_of, log_reach = (sb(rows, "c_" + n, [P, STRIP]) for n in ("bucket_of", "log_reach"))
                fetch(flip[:, :], dr["c_flip"], "strips")
                fetch(bucket_of[:, :], dr["c_bucket_of"], "strips")
                t_in = fetch(log_reach[:, :], dr["c_log_reach"], "strips")
                yield
                b = take(2)
                mm(psum[0:NH, b, 0:512], small["rel_bias"][0:REL_BUCKETS, :], bucket_of[0:REL_BUCKETS, 0:512], True, True,
                   t_in, loaded, bank_free[b])
                m = mm(psum[0:NH, b + 1, 0:STRIP - 512], small["rel_bias"][0:REL_BUCKETS, :], bucket_of[0:REL_BUCKETS, 512:STRIP],
                       True, True, bank_free[b + 1], signal=True)
                m = v_tt(bias_rows[0:NH, :], bank(b, STRIP, 2)[0:NH, :], log_reach[0:NH, :], ALU.add, m, t_in)
                bank_free[b] = bank_free[b + 1] = m
                yield
                rows_saved = dma(pool, s_rows, 16, ROWS, bias_rows[0:NH, :], m)
                for lane in lanes:
                    lane.wait(rows_saved)
            yield
            raw = sb(scope, "strip_raw", [P, 2, S])
            out = sb(scope, "strip_out", [P, 2, S])
            flipped, loaded_raw = [None, None], {}

            def fetch_raw(h):
                src = bass.AP(tensor=ROWS.tensor, offset=ROWS.offset + h * STRIP, ap=[[1, P], [1, S]])
                loaded_raw[h] = dma(pool, s_raw[h % 2], 16 * (h // 2 + 1), raw[:, h % 2, :], src, rows_saved, flipped[h % 2])
            fetch_raw(0)
            for h in range(NH):
                k = h % 2
                if h + 1 < NH:
                    fetch_raw(h + 1)
                yield
                b = take(1)
                flipped[k] = mm(bank(b), flip[:, :], raw[:, k, :], True, True, loaded_raw[h], bank_free[b], signal=True)
                m = copy(out[:, k, :], bank(b), flipped[k], strip_saved[k])
                bank_free[b] = m
                strip_saved[k] = dma(pool, s_saved[k], 16 * (h // 2 + 1), STRIPS[h], out[:, k, :], m)

        dsts = [QK[0][:, i, :] for i in range(6)] + [B_[:, i, :] for i in range(4)] + [QK[1][:, i, :] for i in range(6)]
        beside = ExitStack()
        strips_made = make_strips(beside)
        modulated = modulation(beside, "_a", [(0, t) for t in range(MOD_FIRST)])
        next(strips_made)
        next(modulated)
        dsts.append(B_[:, 4, :])
        product([("w_in1", 0), ("w_in1", 1)], x_of, h_ready, X1, [keep(dsts[0]), keep(dsts[1])])
        for i in range(2, len(dsts)):
            product([("w_in1", i)], x_of, h_ready, X1, [keep(dsts[i])])
            next(modulated, None)
            if i > 2:
                next(strips_made, None)
            if i > 3:
                next(modulated, None)
        for half in range(2):
            bs = [take(1) for _ in range(4)]
            for s in range(4):
                slot, ready = load_split("w_v1", (half, s))
                for j in range(2):
                    k = 2 * s + j
                    for part, w in ((0, 0), (1, 0), (0, 1)):
                        for t in range(4):
                            m = mm(bank(bs[t]), HS[:, part, k, t * P:(t + 1) * P], WS[:, slot, w, j * 512:(j + 1) * 512],
                                   k == 0 and part + w == 0, k == KT - 1 and w == 1, ready,
                                   bank_free[bs[t]] if k == 0 and part + w == 0 else None, signal=(j == 1 and t == 3 and w == 1))
                split_free[slot] = m
                next(strips_made, None)
                next(modulated, None)
                next(modulated, None)
            for t in range(4):
                c = copy(V[:, t, half * 512:(half + 1) * 512], bank(bs[t]), m)
                bank_free[bs[t]] = c
                proj.append(c)
        for _ in strips_made:
            pass
        for _ in modulated:
            pass
        for lane in lanes:
            lane.wait(proj, strip_saved, loaded)
        fence()
        beside.close()
        HS_1.close()
        mix1 = ExitStack()
        H = sb(mix1, "mix_1", [P, KT, S], high=True)

        s_strip = [sem("strip_load_0"), sem("strip_load_1")]
        front = ExitStack()

        def ch(x):
            return x.rearrange("p (n c) -> p n c", c=B_CHUNK)

        def gla_buf(scope, name, *shape):
            return sb(scope, "gla_" + name, [P, *shape])
        gla = {}

        def gla_front():
            Bc, la, eb, kt = (gla_buf(front, n, S) for n in ("b", "la", "eb", "kt"))
            VT, ktok, dec = gla_buf(front, "vT", 2, S), gla_buf(front, "ktok", 4, P), gla_buf(front, "dec", NCHUNK)
            Q, K_, G_ = B_[:, 0, :], B_[:, 1, :], B_[:, 4, :]
            e1 = eb
            b = take(1, "turn")
            m = mm(bank(b), small["w_a2"][0:B_RANK, :], G_[0:B_RANK, :], True, True, bank_free[b], signal=True)
            yield
            z = v_ts(la[:, :], bank(b), vec("gla_b"), None, ALU.add, None, m)
            bank_free[b] = z
            q_s = v_ts(Q, Q, B_DK ** -0.5, None, ALU.mult, None)
            yield
            m = fn(e1[:, :], la[:, :], ACT.Abs, z)
            m = fn(e1[:, :], e1[:, :], ACT.Exp, m, scale=-1.0)
            m = fn(e1[:, :], e1[:, :], ACT.Ln, m, bias=1.0)
            yield
            m = v_stt(la[:, :], la[:, :], 0.0, e1[:, :], ALU.min, ALU.subtract, m)
            m = v_ts(la[:, :], la[:, :], 1.0 / B_TAU, None, ALU.mult, None, m)
            b_ready = scan(Bc[:, :], C["not_first"][:, :], la[:, :], m)
            yield
            last_b = ch(Bc[:, :])[:, :, B_CHUNK - 1:B_CHUNK].broadcast_to([P, NCHUNK, B_CHUNK])
            k0 = v_tt(ch(kt[:, :]), last_b, ch(Bc[:, :]), ALU.subtract, b_ready, lane=pool)
            dec_ready = fn(dec[:, :], ch(Bc[:, :])[:, :, B_CHUNK - 1], ACT.Exp, b_ready)
            m = fn(eb[:, :], Bc[:, :], ACT.Exp, b_ready)
            q_in = v_tt(eb[:, :], eb[:, :], Q, ALU.mult, m, q_s, lane=pool)
            yield
            m = fn(kt[:, :], kt[:, :], ACT.Exp, k0)
            k_end = v_tt(kt[:, :], kt[:, :], K_, ALU.mult, m, lane=pool)
            vt = []
            for f in range(2):
                b = take(1, "turn")
                for t in range(4):
                    m = turn(psum[:, b, t * P:(t + 1) * P], V[:, t, 384 + f * P:384 + (f + 1) * P], bank_free[b], signal=t == 3)
                vt.append(copy(VT[:, f, :], bank(b), m))
                bank_free[b] = vt[-1]
                yield
            b = take(1, "turn")
            for t in range(4):
                m = turn(psum[:, b, t * P:(t + 1) * P], kt[:, t * P:(t + 1) * P], k_end, bank_free[b], signal=t == 3)
            k_tok = copy(ktok[:, :, :].rearrange("p t c -> p (t c)"), bank(b), m)
            bank_free[b] = k_tok
            gla.update(Bc=Bc, la=la, eb=eb, e1=kt, VT=VT, ktok=ktok, dec=dec, b_ready=b_ready, q_s=q_s, q_in=q_in,
                       dec_ready=dec_ready, vt=vt, k_tok=k_tok)

        strip_loads = [0]
        for g in range(2):
            with ExitStack() as scope:
                ST = sb(scope, f"strips_{g}", [P, 2, S])
                strip_in = {}

                def fetch_strip(h):
                    k = strip_loads[0] % 2
                    strip_in[h] = dma(sp, s_strip[k], 16 * (strip_loads[0] // 2 + 1), ST[:, k, :], STRIPS[6 * g + h], sp_start, strip_saved,
                                      last_use.get(h - 2))
                    strip_loads[0] += 1
                sp_start = [lane.now() for lane in lanes]
                last_use = {}
                units = [(h, [(P * i, P * (i + 1)) for i in range(4)], 0) for h in range(6)]

                def strip_of(h, q0, w):
                    return ST[:, h % 2, 384 - q0:384 - q0 + w]
                fetch_strip(0)
                fetch_strip(1)
                attention(scope, f"att{g}", units, DH ** -0.5,
                          lambda h, a, z: QK[g][64 * (h % 2):64 * (h % 2) + 64, h // 2, a:z],
                          lambda h, a, z: QK[g][64 * (h % 2):64 * (h % 2) + 64, 3 + h // 2, a:z],
                          lambda h, t: V[:, t, (640 if g else 0) + h * DH:(640 if g else 0) + (h + 1) * DH],
                          strip_of,
                          lambda h, ps, a, z, mark: copy(H[64 * (h % 2):64 * (h % 2) + 64, (5 if g else 0) + h // 2, a:z], ps, mark), S,
                          gla_front() if g else iter(()), strips=(strip_in, last_use, fetch_strip))
            qk[g].close()

        with ExitStack() as scope:
            Bc, la, eb, e1, VT, ktok, dec = (gla[n] for n in ("Bc", "la", "eb", "e1", "VT", "ktok", "dec"))
            b_ready, q_s, q_in, vt, k_tok = (gla[n] for n in ("b_ready", "q_s", "q_in", "vt", "k_tok"))
            Q, K_ = B_[:, 0, :], B_[:, 1, :]
            vm = gla_buf(scope, "vm", 2, 512)
            UX, DX = gla_buf(scope, "u", DH, NCHUNK), gla_buf(scope, "dec_all", DH, NCHUNK)
            BX = gla_buf(scope, "state_blocks", 2, DH, NCHUNK)
            ACC, D1, D2, E_ = (gla_buf(scope, n, 2, S) for n in ("acc", "decays", "qk", "mul"))

            def states():
                split_next_two()
                z0 = copy_on(act, DX[:, :, :], dec[:, :].unsqueeze(1).broadcast_to([P, DH, NCHUNK]), gla["dec_ready"])
                z0 = zero(pool, DX[:, :, 0:1], z0)
                z1 = []
                mask = C["in_chunk"][:, :].unsqueeze(2).broadcast_to([P, P // B_CHUNK, DH])
                vm_read = [None, None]
                u_done = []
                i = 0
                for t in range(4):
                    b = take(1, "turn")
                    for h in range(B_HEADS):
                        src = V[:, t, 384 + h * DH:384 + (h + 1) * DH].unsqueeze(1).broadcast_to([P, P // B_CHUNK, DH])
                        m = v_tt(vm[:, i % 2, :].rearrange("p (n v) -> p n v", v=DH), src, mask, ALU.mult, vm_read[i % 2])
                        m = mm(psum[32 * h:32 * h + 32, b, :], ktok[:, t, 32 * h:32 * h + 32], vm[:, i % 2, :], True, True, m, k_tok,
                               bank_free[b] if h == 0 else None, signal=True)
                        vm_read[i % 2] = m
                        i += 1
                        if h % 2:
                            z1.append(zero(pool, BX[:, h // 2, 16 * t:16 * t + 16, :]))
                            yield
                    m = copy_on(act, UX[:, :, 8 * t:8 * t + 8].rearrange("p v n -> p n v"),
                                bank(b).rearrange("p (n v) -> p n v", v=DH), m)
                    bank_free[b] = m
                    u_done.append(m)
                flat = lambda x: x[:, :, :].rearrange("p v n -> p (v n)")
                m = scan(flat(UX), flat(DX), flat(UX), u_done, z0)
                yield
                bx = [copy_on(act, BX[32 * h:32 * h + 32, h % 2], UX[32 * h:32 * h + 32], m, z1) for h in range(B_HEADS)]
                for pr, x in enumerate((la[:, :], e1[:, :])):
                    rr = B_[:, 2 + pr, :]
                    m = fn(x, rr, ACT.Exp, scale=-1.0)
                    m = fn(x, x, ACT.Ln, m, bias=1.0)
                    m = fn(x, x, ACT.Exp, m, scale=-1.0)
                    gate_r.append(v_tt(x, x, rr, ALU.mult, m, lane=pool))
                yield
                for n in range(1, NCHUNK):
                    for pr in range(2):
                        m = mm(psum[:, 6 + pr, n * B_CHUNK:(n + 1) * B_CHUNK], BX[64 * pr:64 * pr + 64, :, :, n - 1],
                               eb[64 * pr:64 * pr + 64, n * B_CHUNK:(n + 1) * B_CHUNK], True, True, bx[2 * pr:2 * pr + 2], q_in,
                               bank_free[6 + pr], signal=n == NCHUNK - 1)
                        if n == NCHUNK - 1:
                            carried[pr] = m
                    if n % 4 == 0:
                        yield

            carried, gate_r = [None, None], []
            work = states()
            p_read, e_read, acc_done = [None, None], [None, None], [None, None]
            ready = {}

            def cut(x, s):
                w = B_CHUNK - s
                return x[:, 0:NCHUNK * w].rearrange("p (c w) -> p c w", w=w)

            def decay(s):
                j, w, n = s % 2, B_CHUNK - s, NCHUNK * (B_CHUNK - s)
                m = v_tt(cut(D1[:, j, :], s), ch(Bc[:, :])[:, :, s:], ch(Bc[:, :])[:, :, 0:w], ALU.subtract, p_read[j], b_ready)
                m = fn(D1[:, j, 0:n], D1[:, j, 0:n], ACT.Exp, m)
                m2 = v_tt(cut(D2[:, j, :], s), ch(Q)[:, :, s:], ch(K_)[:, :, 0:w], ALU.mult, q_s, p_read[j], lane=pool)
                ready[s] = v_tt(D1[:, j, 0:n], D1[:, j, 0:n], D2[:, j, 0:n], ALU.mult, m, m2, lane=pool)

            def gather(s):
                j, w, n = s % 2, B_CHUNK - s, NCHUNK * (B_CHUNK - s)
                for pr in range(2):
                    b = take(1, "row")
                    m = mm(bank(b, n), C["spread"][64 * pr:64 * pr + 64, :], D1[64 * pr:64 * pr + 64, j, 0:n], True, True,
                           ready[s], bank_free[b], signal=True)
                    p_read[j] = [m, ready[s]]
                    if s == 0:
                        a = v_tt(ACC[:, pr, :], bank(b), VT[:, pr, :], ALU.mult, m, vt)
                        bank_free[b] = acc_done[pr] = a
                    else:
                        a = v_tt(cut(E_[:, pr, :], s), bank(b, n).rearrange("p (c w) -> p c w", w=w), ch(VT[:, pr, :])[:, :, 0:w],
                                 ALU.mult, m, e_read[pr])
                        bank_free[b] = a
                        acc_done[pr] = e_read[pr] = v_tt(ch(ACC[:, pr, :])[:, :, s:], ch(ACC[:, pr, :])[:, :, s:],
                                                         cut(E_[:, pr, :], s), ALU.add, a, acc_done[pr])
            decay(0)
            for s in range(B_CHUNK):
                if s + 1 < B_CHUNK:
                    decay(s + 1)
                gather(s)
                next(work, None)
                if s % 2:
                    next(work, None)
            for _ in work:
                pass
            mean_eps = []
            for pr in range(2):
                sq, inv = E_[:, pr, :], D1[:, pr, :]
                m = v_tt(ACC[:, pr, B_CHUNK:], psum[:, 6 + pr, B_CHUNK:], ACC[:, pr, B_CHUNK:], ALU.add, carried[pr], acc_done[pr])
                bank_free[6 + pr] = m
                m = v_tt(sq, ACC[:, pr, :], ACC[:, pr, :], ALU.mult, m, acc_done[pr])
                b = take(1, "row")
                m = mm(bank(b), C["mean64"][:, :], sq, True, True, m, bank_free[b], signal=True)
                bank_free[b] = v_ts(inv, bank(b), EPS, None, ALU.add, None, m, pool.now())
                mean_eps.append(bank_free[b])
            logs = [fn(D1[:, pr, :], D1[:, pr, :], ACT.Ln, mean_eps[pr]) for pr in range(2)]
            roots = [fn(D1[:, pr, :], D1[:, pr, :], ACT.Exp, logs[pr], scale=-0.5) for pr in range(2)]
            for pr in range(2):
                inv = D1[:, pr, :]
                m = v_stt(inv, inv, vec("gla_norm", pr), ACC[:, pr, :], ALU.mult, ALU.mult, roots[pr])
                v_tt(H[:, 3 + pr, 0:S], (la, e1)[pr][:, :], inv, ALU.mult, gate_r[pr], m)
        front.close()
        block1.close()

        with ExitStack() as tail:
            HS = sb(tail, "mix_split_1", [P, 2, KT, S], F32R)
            ready = split_mix(HS, H, X1)
            sums = SquareSum(X1)
            def add_x(m_):
                def f(ps, a, z, mark):
                    done = v_tt(X[:, m_, a:z], ps, X[:, m_, a:z], ALU.add, mark)
                    sums.add(X[:, m_, :], done)
                    return done
                return f
            x_of = lambda part, k, a, z: HS[:, part, k, a:z]
            for ms in [(0, 1)] + [(i,) for i in range(2, KT)]:
                product([("w_out1", i) for i in ms], x_of, ready, X1, [add_x(i) for i in ms])
            fence()
            mix1.close()
            h_ready = normed_split(inverse(sums, D), HS, X1, lambda t, r: vec("norm2", t))
            squares_2 = sb(tail, "squares_with_gain", [P, 2, S])
            sums_gained = SquareSum(X1, squares_2)
            context_sums = []

            def beside_mlp(scope):
                yield from modulation(scope, "_b", [(0, t) for t in range(MOD_FIRST, 48)] + [(1, t) for t in range(48)])
                act.wait(dve.now())
                landed = fetch(X[:, :, S:T2], dr["ctx_t"], "context")
                for _ in range(3):
                    yield
                context_sums.append(SquareSum([(S, T2)]))
                for t in range(KT):
                    context_sums[0].add(X[:, t, :], landed)
                    yield
            with ExitStack() as scope:
                sums = mlp("1", lambda f: ("w_ff1", f), lambda g, m: ("w_ff2", (g, m)), HS, X1, h_ready, None,
                           beside_mlp(scope), (sums_gained, lambda t: vec("final1", t)))
            b, m, _ = column_sums([sums, sums_gained, context_sums[0]])
            m1 = v_ts(rs[:, 0:4], psum[:, b, 0:4], 1.0 / D, EPS, ALU.mult, ALU.add, m)
            m1 = inverse_root(rs[:, 0:4], m1)
            m2 = v_tt(rs[:, 4:8], psum[:, b, 4:8], rs[:, 0:4], ALU.mult, m1)
            m2 = v_tt(rs[:, 4:8], rs[:, 4:8], rs[:, 0:4], ALU.mult, m2)
            m2 = v_ts(rs[:, 4:8], rs[:, 4:8], 1.0 / D, EPS, ALU.mult, ALU.add, m2)
            m = v_ts(rs[:, 8:10], psum[:, b, 8:10], 1.0 / D, EPS, ALU.mult, ALU.add, m)
            bank_free[b] = m
            m = inverse_root(rs[:, 4:10], [m, m2])
            m = v_tt(rs[:, 4:8], rs[:, 4:8], rs[:, 0:4], ALU.mult, m)
            b = take(2)
            both_spread = (b, on_all_partitions(bank(b, T2, 2), rs[:, 4:10], SQ[:, 1, :], m, bank_free[b], bank_free[b + 1]))
            final_bank = take(1)
            final_ready = on_all_partitions(bank(final_bank), rs[:, 0:4], SQ[:, 0, 0:S], m1, bank_free[final_bank])
            gain_both = v_tt(gain_12[:, :], vecs[:, VEC["final1"][0]:VEC["final1"][0] + KT], GS[:, 0, 0, 0, :], ALU.mult)

        FILTERS = [{nm: nc.dram_tensor(f"filters_{l}{nm}", [P, L // P, 2, HY], F32, kind="Internal").ap()
                    for nm, L in (("x", S), ("c", SC))} for l in range(2)]
        filter_sem = [sem("filter_saved_0"), sem("filter_saved_1")]
        filter_saves = [0]
        s_filter = sem("filter_load")
        filter_loads = [0]

        def make_filters(scope, l, streams, norms):
            h1, h2, turns = (sb(scope, f"filter_{n}_{l}", [P, S]) for n in ("h1", "h2", "turns"))
            raw, both = sb(scope, f"filter_raw_{l}", [P, 2, 512]), sb(scope, f"filter_pair_{l}", [P, 2, 2, HY])
            saved, raw_read = [None, None], [None, None]
            h1_read = h2_read = None
            yield
            for si, (lo, hi, nm) in enumerate(streams):
                L = hi - lo
                nt = L // P

                def sine(dst, ps, mark, bias_name, free):
                    d, n_ = dst[0:64, 0:L], turns[0:64, 0:L]
                    a0 = v_ts(d, ps, vec(bias_name, 0, 64), vec(f"ffr_{l}", 0, 64), ALU.add, ALU.mult, mark, free)
                    magic = 1.5 * 2 ** 23
                    m = v_ts(n_, d, 1.0 / (2 * math.pi), magic, ALU.mult, ALU.add, a0)
                    m = v_ts(n_, n_, magic, None, ALU.subtract, None, m)
                    c1 = 6.28125
                    c2 = float(np.float32(np.round((2 * math.pi - c1) * 2 ** 22) / 2 ** 22))
                    c3 = 2 * math.pi - c1 - c2
                    for c in (c1, c2, c3):
                        m = v_stt(d, n_, -c, d, ALU.mult, ALU.add, m)
                    m = v_ts(d, d, 3.1415925, -3.1415925, ALU.min, ALU.max, m)
                    return a0, fn(d, d, ACT.Sin, m)

                slot, landed = load("tables", plan["emb_" + nm][0], L)
                b = take(1)
                m = mm(psum[0:64, b, 0:L], small["fw1"][0:33, 64 * l:64 * l + 64], ring[0:33, slot % RING, 0:L], True, True,
                       landed, bank_free[b], signal=True)
                free_slot(slot, m)
                bank_free[b], h1_ready = sine(h1, psum[0:64, b, 0:L], m, f"fb1_{l}", h1_read)
                yield
                b = take(1)
                m = mm(psum[0:64, b, 0:L], small["fw2"][0:64, 64 * l:64 * l + 64], h1[0:64, 0:L], True, True, h1_ready,
                       bank_free[b], signal=True)
                bank_free[b], h2_ready = sine(h2, psum[0:64, b, 0:L], m, f"fb2_{l}", h2_read)
                magnitudes, mag_ready = h1, m
                yield
                for t0 in range(0, nt, 2):
                    slot, landed = load("tables", plan["decay_" + nm][0] + t0 // 2)
                    for t in (t0, t0 + 1):
                        j = t % 2
                        b = take(1)
                        h2_read = mm(bank(b), h2[0:64, t * P:(t + 1) * P], small["fw3"][0:64, 512 * l:512 * l + 512], True, True,
                                     h2_ready, bank_free[b], signal=True)
                        m = v_tt(raw[:, j, :], bank(b), ring[:, slot % RING, j * 512:j * 512 + 512], ALU.mult, h2_read, landed,
                                 raw_read[j])
                        bank_free[b] = m
                        u1 = v_tt(both[:, j, 0, :], raw[:, j, 0:HY], raw[:, j, HY:512], ALU.add, m, saved[j], lane=pool)
                        u2 = v_tt(both[:, j, 1, :], raw[:, j, 0:HY], raw[:, j, HY:512], ALU.subtract, m, saved[j], lane=pool)
                        filter_saves[0] += 1
                        saved[j] = dma(pool, filter_sem[j], 16 * ((filter_saves[0] + 1) // 2), FILTERS[l][nm][:, t], both[:, j], u1, u2)
                        if t == 0:
                            raw_read[j] = mag_ready = fn(magnitudes[:, :], raw[:, j, :], ACT.Abs, m, mag_ready)
                        else:
                            ab = fn(raw[:, j, :], raw[:, j, :], ACT.Abs, m, u1, u2)
                            raw_read[j] = mag_ready = v_tt(magnitudes[:, :], magnitudes[:, :], raw[:, j, :], ALU.add, ab, mag_ready)
                        raw_read[j] = [raw_read[j], u1, u2]
                    free_slot(slot, m)
                    yield
                b = take(1)
                for ct in range(2):
                    for side_ in range(2):
                        m = mm(psum[:, b, ct:ct + 1], magnitudes[:, side_ * HY + ct * P:side_ * HY + (ct + 1) * P], C["ones"][:, 0:1],
                               side_ == 0, side_ == 1, mag_ready, bank_free[b], signal=side_ == 1)
                h1_read = m
                bank_free[b] = recip(norms[:, si, :], psum[:, b, 0:2], m)
                filters_made[nm] = [saved, bank_free[b]]
                yield

        for l in range(2):
            last_layer = l == 1
            RG = X1 if last_layer else XB
            streams = [(0, S, "x")] if last_layer else [(0, S, "x"), (S, T2, "c")]
            norm_in = ExitStack()
            layer = ExitStack()
            LAT = sb(layer, f"latents_{l}", [P, 5, T2])
            KR = sb(layer, f"k_rope_{l}", [P, T2])
            norms = sb(layer, f"filter_norms_{l}", [P, 2, 2])
            tmp = SQ
            mixed = ExitStack()
            early = ExitStack()
            FU = sb(early, f"fourier_in_{l}", [P, 2, T2])
            HU = sb(early, f"hyena_in_{l}", [P, 6, T2])
            HS = sb(norm_in, f"normed_in_{l}", [P, 2, KT, T2], F32R)
            filters_made = {}
            gain = (lambda t, r: gain_12[:, t:t + 1] if r == 0 else GS[:, 0, 0, 1, t:t + 1]) if l == 0 else (
                lambda t, r: GS[:, 1, 0, r, t:t + 1])
            spread = (both_spread[0], [both_spread[1], final_ready, gain_both]) if l == 0 else inverse(sums, D)
            h_ready = normed_split(spread, HS, XB, gain, lambda t, r: MOD[:, l, r, t:t + 1])
            proj = []

            def keep2(dst):
                def f(ps, a, z, mark):
                    m = copy(dst[:, a:z], ps, mark)
                    proj.append(m)
                    return m
                return f

            def rotated(dst, ps, a, mark, free=None):
                m0 = v_tt(tmp[64:96, 0, 0:S], ps[64:96], C["rope"][64:96, :], ALU.mult, mark, dve.now())
                m1 = v_tt(tmp[64:96, 1, 0:S], ps[96:128], C["rope"][96:128, :], ALU.mult, mark, dve.now())
                m = v_tt(dst, tmp[64:96, 0, 0:S], tmp[64:96, 1, 0:S], ALU.add, m0, m1, free)
                return m, m1

            def kr_out(ps, a, z, mark):
                if a == 0:
                    m, m1 = rotated(KR[64:96, a:z], ps, a, [mark, h_ready])
                    proj.append(m)
                    return m
                m = copy(KR[64:96, a:z], ps[64:96], mark)
                proj.append(m)
                return m

            x_of = lambda part, k, a, z: HS[:, part, k, a:z]
            beside = ExitStack()
            filters = make_filters(beside, l, streams, norms)
            next(filters)
            tiles_in = [(i, RG, keep2(LAT[:, i, :])) for i in range(3)] + [(i, XB, keep2(LAT[:, i, :])) for i in range(3, 5)]
            tiles_in += [(13, XB, kr_out)] + [(7 + i, RG, keep2(HU[:, i, :])) for i in range(6)]
            tiles_in += [(5 + i, RG, keep2(FU[:, i, :])) for i in range(2)]
            together = tiles_in[:2]
            product([("w_in2", (l, i)) for i, _, _ in together], x_of, h_ready, RG, [out for _, _, out in together])
            if l == 0:
                split_next_two()
                for t in range(KT):
                    m = v_stt(X[:, t, 0:S], X[:, t, 0:S], vec("final1", t), bank(final_bank), ALU.mult, ALU.mult, final_ready)
                bank_free[final_bank] = m
            for i, rg, out in tiles_in[2:]:
                product([("w_in2", (l, i))], x_of, h_ready, rg, [out])
                next(filters, None)
            for _ in filters:
                pass
            for lane in lanes:
                lane.wait(proj, list(filters_made.values()))
            beside.close()
            norm_in.close()
            mix2 = ExitStack()
            H = sb(mix2, f"mix_2_{l}", [P, KT, T2], high=True)
            U = sb(mixed, f"conv_out_{l}", [P, 6, T2])

            cw, cb = VEC[f"cw_{l}"][0], VEC[f"cb_{l}"][0]
            hi_all = streams[-1][1]

            def short_conv(i):
                m = fn(U[:, i, 0:hi_all], HU[:, i, 0:hi_all], ACT.Identity, bias=vecs[:, cb + i:cb + i + 1],
                       scale=vecs[:, cw + 6 + i:cw + 7 + i])
                for lo, hi, nm in streams:
                    m = v_stt(U[:, i, lo + 1:hi], HU[:, i, lo:hi - 1], vecs[:, cw + i:cw + i + 1], U[:, i, lo + 1:hi], ALU.mult, ALU.add, m)
                    m = v_stt(U[:, i, lo:hi - 1], HU[:, i, lo + 1:hi], vecs[:, cw + 12 + i:cw + 13 + i], U[:, i, lo:hi - 1], ALU.mult, ALU.add, m)
                return m

            Z = lambda i: U[:, 2 + i, :]
            z_ready = [None, None]

            def make_z(i):
                m = short_conv(4 + i)
                z_ready[i] = v_tt(Z(i)[:, 0:hi_all], Z(i)[:, 0:hi_all], U[:, 4 + i, 0:hi_all], ALU.mult, m)

            lat_q = lambda t: LAT[:, t, :]
            lat_kv = lambda t: LAT[:, 3 + t, :]
            narrow = [None]
            made_norm = {}

            def q_squares():
                narrow[0] = all_squares(lat_q, 3, RG, None)

            def q_norm():
                nt, m = narrow[0]
                m = v_ts(rs[:, 0:nt], rs[:, 0:nt], 1.0 / math.sqrt(NOPE + ROPE), None, ALU.mult, None, m)
                made_norm["q"] = normed(inverse_spread(nt, m), lat_q, lat_q, 3, RG, lambda t, r: vec(f"qn_{l}", t))

            def kv_squares():
                narrow[0] = all_squares(lat_kv, 2, XB, None)

            def kv_norm():
                made_norm["kv"] = normed(inverse_spread(*narrow[0]), lat_kv, lat_kv, 2, XB, lambda t, r: vec(f"kvn_{l}", t))

            def to_narrow(n):
                def f():
                    narrow[0] = inverse_narrow(narrow[0], n)
                return f
            conv = lambda i: lambda: short_conv(i)
            z_of = lambda i: lambda: make_z(i)
            with ExitStack() as scope:
                A_ = sb(scope, f"fourier_mid_{l}", [P, T2 // P, 512])
                a_done = []

                def mid(t):
                    b = take(1)
                    for f in range(2):
                        m = mm(psum[:, b, f * 256:(f + 1) * 256], FU[:, f, t * P:(t + 1) * P], C["dft64"][:, :],
                               True, True, bank_free[b] if f == 0 else None, signal=f == 1)
                    bank_free[b] = copy(A_[:, t, :], bank(b), m)
                    a_done.append(bank_free[b])

                def over_tokens(lo, hi, nm, works):
                    b = take(2)
                    i0, _, wid = plan["fourier_" + nm]
                    L = hi - lo
                    nt = L // P
                    for t in range(nt):
                        slot, landed = load("tables", i0 + t, wid)
                        for f in range(2):
                            for cs in range(2):
                                m = mm(psum[:, b + f, 0:L], A_[:, lo // P + t, f * 256 + cs * P:f * 256 + (cs + 1) * P],
                                       ring[:, slot % RING, cs * L:(cs + 1) * L], t == 0 and cs == 0, t == nt - 1 and cs == 1,
                                       landed, a_done[lo // P + t], bank_free[b + f] if t == 0 and cs == 0 else None,
                                       signal=f == 1 and cs == 1)
                        free_slot(slot, m)
                        for work in works[t:t + 1]:
                            work()
                    for f in range(2):
                        bank_free[b + f] = copy(H[:, 4 + f, lo:hi], psum[:, b + f, 0:L], m)
                q_squares()
                for t in range(hi_all // P):
                    mid(t)
                to_narrow(QL)()
                short_conv(2)
                over_tokens(0, S, "x", [lambda: (q_norm(), kv_squares()), conv(3), lambda: (to_narrow(KVL)(), make_z(0)), kv_norm])
                short_conv(0)
                if not last_layer:
                    over_tokens(S, T2, "c", [z_of(1)])
                else:
                    make_z(1)
                short_conv(1)
            q_ready, kv_ready = made_norm["q"], made_norm["kv"]
            early.close()

            VH = sb(layer, f"v_heads_{l}", [P, T2 // P, MH * DH])
            v_made = []

            def make_values(ts):
                slot, landed = load("w_uv", l)
                for t in ts:
                    b = take(1)
                    for k in range(2):
                        m = mm(bank(b), LAT[:, 3 + k, t * P:(t + 1) * P], ring[:, slot % RING, k * 512:(k + 1) * 512], k == 0, k == 1,
                               landed, kv_ready[k], bank_free[b] if k == 0 else None, signal=k == 1)
                    bank_free[b] = copy(VH[:, t, :], bank(b), m)
                    v_made.append(bank_free[b])
                free_slot(slot, m)

            with ExitStack() as one:
                IN = [sb(one, f"spectrum_in_{n}_{l}", [P, S // P, 512]) for n in ("cos", "sin")]
                RE = sb(one, f"spectrum_re_{l}", [P, 2, 512])
                IM = sb(one, f"spectrum_im_{l}", [P, 2, 512])
                Y = sb(one, f"spectrum_product_{l}", [P, S // P, 2, HY])
                T0 = SQ
                z_tokens, filter_in = {}, {}
                in_read, y_read = None, None
                t0_free = [dve.now(), pe.now(), act.now(), pool.now()]

                def put_in(lo, hi, nm):
                    nt = (hi - lo) // P
                    for c in range(2):
                        filter_loads[0] += 16
                        filter_in[nm] = dma(pool, s_filter, filter_loads[0], IN[c][:, 0:nt, HY:512], FILTERS[l][nm][:, :, c, :],
                                            filters_made[nm], in_read)
                    z_tokens[nm] = []
                    for t in range(nt):
                        b = take(1)
                        for ct in range(2):
                            m = turn(psum[:, b, ct * P:(ct + 1) * P], Z(ct)[:, lo + t * P:lo + (t + 1) * P], z_ready, bank_free[b],
                                     signal=ct == 1)
                        m1 = copy_on(act, IN[0][:, t, 0:HY], psum[:, b, 0:HY], m, in_read)
                        m2 = copy_on(dve, IN[1][:, t, 0:HY], psum[:, b, 0:HY], m, m1, in_read)
                        bank_free[b] = m2
                        z_tokens[nm].append([m1, m2])

                def multiply_spectra(lo, hi, nm):
                    nt = (hi - lo) // P
                    i0, _, wid = plan["fwd_" + nm]
                    y_done = [None] * nt
                    for f in range(nt):
                        j = f % 2
                        slot, landed = load("tables", i0 + f, wid)
                        b = take(2)
                        for cs in range(2):
                            for t in range(nt):
                                m = mm(bank(b + cs), ring[:, slot % RING, cs * nt * P + t * P:cs * nt * P + (t + 1) * P],
                                       IN[cs][:, t, :], t == 0, t == nt - 1, landed, z_tokens[nm][t], filter_in[nm],
                                       bank_free[b + cs] if t == 0 else None, signal=t == nt - 1)
                        free_slot(slot, m)
                        free = spectra_read[j]
                        re = copy_on(act, RE[:, j, :], bank(b), m, free)
                        im = copy_on(act, IM[:, j, :], bank(b + 1), m, free)
                        bank_free[b], bank_free[b + 1] = re, im
                        zr, kr, zi, ki = RE[:, j, 0:HY], RE[:, j, HY:512], IM[:, j, 0:HY], IM[:, j, HY:512]
                        before = spectra_read[1 - j]
                        p1 = v_tt(Y[:, f, 0, :], zr, kr, ALU.mult, im, y_read)
                        p2 = v_tt(T0[:, 0, 0:HY], zi, ki, ALU.mult, im, before, t0_free)
                        p3 = v_tt(Y[:, f, 0, :], Y[:, f, 0, :], T0[:, 0, 0:HY], ALU.subtract, p1, p2)
                        q1 = v_tt(Y[:, f, 1, :], zr, ki, ALU.mult, im, y_read, lane=pool)
                        q2 = v_tt(T0[:, 1, 0:HY], zi, kr, ALU.mult, im, before, t0_free, lane=pool)
                        q3 = v_tt(Y[:, f, 1, :], Y[:, f, 1, :], T0[:, 1, 0:HY], ALU.add, q1, q2, lane=pool)
                        y_done[f] = spectra_read[j] = [p3, q3]
                    return y_done, m

                def back(si, lo, hi, nm, y_done):
                    L = hi - lo
                    nt = L // P
                    i0, _, wid = plan["inv_" + nm]
                    b = take(2)
                    for f in range(nt):
                        slot, landed = load("tables", i0 + f, wid)
                        for ct in range(2):
                            for cs in range(2):
                                m = mm(psum[:, b + ct, 0:L], Y[:, f, cs, ct * P:(ct + 1) * P], ring[:, slot % RING, cs * L:(cs + 1) * L],
                                       f == 0 and cs == 0, f == nt - 1 and cs == 1, landed, y_done[f],
                                       bank_free[b + ct] if f == 0 and cs == 0 else None, signal=ct == 1 and cs == 1)
                        free_slot(slot, m)
                    for ct in range(2):
                        dz = v_ts(Z(ct)[:, lo:hi], Z(ct)[:, lo:hi], vec(f"hd_{l}", ct), None, ALU.mult, None, m)
                        y = v_stt(Z(ct)[:, lo:hi], psum[:, b + ct, 0:L], norms[:, si, ct:ct + 1], Z(ct)[:, lo:hi], ALU.mult, ALU.add, dz)
                        bank_free[b + ct] = y
                        v_tt(H[:, 6 + ct, lo:hi], U[:, ct, lo:hi], Z(ct)[:, lo:hi], ALU.mult, y)
                    return m

                spectra_read = [None, None]
                put_in(*streams[0])
                make_values(range(0, 3))
                y_done, in_read = multiply_spectra(*streams[0])
                if last_layer:
                    make_values(range(3, 6))
                    back(0, *streams[0], y_done)
                else:
                    put_in(*streams[1])
                    make_values(range(3, 5))
                    y_read = back(0, *streams[0], y_done)
                    y_done, _ = multiply_spectra(*streams[1])
                    make_values(range(5, 6))
                    back(1, *streams[1], y_done)
            mixed.close()

            with ExitStack() as scope:
                QH = sb(scope, f"q_heads_{l}", [P, 3, T2])
                KH = sb(scope, f"k_heads_{l}", [P, 3, T2])
                made, logits_done = {}, {}

                def make_pair(p):
                    heads = (2 * p, 2 * p + 1)
                    for h in heads:
                        made[h] = [v_made, copy_on(pool, KH[64:96, h % 3, :], KR[64:96, :], logits_done.get(h - 3))]
                        pool.wait(pool.now())
                    slot, landed = load("w_uq", (l, p), 2 * 3 * P)
                    for h in heads:
                        free = logits_done.get(h - 3)
                        for lo, hi in RG:
                            b = take(1, "turn")
                            for k in range(3):
                                m = mm(psum[:, b, 0:hi - lo], ring[:, slot % RING, ((h % 2) * 3 + k) * P:((h % 2) * 3 + k + 1) * P],
                                       LAT[:, k, lo:hi], k == 0, k == 2, landed, q_ready[k], bank_free[b] if k == 0 else None, signal=k == 2)
                            if lo == 0:
                                m1, m2 = rotated(QH[64:96, h % 3, 0:S], psum[:, b, 0:S], 0, m, free)
                                m3 = copy_on(act, QH[0:64, h % 3, 0:S], psum[0:64, b, 0:S], m, m2, free)
                                made[h] += [m1, m3]
                            else:
                                m3 = copy_on(act, QH[0:96, h % 3, lo:hi], psum[0:96, b, 0:hi - lo], m, free)
                                made[h].append(m3)
                            bank_free[b] = m3
                            yield
                    free_slot(slot, m)
                    slot, landed = load("w_uk", (l, p), 2 * P)
                    for lo, hi in XB:
                        b = take(1, "turn")
                        for k in range(2):
                            m = mm(psum[:, b, 0:hi - lo], ring[:, slot % RING, k * P:(k + 1) * P], LAT[:, 3 + k, lo:hi],
                                   k == 0, k == 1, landed, kv_ready[k], bank_free[b] if k == 0 else None, signal=k == 1)
                        for j, h in enumerate(heads):
                            m5 = copy_on((dve, act)[j], KH[0:64, h % 3, lo:hi], psum[64 * j:64 * j + 64, b, 0:hi - lo], m,
                                         m5 if j else None, logits_done.get(h - 3))
                            made[h].append(m5)
                        bank_free[b] = m5
                        yield
                    free_slot(slot, m)
                for _ in make_pair(0):
                    pass
                units = []
                for h in range(MH):
                    units.append((h, [(P * i, T2) for i in range(4)], 0))
                    if not last_layer:
                        units.append((h, [(S + P * i, SC) for i in range(2)], S))
                making = [iter(())]

                def feed(h, first):
                    if first and h == MH - 1:
                        split_next_two()
                    if first and h % 2 == 0:
                        for _ in making[0]:
                            pass
                    if first and h % 2 and h + 1 < MH:
                        making[0] = make_pair((h + 1) // 2)
                    next(making[0], None)
                attention(scope, f"mla{l}", units, None,
                          lambda h, a, z: QH[0:96, h % 3, a:z], lambda h, a, z: KH[0:96, h % 3, a:z],
                          lambda h, t: VH[:, t, h * DH:(h + 1) * DH], None,
                          lambda h, ps, a, z, mark: copy(H[64 * (h % 2):64 * (h % 2) + 64, h // 2, a:z], ps, mark), T2,
                          heads=(feed, made, logits_done))
            layer.close()

            def gate(comp):
                return lambda m, a: MOD[:, l, 0 if a == 0 else 1, comp * 8 + m:comp * 8 + m + 1]
            with ExitStack() as tail:
                HS = sb(tail, f"mix_split_2_{l}", [P, 2, KT, T2], F32R)
                ready = split_mix(HS, H, RG)
                sums = SquareSum(RG)
                x_of = lambda part, k, a, z: HS[:, part, k, a:z]
                def add_x(m_):
                    ms = []

                    def f(ps, a, z, mark):
                        ms.append(v_stt(X[:, m_, a:z], ps, gate(2)(m_, a), X[:, m_, a:z], ALU.mult, ALU.add, mark))
                        if z == RG[-1][1]:
                            sums.add(X[:, m_, :], ms)
                        return ms[-1]
                    return f
                for ms in [(0, 1)] + [(i,) for i in range(2, KT)]:
                    product([("w_out2", (l, i)) for i in ms], x_of, ready, RG, [add_x(i) for i in ms])
                fence()
                mix2.close()
                h_ready = normed_split(inverse(sums, D), HS, RG, lambda t, r: GS[:, l, 1, r, t:t + 1], lambda t, r: MOD[:, l, r, 24 + t:25 + t])
                sums = mlp(f"2_{l}", lambda f: ("w_mlp1", (l, f)), lambda g, m: ("w_mlp2", (l, g, m)), HS, RG, h_ready, gate(5), iter(()))
            fence()

        done = normed(inverse(sums, D), lambda t: X[:, t, :], lambda t: X[:, t, :], KT, X1, lambda t, r: vec("final2", t))
        stored = sem("stored")
        for t in range(KT):
            m = dma(sp, stored, 16 * (t + 1), out_t[:, t, :], X[:, t, 0:S], done[t])
        sp.wait(m)

        if order is None:
            return used
        with nc.Block() as block:
            @block.tensor
            def _(eng):
                pe.run(eng)

            @block.vector
            def _(eng):
                dve.run(eng)

            @block.scalar
            def _(eng):
                act.run(eng)

            @block.gpsimd
            def _(eng):
                pool.run(eng)

            @block.sync
            def _(eng):
                sp.run(eng)


def tiles(w, cols):
    return slots_of(w[:, cols])


def lay_out(a):
    d = {}
    fm = lambda v: np.ascontiguousarray(v.reshape(-1, P).T)
    cols = lambda m: [slice(i * P, (i + 1) * P) for i in range(m)]
    d["x_t"] = np.ascontiguousarray(a["x"][0].T.reshape(KT, P, S).transpose(1, 0, 2))
    d["ctx_t"] = np.ascontiguousarray(a["ctx_2"][0].T.reshape(KT, P, SC).transpose(1, 0, 2))
    w = a["w_in"][0]
    AQ, AK, AV, BQ, BK, BV, BR, BA, CQ, CK, CV, _ = np.cumsum([0, 384, 384, 384, 128, 128, 256, 256, 16, 384, 384, 384])
    starts = [AQ + P * i for i in range(3)] + [AK + P * i for i in range(3)] + [BQ, BK, BR, BR + P]
    starts += [CQ + P * i for i in range(3)] + [CK + P * i for i in range(3)]
    ba = np.concatenate([w[:, BA:BA + B_RANK], np.zeros((D, P - B_RANK), np.float32)], 1)
    d["w_in1"] = np.stack([tiles(w, slice(s, s + P)) for s in starts] + [slots_of(ba)])
    wv = np.concatenate([w[:, AV:AV + 384], w[:, BV:BV + 256], w[:, CV:CV + 384]], 1)
    d["w_v1"] = np.ascontiguousarray(wv.reshape(4, 2, P, 2, 512).transpose(3, 0, 2, 1, 4).reshape(2, 4, P, 1024))
    d["w_out1"] = np.stack([tiles(a["w_out"][0], c) for c in cols(KT)])

    def ff2(w):
        return np.ascontiguousarray(w.reshape(NGROUP, GROUP, P, KT // 2, 2, P).transpose(0, 3, 2, 4, 1, 5).reshape(NGROUP, KT // 2, P, SLOT))
    d["w_ff1"] = np.stack([tiles(a["w_ff1"][0], c) for c in cols(FT)])
    d["w_ff2"] = ff2(a["w_ff2"][0])
    j = np.arange(ROPE)
    swap = np.where(j % 16 < 8, j + 8, j - 8)
    w2 = a["w_in_2"]
    off_kr, off_f = QL + KVL, QL + KVL + ROPE
    st = [P * i for i in range(5)] + [off_f + P * i for i in range(8)]
    pad = np.zeros((D, 64), np.float32)
    kr = [slots_of(np.concatenate([pad, w2[l][:, off_kr + j], w2[l][:, off_kr + swap]], 1)) for l in range(2)]
    d["w_in2"] = np.stack([np.stack([tiles(w2[l], slice(s, s + P)) for s in st] + [kr[l]]) for l in range(2)])
    uq = a["w_uq_2"]
    head = lambda h: np.concatenate([96 * h + np.arange(64), 96 * h + 64 + j, 96 * h + 64 + swap])
    d["w_uq"] = np.stack([np.stack([np.concatenate([tiles(uq[l], head(2 * p)), tiles(uq[l], head(2 * p + 1))], 1)
                                    for p in range(4)]) for l in range(2)])
    ukv = a["w_ukv_2"]
    nope = lambda p: np.concatenate([128 * (2 * p + i) + np.arange(64) for i in range(2)])
    vals = np.concatenate([128 * h + 64 + np.arange(64) for h in range(MH)])
    d["w_uk"] = np.stack([np.stack([tiles(ukv[l], nope(p)) for p in range(4)]) for l in range(2)])
    d["w_uv"] = np.stack([tiles(ukv[l], vals) for l in range(2)])
    d["w_out2"] = np.stack([np.stack([tiles(a["w_out_2"][l], c) for c in cols(KT)]) for l in range(2)])
    d["w_mlp1"] = np.stack([np.stack([tiles(a["w_mlp1_2"][l], c) for c in cols(FT)]) for l in range(2)])
    d["w_mlp2"] = np.stack([ff2(a["w_mlp2_2"][l]) for l in range(2)])
    d["w_mod"] = np.ascontiguousarray(a["w_mod_2"].transpose(0, 2, 1).reshape(2, 48, P, D))
    d["cond"] = np.stack([a["c_2"][0], a["c_ctx_2"]])
    d["w_a2"] = np.ascontiguousarray(a["gla_w_a2"][0])
    d["rel_bias"] = np.ascontiguousarray(a["rel_bias"])
    d["fw1"] = np.ascontiguousarray(np.concatenate([a["hy_w1_2"][l] for l in range(2)], 1))
    d["fw2"] = np.ascontiguousarray(np.concatenate([a["hy_w2_2"][l] for l in range(2)], 1))
    d["fw3"] = np.ascontiguousarray(np.concatenate([a["hy_w3_2"][l] for l in range(2)], 1))
    v = np.zeros((P, VECS), np.float32)

    def put(name, x):
        at, n = VEC[name]
        v[0:x.shape[0], at:at + n] = x
    put("norm1", fm(a["norm1_w"][0])); put("norm2", fm(a["norm2_w"][0])); put("final1", fm(a["final_norm_w"]))
    put("gla_norm", fm(a["gla_norm_w"][0])); put("gla_b", fm(a["gla_b_a"][0])); put("final2", fm(a["final_norm_g_2"]))
    for l in range(2):
        put(f"n1_{l}", fm(a["norm1_g_2"][l])); put(f"n2_{l}", fm(a["norm2_g_2"][l]))
        put(f"qn_{l}", fm(a["q_norm_g_2"][l])); put(f"kvn_{l}", fm(a["kv_norm_g_2"][l]))
        put(f"bmod_{l}", fm(a["b_mod_2"][l])); put(f"cw_{l}", fm(a["hy_conv_w_2"][l].reshape(-1)))
        put(f"cb_{l}", fm(a["hy_conv_b_2"][l])); put(f"hd_{l}", fm(a["hy_d_2"][l]))
        put(f"fb1_{l}", a["hy_b1_2"][l][:, None]); put(f"ffr_{l}", a["hy_freq_2"][l][:, None])
        put(f"fb2_{l}", a["hy_b2_2"][l][:, None])
    d["vecs"] = v
    for n, t in shape_constants().items():
        d["c_" + n] = t
    d["tables"], at = sequence_tables()
    return d, at


def kernel(**inputs):
    import concourse.bacc as bacc
    from concourse.bass_utils import run_bass_kernel_spmd as run

    arrays, at = lay_out({k: np.asarray(v) for k, v in inputs.items()})
    def blank():
        nc = bacc.Bacc("TRN2", target_bir_lowering=False, num_devices=1)
        dr = {n: nc.dram_tensor("in_" + n, a.shape, F32, kind="ExternalInput").ap() for n, a in arrays.items()}
        return nc, dr, nc.dram_tensor("out_t", (P, KT, S), F32, kind="ExternalOutput").ap()

    order = build(*blank(), at, None)
    nc, dr, out_t = blank()
    build(nc, dr, out_t, at, order)
    r = run(nc, [{"in_" + n: np.ascontiguousarray(a) for n, a in arrays.items()}], core_ids=[0])
    o = np.asarray(r.results[0]["out_t"])
    return np.ascontiguousarray(o.transpose(1, 0, 2).reshape(D, S).T)[None]
```
